# Optimizing a Trainium2 kernel written in Bass

```python
import math
import jax, jax.numpy as jnp
from jax import lax
import numpy as np

D_MODEL = 1024
BATCH = 1
SEQ = 1024
DEPTH = 2

N_ATTN_HEADS = 4
QK_NOPE_DIM = 128
QK_ROPE_DIM = 64
QK_HEAD_DIM = QK_NOPE_DIM + QK_ROPE_DIM
V_HEAD_DIM = 128
Q_RANK = 256
KV_RANK = 128
ATTN_WIDTH = N_ATTN_HEADS * V_HEAD_DIM
ROPE_THETA = 10000.0
Q_BLOCK = 128
CONV_CH = 512
CONV_WIDTH = 31
CONV_PAD = CONV_WIDTH // 2
D_MIX = ATTN_WIDTH + CONV_CH
IN_WIDTH = Q_RANK + KV_RANK + QK_ROPE_DIM + 2 * CONV_CH
N_EXPERTS = 16
CAPACITY_FACTOR = 2
EXPERT_FF = 1024
N_MOD = 6
EPS = 1e-6


def rms_norm(x, g):
    xf = x.astype(jnp.float32)
    y = xf * lax.rsqrt(jnp.mean(xf * xf, axis=-1, keepdims=True) + EPS)
    return (y * g.astype(jnp.float32)).astype(x.dtype)

def layer_norm(x, g, b):
    xf = x.astype(jnp.float32)
    mu = jnp.mean(xf, axis=-1, keepdims=True)
    var = jnp.mean(jnp.square(xf - mu), axis=-1, keepdims=True)
    y = (xf - mu) * lax.rsqrt(var + EPS)
    return (y * g.astype(jnp.float32) + b.astype(jnp.float32)).astype(x.dtype)

def rope_tables(positions):
    inv_freq = 1.0 / (ROPE_THETA ** (jnp.arange(0, QK_ROPE_DIM, 2, dtype=jnp.float32) / QK_ROPE_DIM))
    ang = positions.astype(jnp.float32)[..., None] * inv_freq
    return jnp.cos(ang), jnp.sin(ang)

def apply_rope(x, cos, sin):
    half = x.shape[-1] // 2
    x1 = x[..., :half].astype(jnp.float32)
    x2 = x[..., half:].astype(jnp.float32)
    c = cos[:, :, None, :]
    s = sin[:, :, None, :]
    return jnp.concatenate([x1 * c - x2 * s, x2 * c + x1 * s], axis=-1).astype(x.dtype)

def mla_group(c_q, c_kv, k_rope, cos, sin, q_latent_g, w_uq, kv_latent_g, w_ukv, q_head_g, k_head_g):
    B, S, _ = c_q.shape
    q = jnp.einsum('bsr,rk->bsk', rms_norm(c_q, q_latent_g), w_uq).reshape(B, S, N_ATTN_HEADS, QK_HEAD_DIM)
    kv = jnp.einsum('bsr,rk->bsk', rms_norm(c_kv, kv_latent_g), w_ukv).reshape(
        B, S, N_ATTN_HEADS, QK_NOPE_DIM + V_HEAD_DIM)
    k_nope, v = kv[..., :QK_NOPE_DIM], kv[..., QK_NOPE_DIM:]
    k_r = jnp.broadcast_to(k_rope[:, :, None, :], (B, S, N_ATTN_HEADS, QK_ROPE_DIM))
    k = jnp.concatenate([k_nope, k_r], axis=-1)
    q = rms_norm(q, q_head_g)
    k = rms_norm(k, k_head_g)
    q = jnp.concatenate([q[..., :QK_NOPE_DIM], apply_rope(q[..., QK_NOPE_DIM:], cos, sin)], axis=-1)
    k = jnp.concatenate([k[..., :QK_NOPE_DIM], apply_rope(k[..., QK_NOPE_DIM:], cos, sin)], axis=-1)
    scale = 1.0 / math.sqrt(QK_HEAD_DIM)
    n_blocks = S // Q_BLOCK
    qb = q.reshape(B, n_blocks, Q_BLOCK, N_ATTN_HEADS, QK_HEAD_DIM).transpose(1, 0, 3, 2, 4)
    kt = k.transpose(0, 2, 1, 3)
    vt = v.transpose(0, 2, 1, 3)

    def attend(q_blk):
        s = jnp.einsum('bhqd,bhkd->bhqk', q_blk, kt, preferred_element_type=jnp.float32) * scale
        p = jax.nn.softmax(s, axis=-1).astype(vt.dtype)
        return jnp.einsum('bhqk,bhkd->bhqd', p, vt)

    o = lax.map(attend, qb)
    return o.transpose(1, 0, 3, 2, 4).reshape(B, S, ATTN_WIDTH)

def conv_group(u, conv_w, conv_b, conv_norm_g, conv_norm_b):
    a, g = u[..., :CONV_CH], u[..., CONV_CH:]
    y = a * jax.nn.sigmoid(g)
    y = lax.conv_general_dilated(
        y, conv_w[:, None, :].astype(y.dtype), window_strides=(1,), padding=[(CONV_PAD, CONV_PAD)],
        dimension_numbers=('NWC', 'WIO', 'NWC'), feature_group_count=CONV_CH)
    y = y + conv_b
    return jax.nn.silu(layer_norm(y, conv_norm_g, conv_norm_b))

def expert_choice_ffn(h, w_router, w_gate, w_up, w_down):
    B, S, D = h.shape
    cap = CAPACITY_FACTOR * S // N_EXPERTS
    logits = jnp.einsum('bsd,de->bse', h, w_router).astype(jnp.float32)
    aff = jax.nn.softmax(logits, axis=-1)
    gate, idx = lax.top_k(aff.transpose(0, 2, 1), cap)
    xe = jax.vmap(lambda hb, ib: hb[ib])(h, idx)
    hid = jax.nn.silu(jnp.einsum('becd,edf->becf', xe, w_gate)) * jnp.einsum('becd,edf->becf', xe, w_up)
    ye = jnp.einsum('becf,efd->becd', hid, w_down) * gate[..., None].astype(h.dtype)
    return jax.vmap(lambda ib, yb: jnp.zeros((S, D), yb.dtype).at[ib.reshape(-1)].add(yb.reshape(-1, D)))(idx, ye)

def first_inputs(seed: int = 0) -> dict:
    key = jax.random.key(seed)
    ks = jax.random.split(key, 24)
    f32 = jnp.float32
    nrm = lambda k, shape, s: jax.random.normal(k, shape, f32) * s
    gain = lambda k, shape: 1.0 + 0.05 * jax.random.normal(k, shape, f32)
    L = DEPTH
    offset = jax.random.randint(ks[2], (BATCH, 1), 0, 1024, dtype=jnp.int32)
    positions = offset + jnp.arange(SEQ, dtype=jnp.int32)[None, :]
    return {
        "x": nrm(ks[0], (BATCH, SEQ, D_MODEL), 1.0),
        "c": nrm(ks[1], (BATCH, D_MODEL), 1.0),
        "positions": positions,
        "norm1_g": gain(ks[3], (L, D_MODEL)),
        "w_ada": nrm(ks[4], (L, D_MODEL, N_MOD * D_MODEL), 0.5 * D_MODEL ** -0.5),
        "b_ada": nrm(ks[5], (L, N_MOD * D_MODEL), 0.01),
        "w_in": nrm(ks[6], (L, D_MODEL, IN_WIDTH), D_MODEL ** -0.5),
        "q_latent_g": gain(ks[7], (L, Q_RANK)),
        "w_uq": nrm(ks[8], (L, Q_RANK, N_ATTN_HEADS * QK_HEAD_DIM), Q_RANK ** -0.5),
        "kv_latent_g": gain(ks[9], (L, KV_RANK)),
        "w_ukv": nrm(ks[10], (L, KV_RANK, N_ATTN_HEADS * (QK_NOPE_DIM + V_HEAD_DIM)), KV_RANK ** -0.5),
        "q_head_g": gain(ks[11], (L, QK_HEAD_DIM)),
        "k_head_g": gain(ks[12], (L, QK_HEAD_DIM)),
        "conv_w": nrm(ks[13], (L, CONV_WIDTH, CONV_CH), CONV_WIDTH ** -0.5),
        "conv_b": nrm(ks[14], (L, CONV_CH), 0.01),
        "conv_norm_g": gain(ks[15], (L, CONV_CH)),
        "conv_norm_b": nrm(ks[16], (L, CONV_CH), 0.01),
        "w_out": nrm(ks[17], (L, D_MIX, D_MODEL), D_MIX ** -0.5),
        "norm2_g": gain(ks[18], (L, D_MODEL)),
        "w_router": nrm(ks[19], (L, D_MODEL, N_EXPERTS), D_MODEL ** -0.5),
        "w_gate": nrm(ks[20], (L, N_EXPERTS, D_MODEL, EXPERT_FF), D_MODEL ** -0.5),
        "w_up": nrm(ks[21], (L, N_EXPERTS, D_MODEL, EXPERT_FF), D_MODEL ** -0.5),
        "w_down": nrm(ks[22], (L, N_EXPERTS, EXPERT_FF, D_MODEL), EXPERT_FF ** -0.5),
    }

def first_block(x, c, positions, norm1_g, w_ada, b_ada, w_in, q_latent_g, w_uq, kv_latent_g, w_ukv,
              q_head_g, k_head_g, conv_w, conv_b, conv_norm_g, conv_norm_b, w_out, norm2_g,
              w_router, w_gate, w_up, w_down):
    cos, sin = rope_tables(positions)
    c_act = jax.nn.silu(c)
    o1 = Q_RANK
    o2 = o1 + KV_RANK
    o3 = o2 + QK_ROPE_DIM
    for l in range(DEPTH):
        mod = jnp.einsum('bd,dk->bk', c_act, w_ada[l]) + b_ada[l]
        shift1, scale1, gate1, shift2, scale2, gate2 = [m[:, None, :] for m in jnp.split(mod, N_MOD, axis=-1)]
        h = rms_norm(x, norm1_g[l]) * (1.0 + scale1) + shift1
        proj = jnp.einsum('bsd,dk->bsk', h, w_in[l])
        c_q, c_kv = proj[..., :o1], proj[..., o1:o2]
        k_rope = proj[..., o2:o3]
        conv_u = proj[..., o3:]
        attn_out = mla_group(c_q, c_kv, k_rope, cos, sin, q_latent_g[l], w_uq[l], kv_latent_g[l], w_ukv[l],
                             q_head_g[l], k_head_g[l])
        conv_out = conv_group(conv_u, conv_w[l], conv_b[l], conv_norm_g[l], conv_norm_b[l])
        mix = jnp.einsum('bsk,kd->bsd', jnp.concatenate([attn_out, conv_out], axis=-1), w_out[l])
        x = x + gate1 * mix
        h2 = rms_norm(x, norm2_g[l]) * (1.0 + scale2) + shift2
        x = x + gate2 * expert_choice_ffn(h2, w_router[l], w_gate[l], w_up[l], w_down[l])
    return x


DEPTH_2 = 1

HEAD_DIM = 64
D_A = D_MODEL // 4
D_B = 3 * D_MODEL // 8
D_C = 3 * D_MODEL // 8
D_MIX_2 = D_A + D_B + D_C
N_HEADS_A = D_A // HEAD_DIM
N_BLOCKS_B = D_B // HEAD_DIM
N_HEADS_C = D_C // HEAD_DIM
CHUNK = 128
CONV_B = 4
LRU_C = 8.0
LORA_W = 64
LORA_A = 64
LORA_G = 128
D_FF = 2816
CONV_FF = 3
LN_EPS = 1e-5
GN_EPS = 64e-5
P_A = 2 * D_A
P_B = 2 * D_B
P_C = 3 * D_C + LORA_W + LORA_A + LORA_G
P_IN = P_A + P_B + P_C


def rms_norm_2(x, g):
    xf = x.astype(jnp.float32)
    y = xf * lax.rsqrt(jnp.mean(xf * xf, axis=-1, keepdims=True) + EPS)
    return (y * g.astype(jnp.float32)).astype(x.dtype)

def causal_dwconv(x, w, b):
    k_w = w.shape[0]
    s = x.shape[1]
    xp = jnp.pad(x, ((0, 0), (k_w - 1, 0), (0, 0)))
    y = b + w[0] * xp[:, 0:s]
    for j in range(1, k_w):
        y = y + w[j] * xp[:, j:j + s]
    return y

def token_shift(x):
    return jnp.pad(x[:, :-1], ((0, 0), (1, 0), (0, 0)))

def chunked_sgu(p, ln_g, ln_b, w_s, b_s):
    z = jax.nn.gelu(p)
    u, v = jnp.split(z, 2, axis=-1)
    vf = v.astype(jnp.float32)
    mu = jnp.mean(vf, axis=-1, keepdims=True)
    var = jnp.mean(jnp.square(vf - mu), axis=-1, keepdims=True)
    v = ((vf - mu) * lax.rsqrt(var + LN_EPS) * ln_g.astype(jnp.float32) + ln_b.astype(jnp.float32)).astype(p.dtype)
    bn, s, _ = v.shape
    v = v.reshape(bn, s // CHUNK, CHUNK, N_HEADS_A, HEAD_DIM)
    mask = jnp.tril(jnp.ones((CHUNK, CHUNK), dtype=bool))
    w = jnp.where(mask, w_s, 0.0)
    mixed = jnp.einsum('hts,bnshd->bnthd', w, v) + b_s.T[None, None, :, :, None]
    return u * mixed.reshape(bn, s, D_A)

def rg_lru_block(p, conv_w, conv_b, w_ra, b_ra, w_ix, b_ix, lam):
    xr, yg = jnp.split(p, 2, axis=-1)
    xr = causal_dwconv(xr, conv_w, conv_b)
    bn, s, _ = xr.shape
    xh = xr.reshape(bn, s, N_BLOCKS_B, HEAD_DIM)
    r = jax.nn.sigmoid(jnp.einsum('bshi,hij->bshj', xh, w_ra).reshape(bn, s, D_B) + b_ra)
    i = jax.nn.sigmoid(jnp.einsum('bshi,hij->bshj', xh, w_ix).reshape(bn, s, D_B) + b_ix)
    log_a = (-LRU_C * r.astype(jnp.float32)) * jax.nn.softplus(-lam.astype(jnp.float32))
    a = jnp.exp(log_a)
    bterm = jnp.sqrt(-jnp.expm1(2.0 * log_a)) * (i * xr).astype(jnp.float32)

    def combine(left, right):
        a1, b1 = left
        a2, b2 = right
        return a1 * a2, a2 * b1 + b2

    _, h = lax.associative_scan(combine, (a, bterm), axis=1)
    return jax.nn.gelu(yg) * h.astype(p.dtype)

def rwkv7_time_mix(p, mu, w0, w2, a0, a2, g2, k_k, k_a, r_k, ln_w, ln_b):
    p = p + (token_shift(p) - p) * mu
    r, k, v, xw, xa, xg = jnp.split(
        p, [D_C, 2 * D_C, 3 * D_C, 3 * D_C + LORA_W, 3 * D_C + LORA_W + LORA_A], axis=-1)
    w = -jax.nn.softplus(-(w0 + jnp.tanh(xw) @ w2)) - 0.5
    decay = jnp.exp(-jnp.exp(w.astype(jnp.float32)))
    a = jax.nn.sigmoid(a0 + xa @ a2)
    g = jax.nn.sigmoid(xg) @ g2
    bn, s, _ = r.shape

    def heads(t):
        return t.astype(jnp.float32).reshape(bn, s, N_HEADS_C, HEAD_DIM)

    kk = heads(k * k_k)
    kk = kk * lax.rsqrt(jnp.maximum(jnp.sum(kk * kk, axis=-1, keepdims=True), 1e-24))
    k = k * (1.0 + (a - 1.0) * k_a)
    rh, kh, vh, wh, ah = heads(r), heads(k), heads(v), heads(decay), heads(a)

    def step(state, inp):
        r_t, w_t, k_t, v_t, kk_t, a_t = inp
        sa = jnp.einsum('bhvk,bhk->bhv', state, kk_t)
        state = (state * w_t[:, :, None, :]
                 - sa[..., :, None] * (kk_t * a_t)[..., None, :]
                 + v_t[..., :, None] * k_t[..., None, :])
        return state, jnp.einsum('bhvk,bhk->bhv', state, r_t)

    seq_first = [jnp.moveaxis(t, 1, 0) for t in (rh, wh, kh, vh, kk, ah)]
    state0 = jnp.zeros((bn, N_HEADS_C, HEAD_DIM, HEAD_DIM), jnp.float32)
    _, out = lax.scan(step, state0, tuple(seq_first))
    out = jnp.moveaxis(out, 0, 1)
    mean = jnp.mean(out, axis=-1, keepdims=True)
    var = jnp.mean(jnp.square(out - mean), axis=-1, keepdims=True)
    out = ((out - mean) * lax.rsqrt(var + GN_EPS) * ln_w.astype(jnp.float32).reshape(N_HEADS_C, HEAD_DIM)
           + ln_b.astype(jnp.float32).reshape(N_HEADS_C, HEAD_DIM))
    bonus = jnp.sum(rh * kh * r_k.astype(jnp.float32), axis=-1, keepdims=True) * vh
    out = (out + bonus).reshape(bn, s, D_C).astype(p.dtype)
    return out * g

def conv_glu_ffn(h, w_up, conv_w, conv_b, w_down):
    gate, val = jnp.split(h @ w_up, 2, axis=-1)
    gate = causal_dwconv(gate, conv_w, conv_b)
    return (jax.nn.silu(gate) * val) @ w_down

def second_inputs(seed: int = 0) -> dict:
    key = jax.random.key(seed)
    ks = jax.random.split(key, 40)
    f32 = jnp.float32
    nrm = lambda k, shape, s: jax.random.normal(k, shape, f32) * s
    L = DEPTH_2
    u_a = jax.random.uniform(ks[15], (L, D_B), f32, 0.9, 0.999)
    s_a = u_a ** (1.0 / LRU_C)
    return {
        "x": nrm(ks[0], (BATCH, SEQ, D_MODEL), 1.0),
        "c": nrm(ks[1], (BATCH, D_MODEL), 1.0),
        "w_mod": nrm(ks[2], (L, D_MODEL, N_MOD * D_MODEL), 0.5 * D_MODEL ** -0.5),
        "b_mod": nrm(ks[3], (L, N_MOD * D_MODEL), 0.02),
        "norm_mix": 1.0 + nrm(ks[4], (L, D_MODEL), 0.02),
        "w_in": nrm(ks[5], (L, D_MODEL, P_IN), D_MODEL ** -0.5),
        "w_out": nrm(ks[6], (L, D_MIX_2, D_MODEL), D_MIX_2 ** -0.5),
        "sgu_ln_g": 1.0 + nrm(ks[7], (L, D_A), 0.02),
        "sgu_ln_b": nrm(ks[8], (L, D_A), 0.02),
        "sgu_w": nrm(ks[9], (L, N_HEADS_A, CHUNK, CHUNK), 0.05),
        "sgu_b": 1.0 + nrm(ks[10], (L, N_HEADS_A, CHUNK), 0.02),
        "lru_conv_w": nrm(ks[11], (L, CONV_B, D_B), CONV_B ** -0.5),
        "lru_conv_b": nrm(ks[12], (L, D_B), 0.02),
        "lru_w_a": nrm(ks[13], (L, N_BLOCKS_B, HEAD_DIM, HEAD_DIM), HEAD_DIM ** -0.5),
        "lru_b_a": nrm(ks[14], (L, D_B), 0.02),
        "lru_w_x": nrm(ks[16], (L, N_BLOCKS_B, HEAD_DIM, HEAD_DIM), HEAD_DIM ** -0.5),
        "lru_b_x": nrm(ks[17], (L, D_B), 0.02),
        "lru_lambda": jnp.log(s_a) - jnp.log1p(-s_a),
        "rwkv_mu": jax.random.uniform(ks[18], (L, P_C), f32, 0.0, 1.0),
        "rwkv_w0": jax.random.uniform(ks[19], (L, D_C), f32, -6.0, -1.0),
        "rwkv_w2": nrm(ks[20], (L, LORA_W, D_C), 0.5 * LORA_W ** -0.5),
        "rwkv_a0": nrm(ks[21], (L, D_C), 0.1),
        "rwkv_a2": nrm(ks[22], (L, LORA_A, D_C), 0.5 * LORA_A ** -0.5),
        "rwkv_g2": nrm(ks[23], (L, LORA_G, D_C), LORA_G ** -0.5),
        "rwkv_k_k": 0.85 + nrm(ks[24], (L, D_C), 0.02),
        "rwkv_k_a": 1.0 + nrm(ks[25], (L, D_C), 0.02),
        "rwkv_r_k": nrm(ks[26], (L, N_HEADS_C, HEAD_DIM), 0.1),
        "rwkv_ln_w": 1.0 + nrm(ks[27], (L, D_C), 0.02),
        "rwkv_ln_b": nrm(ks[28], (L, D_C), 0.02),
        "norm_ffn": 1.0 + nrm(ks[29], (L, D_MODEL), 0.02),
        "ffn_w_up": nrm(ks[30], (L, D_MODEL, 2 * D_FF), D_MODEL ** -0.5),
        "ffn_conv_w": nrm(ks[31], (L, CONV_FF, D_FF), CONV_FF ** -0.5),
        "ffn_conv_b": nrm(ks[32], (L, D_FF), 0.02),
        "ffn_w_down": nrm(ks[33], (L, D_FF, D_MODEL), D_FF ** -0.5),
        "norm_final": 1.0 + nrm(ks[34], (D_MODEL,), 0.02),
    }

def second_block(x, c, w_mod, b_mod, norm_mix, w_in, w_out,
              sgu_ln_g, sgu_ln_b, sgu_w, sgu_b,
              lru_conv_w, lru_conv_b, lru_w_a, lru_b_a, lru_w_x, lru_b_x, lru_lambda,
              rwkv_mu, rwkv_w0, rwkv_w2, rwkv_a0, rwkv_a2, rwkv_g2, rwkv_k_k, rwkv_k_a,
              rwkv_r_k, rwkv_ln_w, rwkv_ln_b,
              norm_ffn, ffn_w_up, ffn_conv_w, ffn_conv_b, ffn_w_down, norm_final):
    c_act = jax.nn.silu(c)
    for l in range(DEPTH_2):
        mod = c_act @ w_mod[l] + b_mod[l]
        sh1, sc1, gt1, sh2, sc2, gt2 = [m[:, None, :] for m in jnp.split(mod, N_MOD, axis=-1)]
        h = rms_norm_2(x, norm_mix[l]) * (1.0 + sc1) + sh1
        p = h @ w_in[l]
        p_a, p_b, p_c = jnp.split(p, [P_A, P_A + P_B], axis=-1)
        y_a = chunked_sgu(p_a, sgu_ln_g[l], sgu_ln_b[l], sgu_w[l], sgu_b[l])
        y_b = rg_lru_block(p_b, lru_conv_w[l], lru_conv_b[l], lru_w_a[l], lru_b_a[l],
                           lru_w_x[l], lru_b_x[l], lru_lambda[l])
        y_c = rwkv7_time_mix(p_c, rwkv_mu[l], rwkv_w0[l], rwkv_w2[l], rwkv_a0[l], rwkv_a2[l],
                             rwkv_g2[l], rwkv_k_k[l], rwkv_k_a[l], rwkv_r_k[l],
                             rwkv_ln_w[l], rwkv_ln_b[l])
        y = jnp.concatenate([y_a, y_b, y_c], axis=-1) @ w_out[l]
        x = x + gt1 * y
        h = rms_norm_2(x, norm_ffn[l]) * (1.0 + sc2) + sh2
        x = x + gt2 * conv_glu_ffn(h, ffn_w_up[l], ffn_conv_w[l], ffn_conv_b[l], ffn_w_down[l])
    return rms_norm_2(x, norm_final)


_first_inputs = second_inputs


def second_inputs(seed=0):
    import zlib

    import numpy as np

    out = dict(_first_inputs(seed))
    spreads = {}
    factors = {'norm_mix': 8.0,
     'sgu_ln_g': 64.0,
     'sgu_ln_b': 64.0,
     'sgu_b': 64.0,
     'lru_conv_b': 34.712,
     'lru_b_a': 64.0,
     'lru_b_x': 64.0,
     'rwkv_w2': 64.0,
     'rwkv_a0': 8.0,
     'rwkv_k_k': 64.0,
     'rwkv_k_a': 8.0,
     'rwkv_ln_w': 64.0,
     'rwkv_ln_b': 64.0,
     'norm_ffn': 64.0,
     'ffn_conv_b': 64.0,
     'norm_final': 7.89,
     'rwkv_w0': 8.0}
    for name, (base, spread) in spreads.items():
        noise = np.random.default_rng([zlib.crc32(name.encode()), seed]).standard_normal(out[name].shape)
        drawn = base * np.exp(spread * noise) if base else spread * noise
        out[name] = __import__('jax').numpy.asarray(drawn.astype(out[name].dtype))
    for name, factor in factors.items():
        out[name] = (out[name] * factor).astype(out[name].dtype)
    return out


_narrow_inputs = second_inputs


def second_inputs(seed=0):

    out = dict(_narrow_inputs(seed))
    wider = {'sgu_ln_g': 12.0,
     'sgu_ln_b': 12.0,
     'sgu_b': 4.91,
     'lru_b_a': 5.84,
     'lru_b_x': 5.64,
     'rwkv_k_k': 12.0,
     'rwkv_ln_w': 12.0,
     'rwkv_ln_b': 12.0,
     'ffn_conv_b': 3.14,
     'norm_final': 3.17}
    for name, times in wider.items():
        mean = out[name].mean()
        out[name] = (mean + times * (out[name] - mean)).astype(out[name].dtype)
    return out


def setup_inputs(seed=0):
    out = dict(first_inputs(seed))
    for name, value in second_inputs(seed + 1).items():
        if name != "x":
            out[name + "_2"] = value
    return out


def reference(
    x, c, positions, norm1_g, w_ada, b_ada, w_in, q_latent_g, w_uq, kv_latent_g, w_ukv,
    q_head_g, k_head_g, conv_w, conv_b, conv_norm_g, conv_norm_b, w_out, norm2_g, w_router,
    w_gate, w_up, w_down, c_2, w_mod_2, b_mod_2, norm_mix_2, w_in_2, w_out_2, sgu_ln_g_2,
    sgu_ln_b_2, sgu_w_2, sgu_b_2, lru_conv_w_2, lru_conv_b_2, lru_w_a_2, lru_b_a_2, lru_w_x_2,
    lru_b_x_2, lru_lambda_2, rwkv_mu_2, rwkv_w0_2, rwkv_w2_2, rwkv_a0_2, rwkv_a2_2, rwkv_g2_2,
    rwkv_k_k_2, rwkv_k_a_2, rwkv_r_k_2, rwkv_ln_w_2, rwkv_ln_b_2, norm_ffn_2, ffn_w_up_2,
    ffn_conv_w_2, ffn_conv_b_2, ffn_w_down_2, norm_final_2,
):
    x = first_block(
        x, c, positions, norm1_g, w_ada, b_ada, w_in, q_latent_g, w_uq, kv_latent_g, w_ukv,
        q_head_g, k_head_g, conv_w, conv_b, conv_norm_g, conv_norm_b, w_out, norm2_g, w_router,
        w_gate, w_up, w_down,
    )
    return second_block(
        x, c_2, w_mod_2, b_mod_2, norm_mix_2, w_in_2, w_out_2, sgu_ln_g_2, sgu_ln_b_2, sgu_w_2,
        sgu_b_2, lru_conv_w_2, lru_conv_b_2, lru_w_a_2, lru_b_a_2, lru_w_x_2, lru_b_x_2,
        lru_lambda_2, rwkv_mu_2, rwkv_w0_2, rwkv_w2_2, rwkv_a0_2, rwkv_a2_2, rwkv_g2_2,
        rwkv_k_k_2, rwkv_k_a_2, rwkv_r_k_2, rwkv_ln_w_2, rwkv_ln_b_2, norm_ffn_2, ffn_w_up_2,
        ffn_conv_w_2, ffn_conv_b_2, ffn_w_down_2, norm_final_2,
    )


_drawn_inputs = setup_inputs


def setup_inputs(seed=0):
    import zlib

    import numpy as np

    out = dict(_drawn_inputs(seed))
    spreads = {}
    factors = {'q_latent_g': 8.0,
     'q_head_g': 8.0,
     'k_head_g': 7.7,
     'conv_b': 3.987,
     'conv_norm_b': 7.432,
     'rwkv_k_k_2': 5.958,
     'rwkv_ln_w_2': 2.809,
     'rwkv_ln_b_2': 2.916}
    for name, (base, spread) in spreads.items():
        noise = np.random.default_rng([zlib.crc32(name.encode()), seed]).standard_normal(out[name].shape)
        drawn = base * np.exp(spread * noise) if base else spread * noise
        out[name] = __import__('jax').numpy.asarray(drawn.astype(out[name].dtype))
    for name, factor in factors.items():
        out[name] = (out[name] * factor).astype(out[name].dtype)
    return out
```

```python
import math
from contextlib import ExitStack, contextmanager

import numpy as np

import concourse.bass as bass
from concourse import mybir

F32 = mybir.dt.float32
I32 = mybir.dt.int32
U32 = mybir.dt.uint32
ALU = mybir.AluOpType
ACT = mybir.ActivationFunctionType
AX_X = mybir.AxisListType.X

P = 128
S = 1024
D = 1024
KD = D // P
HALF = 512
NH = S // HALF
DEPTH = 2
N_MOD = 6
EPS = 1e-6

HEADS, NOPE, ROPE, VD = 4, 128, 64, 128
QKD = NOPE + ROPE
Q_RANK, KV_RANK = 256, 128
CONV_CH, TAPS = 512, 31
PAD = TAPS // 2
KC = CONV_CH // P
IN1 = Q_RANK + KV_RANK + ROPE + 2 * CONV_CH
QT = S // P
N_EXP, FF = 16, 1024
CAP = 2 * S // N_EXP
TOP8 = CAP // 8
ROPE_THETA = 10000.0

HD = 64
D_A, D_B, D_C = D // 4, 3 * D // 8, 3 * D // 8
KA, KB, KCC = D_A // P, D_B // P, D_C // P
LRU_C, LN_EPS, GN_EPS = 8.0, 1e-5, 64e-5
CONV_B, CONV_FF = 4, 3
D_FF = 2816
KF = D_FF // P
P_C = 3 * D_C + 256
IN2 = 2 * D_A + 2 * D_B + P_C
KP = P_C // P
CH = 64
NCH = S // CH


def columns(fields):
    at, n = {}, 0
    for name, k in fields:
        at[name] = n
        n += k
    return at, n


ONE, N_ONE = columns([("b_ada", N_MOD * KD), ("norm1_g", KD), ("norm2_g", KD), ("q_latent_g", 2),
                      ("kv_latent_g", 1), ("qg_nope", 1), ("qg_rope", 1), ("kg_nope", 1), ("kg_rope", 1),
                      ("conv_w", TAPS * KC), ("conv_b", KC), ("conv_norm_g", KC), ("conv_norm_b", KC)])
TWO, N_TWO = columns([("b_mod", N_MOD * KD), ("norm_mix", KD), ("norm_ffn", KD), ("norm_final", KD),
                      ("sgu_ln_g", KA), ("sgu_ln_b", KA), ("lru_conv_w", CONV_B * KB), ("lru_conv_b", KB),
                      ("lru_b_a", KB), ("lru_b_x", KB), ("lru_lambda", KB), ("mu", KP), ("w0", KCC),
                      ("a0", KCC), ("k_k", KCC), ("k_a", KCC), ("r_k", KCC), ("ln_w", KCC), ("ln_b", KCC),
                      ("ffn_conv_w", CONV_FF * KF), ("ffn_conv_b", KF)])
CON, N_CON = columns([("ident", P), ("ones", P), ("pair", P), ("swap", ROPE), ("slot", 1), ("inv_freq", 1),
                      ("eps", 1), ("ln_eps", 1), ("gn_eps", 1), ("token", S), ("strict", P), ("strictT", P),
                      ("upper", CH), ("causal", P), ("level0", P), ("levelsT", 6 * P)])


def constants():
    c = np.zeros((P, N_CON), np.float32)
    i, j = np.arange(P)[:, None], np.arange(P)[None, :]
    same = (i // CH) == (j // CH)

    def put(name, value):
        value = np.asarray(value, np.float32)
        c[:value.shape[0], CON[name]:CON[name] + value.shape[1]] = value

    put("ident", i == j)
    put("ones", np.ones((P, P)))
    put("pair", same)
    half = ROPE // 2
    swap = np.zeros((ROPE, ROPE))
    swap[np.arange(half) + half, np.arange(half)] = -1.0
    swap[np.arange(half), np.arange(half) + half] = 1.0
    put("swap", swap)
    put("slot", i)
    freq = (1.0 / (np.float32(ROPE_THETA) ** (np.arange(0, ROPE, 2, dtype=np.float32) / np.float32(ROPE)))).astype(np.float32)
    put("inv_freq", np.concatenate([freq, freq])[:, None])
    put("eps", np.full((P, 1), EPS))
    put("ln_eps", np.full((P, 1), LN_EPS))
    put("gn_eps", np.full((P, 1), GN_EPS))
    put("token", np.tile(np.arange(S)[None, :], (P, 1)))
    put("strict", same & (i % CH < j % CH))
    put("strictT", same & (j % CH < i % CH))
    put("upper", (i % CH) <= j[:, :CH])
    put("causal", i <= j)
    for level in range(6):
        n = 1 << level
        a, b = i % CH, j % CH
        join = same & (a // (2 * n) == b // (2 * n)) & (a % (2 * n) < n) & (b % (2 * n) >= n)
        if level == 0:
            put("level0", join)
        c[:, CON["levelsT"] + level * P:CON["levelsT"] + (level + 1) * P] = join.T
    return c


def flat(x):
    return x.rearrange("p a n -> p (a n)")


@contextmanager
def stage(nc, *names):
    with ExitStack() as held:
        sems = [held.enter_context(nc.semaphore(n)) for n in names]
        yield sems
        nc.clear_and_free_semaphores(sems)
        nc.all_engine_barrier()


class Core:

    def __init__(self, nc, ctx):
        def sb(name, shape, dt=F32):
            return ctx.enter_context(nc.sbuf_tensor(name, shape, dt, allow_name_mangling=True))

        self.nc = nc
        self.x = sb("x_res", [P, KD, S])
        self.h = sb("h_act", [P, KD, S])
        self.con = sb("con", [P, N_CON])
        self.one = sb("par_one", [P, N_ONE])
        self.two = sb("par_two", [P, N_TWO])
        self.cact = sb("cact", [P, 2, KD])
        self.mod = sb("mod", [P, N_MOD * KD])
        self.gain = sb("gain", [P, KD])
        self.ps = ctx.enter_context(nc.psum_tensor("ps", [P, 8, HALF], F32))

    def c(self, name, n=1, rows=P):
        return self.con[0:rows, CON[name]:CON[name] + n]

    def p1(self, name, j=0, rows=P, n=1):
        return self.one[0:rows, ONE[name] + j:ONE[name] + j + n]

    def p2(self, name, j=0, n=1):
        return self.two[:, TWO[name] + j:TWO[name] + j + n]


def load_inputs(core, cos, sin, xT, cT, pos, con, par_two):
    nc = core.nc
    with ExitStack() as held, stage(nc, "loaded", "c_loaded", "pos_loaded", "c_ready", "angle", "turned", "tabled") as \
            (loaded, c_loaded, pos_loaded, c_ready, angle, turned, tabled):
        craw = held.enter_context(nc.sbuf_tensor("craw", [P, 2, KD], F32, allow_name_mangling=True))
        posi = held.enter_context(nc.sbuf_tensor("posi", [ROPE, S], I32, allow_name_mangling=True))
        ang = held.enter_context(nc.sbuf_tensor("ang", [ROPE, S], F32, allow_name_mangling=True))
        cyc = held.enter_context(nc.sbuf_tensor("cyc", [ROPE, S], F32, allow_name_mangling=True))
        red = held.enter_context(nc.sbuf_tensor("red", [ROPE, 2, S], F32, allow_name_mangling=True))
        full = 2.0 * math.pi
        two_a = 6.28125
        two_b = float(np.float32(np.round((full - two_a) * 2.0 ** 20) / 2.0 ** 20))
        two_c = float(np.float32(full - two_a - two_b))
        magic = 1.5 * 2.0 ** 23
        pi_below = 3.1415925
        with nc.Block() as block:
            @block.sync
            def _(sp):
                sp.dma_start(posi[:], pos.partition_broadcast(ROPE)).then_inc(pos_loaded, 16)
                sp.dma_start(craw[:], cT).then_inc(c_loaded, 16)
                sp.dma_start(core.con[:], con).then_inc(pos_loaded, 16)
                sp.dma_start(core.two[:], par_two).then_inc(loaded, 16)
                sp.dma_start(core.x[:], xT.rearrange("(k p) s -> p k s", p=P)).then_inc(loaded, 16)
                sp.wait_ge(loaded, 32)

            @block.scalar
            def _(act):
                act.wait_ge(c_loaded, 16)
                nc.scalar.activation(core.cact[:], craw[:], ACT.Silu).then_inc(c_ready, 1)
                act.wait_ge(turned, 2)
                nc.scalar.activation(sin[:], red[:, 0, :], ACT.Sin).then_inc(tabled, 1)
                nc.scalar.activation(cos[:], red[:, 1, :], ACT.Sin).then_inc(tabled, 1)

            @block.vector
            def _(dve):
                n = [0]

                def after(ins):
                    ins.then_inc(angle, 1)
                    n[0] += 1
                    dve.wait_ge(angle, n[0])

                dve.wait_ge(pos_loaded, 32)
                after(nc.vector.tensor_copy(ang[:], posi[:]))
                after(nc.vector.tensor_scalar(ang[:], ang[:], core.c("inv_freq", rows=ROPE), None, ALU.mult))
                for j, shift in enumerate((0.0, 0.25)):
                    after(nc.vector.tensor_scalar(cyc[:], ang[:], 1.0 / full, shift, ALU.mult, ALU.add))
                    after(nc.vector.tensor_scalar(cyc[:], cyc[:], magic, None, ALU.add))
                    after(nc.vector.tensor_scalar(cyc[:], cyc[:], magic, None, ALU.subtract))
                    after(nc.vector.scalar_tensor_tensor(red[:, j, :], cyc[:], -two_a, ang[:], ALU.mult, ALU.add))
                    after(nc.vector.scalar_tensor_tensor(red[:, j, :], cyc[:], -two_b, red[:, j, :], ALU.mult, ALU.add))
                    after(nc.vector.scalar_tensor_tensor(red[:, j, :], cyc[:], -two_c, red[:, j, :], ALU.mult, ALU.add))
                    if j:
                        after(nc.vector.tensor_scalar(red[:, j, :], red[:, j, :], math.pi / 2, None, ALU.add))
                    nc.vector.tensor_scalar(red[:, j, :], red[:, j, :], pi_below, -pi_below, ALU.min, ALU.max).then_inc(turned, 1)


def modulation(core, which, w, bias, par=None):
    nc = core.nc
    slots = 4
    nm = N_MOD * KD
    with ExitStack() as held, stage(nc, "w0", "w1", "w2", "w3", "par_loaded", "used", "summed") as \
            (w0, w1, w2, w3, par_loaded, used, summed):
        wm = held.enter_context(nc.sbuf_tensor("wmod", [P, slots, N_MOD * D], F32, allow_name_mangling=True))
        acc = core.ps[:, 0, 0:nm]
        landed = [w0, w1, w2, w3]
        with nc.Block() as block:
            @block.sync
            def _(sp):
                if par is not None:
                    sp.dma_start(core.one[:], par).then_inc(par_loaded, 16)
                for k in range(KD):
                    if k >= slots:
                        sp.wait_ge(used, k - slots + 1)
                    sp.dma_start(wm[:, k % slots, :], w[k * P:(k + 1) * P, :]).then_inc(landed[k % slots], 16)

            @block.tensor
            def _(pe):
                for k in range(KD):
                    pe.wait_ge(landed[k % slots], 16 * (k // slots + 1))
                    for j in range(nm):
                        last = nc.tensor.matmul(acc[:, j:j + 1], wm[:, k % slots, j * P:(j + 1) * P],
                                                core.cact[:, which, k:k + 1], start=(k == 0 and j == 0),
                                                stop=(k == KD - 1), skip_group_check=True)
                    last.then_inc(used, 1)

            @block.vector
            def _(dve):
                dve.wait_ge(used, KD)
                if par is not None:
                    dve.wait_ge(par_loaded, 16)
                nc.vector.tensor_tensor(core.mod[:], acc, bias(), ALU.add).then_inc(summed, 1)


def normalise(core, gains, shift_at, scale_at, dest=None):
    nc = core.nc
    with ExitStack() as held, stage(nc, "squared", "summed", "rooted", "gained", "inverted", "scaled", "shifted") as \
            (squared, summed, rooted, gained, inverted, scaled, shifted):
        sq = held.enter_context(nc.sbuf_tensor("sq", [P, KD, S], F32, allow_name_mangling=True))
        std = held.enter_context(nc.sbuf_tensor("std", [P, S], F32, allow_name_mangling=True))
        rstd = held.enter_context(nc.sbuf_tensor("rstd", [P, S], F32, allow_name_mangling=True))
        out = core.h if dest is None else dest
        total = core.ps[:, 0:NH, :]
        with nc.Block() as block:
            @block.scalar
            def _(act):
                for k in range(KD):
                    nc.scalar.activation(sq[:, k, :], core.x[:, k, :], ACT.Square).then_inc(squared, 1)
                act.wait_ge(summed, 1)
                nc.scalar.activation(std[:], total, ACT.Sqrt, bias=core.c("eps"), scale=1.0 / D).then_inc(rooted, 1)
                if scale_at is not None:
                    for k in range(KD):
                        act.wait_ge(scaled, k + 1)
                        nc.scalar.activation(out[:, k, :], out[:, k, :], ACT.Identity,
                                             bias=core.mod[:, shift_at + k:shift_at + k + 1]).then_inc(shifted, 1)

            @block.tensor
            def _(pe):
                for k in range(KD):
                    pe.wait_ge(squared, k + 1)
                    for i in range(NH):
                        last = nc.tensor.matmul(core.ps[:, i, :], core.c("ones", P), sq[:, k, i * HALF:(i + 1) * HALF],
                                                start=(k == 0), stop=(k == KD - 1))
                last.then_inc(summed, 1)

            @block.vector
            def _(dve):
                if scale_at is None:
                    nc.vector.tensor_copy(core.gain[:], gains).then_inc(gained, 1)
                else:
                    nc.vector.scalar_tensor_tensor(core.gain[:], core.mod[:, scale_at:scale_at + KD], 1.0, gains,
                                                   ALU.add, ALU.mult).then_inc(gained, 1)
                dve.wait_ge(rooted, 1)
                nc.vector.reciprocal(rstd[:], std[:]).then_inc(inverted, 1)
                dve.wait_ge(inverted, 1)
                dve.wait_ge(gained, 1)
                for k in range(KD):
                    nc.vector.scalar_tensor_tensor(out[:, k, :], core.x[:, k, :], core.gain[:, k:k + 1], rstd[:],
                                                   ALU.mult, ALU.mult).then_inc(scaled, 1)


def project_one(core, w, cq, ckv, kr, y):
    nc = core.nc
    groups = [(0, P), (P, P), (Q_RANK, P), (Q_RANK + KV_RANK, ROPE)]
    first = Q_RANK + KV_RANK + ROPE
    for j in range(KC):
        groups += [(first + j * P, P), (first + CONV_CH + j * P, P)]
    plain = 4
    with ExitStack() as held, stage(nc, "w_lat", "w_conv", "grouped", "copied", "gated", "cleared") as \
            (w_lat, w_conv, grouped, copied, gated, cleared):
        ws = held.enter_context(nc.sbuf_tensor("w_in", [P, KD, IN1], F32, allow_name_mangling=True))
        sig = held.enter_context(nc.sbuf_tensor("sig", [P, 2, S], F32, allow_name_mangling=True))
        w_k = w.rearrange("(k p) n -> p k n", p=P)
        dests = [cq[:, 0, :], cq[:, 1, :], ckv[:, :], kr[:, :]]
        with nc.Block() as block:
            @block.sync
            def _(sp):
                sp.dma_start(ws[:, :, 0:first], w_k[:, :, 0:first]).then_inc(w_lat, 16)
                sp.dma_start(ws[:, :, first:IN1], w_k[:, :, first:IN1]).then_inc(w_conv, 16)

            @block.tensor
            def _(pe):
                pe.wait_ge(w_lat, 16)
                for g, (col, width) in enumerate(groups):
                    if g == plain:
                        pe.wait_ge(w_conv, 16)
                    if 4 <= g < 8:
                        pe.wait_ge(copied, g - 3)
                    elif g >= 8:
                        if g % 2 == 0:
                            pe.wait_ge(gated, (g - 8) // 2 + 1)
                        else:
                            pe.wait_ge(copied, plain + (g - 9) // 2 + 1)
                    for i in range(NH):
                        for k in range(KD):
                            last = nc.tensor.matmul(core.ps[0:width, 2 * (g % 4) + i, :], ws[:, k, col:col + width],
                                                    core.h[:, k, i * HALF:(i + 1) * HALF],
                                                    start=(k == 0), stop=(k == KD - 1))
                    last.then_inc(grouped, 1)

            @block.scalar
            def _(act):
                for g in range(plain):
                    act.wait_ge(grouped, g + 1)
                    rows = groups[g][1]
                    nc.scalar.activation(dests[g], core.ps[0:rows, 2 * g:2 * g + 2, :], ACT.Copy).then_inc(copied, 1)
                for j in range(KC):
                    g = plain + 2 * j + 1
                    act.wait_ge(grouped, g + 1)
                    if j >= 2:
                        act.wait_ge(gated, j - 1)
                    b = 2 * (g % 4)
                    nc.scalar.activation(sig[:, j % 2, :], core.ps[:, b:b + 2, :], ACT.Sigmoid).then_inc(copied, 1)

            @block.vector
            def _(dve):
                nc.vector.memset(y[:, :, 0:PAD], 0.0)
                nc.vector.memset(y[:, :, PAD + S:], 0.0).then_inc(cleared, 1)
                for j in range(KC):
                    dve.wait_ge(copied, plain + j + 1)
                    b = 2 * ((plain + 2 * j) % 4)
                    nc.vector.tensor_tensor(y[:, j, PAD:PAD + S], core.ps[:, b:b + 2, :], sig[:, j % 2, :],
                                            ALU.mult).then_inc(gated, 1)


def latent_norm(core, cq, ckv):
    nc = core.nc
    parts = [(cq, 2, Q_RANK, "q_latent_g"), (ckv, 1, KV_RANK, "kv_latent_g")]
    with ExitStack() as held, stage(nc, "squared", "summed", "rooted", "inverted", "scaled") as \
            (squared, summed, rooted, inverted, scaled):
        sq = held.enter_context(nc.sbuf_tensor("sq", [P, 3, S], F32, allow_name_mangling=True))
        std = held.enter_context(nc.sbuf_tensor("std", [P, 2, S], F32, allow_name_mangling=True))
        rstd = held.enter_context(nc.sbuf_tensor("rstd", [P, 2, S], F32, allow_name_mangling=True))

        def tile(t, k):
            return cq[:, k, :] if t is cq else ckv[:, :]
        with nc.Block() as block:
            @block.scalar
            def _(act):
                n = 0
                for t, kt, _, _ in parts:
                    for k in range(kt):
                        nc.scalar.activation(sq[:, n, :], tile(t, k), ACT.Square).then_inc(squared, 1)
                        n += 1
                for m, (_, _, width, _) in enumerate(parts):
                    act.wait_ge(summed, m + 1)
                    nc.scalar.activation(std[:, m, :], core.ps[:, 2 * m:2 * m + 2, :], ACT.Sqrt, bias=core.c("eps"),
                                         scale=1.0 / width).then_inc(rooted, 1)

            @block.tensor
            def _(pe):
                n = 0
                for m, (_, kt, _, _) in enumerate(parts):
                    for k in range(kt):
                        pe.wait_ge(squared, n + 1)
                        for i in range(NH):
                            last = nc.tensor.matmul(core.ps[:, 2 * m + i, :], core.c("ones", P),
                                                    sq[:, n, i * HALF:(i + 1) * HALF], start=(k == 0), stop=(k == kt - 1))
                        n += 1
                    last.then_inc(summed, 1)

            @block.vector
            def _(dve):
                for m, (t, kt, _, g) in enumerate(parts):
                    dve.wait_ge(rooted, m + 1)
                    nc.vector.reciprocal(rstd[:, m, :], std[:, m, :]).then_inc(inverted, 1)
                    dve.wait_ge(inverted, m + 1)
                    for k in range(kt):
                        nc.vector.scalar_tensor_tensor(tile(t, k), tile(t, k), core.p1(g, k), rstd[:, m, :],
                                                       ALU.mult, ALU.mult).then_inc(scaled, 1)


def attention(core, cos, sin, w_uq, w_ukv, cq, ckv, kr, y):
    nc = core.nc
    scale = 1.0 / math.sqrt(QKD)
    units = HEADS * QT
    taps = [(t, j) for t in range(TAPS) for j in range(KC)]
    per_unit = -(-len(taps) // units)
    with ExitStack() as held, stage(
            nc, "w_loaded", "v_made", "v_kept", "raw", "squared", "summed", "rooted", "inverted", "head_scaled",
            "turned", "part_made", "head_ready", "scores_ready", "peak_found", "shift_ready", "probs_ready",
            "total_inverted", "probs_scaled", "probs_turned", "turned_kept", "out_ready", "out_kept", "tapped") as \
            (w_loaded, v_made, v_kept, raw, squared, summed, rooted, inverted, head_scaled,
             turned, part_made, head_ready, scores_ready, peak_found, shift_ready, probs_ready,
             total_inverted, probs_scaled, probs_turned, turned_kept, out_ready, out_kept, tapped):
        def sb(name, shape):
            return held.enter_context(nc.sbuf_tensor(name, shape, F32, allow_name_mangling=True))

        wq = sb("wq", [P, 2, HEADS * QKD])
        wkv = sb("wkv", [P, HEADS * (NOPE + VD)])
        v = sb("v", [P, QT, HEADS * VD])
        nope = sb("nope", [P, 2, S])
        rope = sb("rope", [ROPE, 2, S])
        sqn = sb("sqn", [P, S])
        sqr = sb("sqr", [ROPE, S])
        std = sb("std", [P, S])
        rstd = sb("rstd", [P, S])
        rope0 = sb("rope0", [ROPE, S])
        part = sb("part", [ROPE, 2, S])
        probs = sb("probs", [P, 2, S])
        probsT = sb("probsT", [P, QT, P])
        peak = sb("peak", [P, 2])
        shift = sb("shift", [P, 2])
        total = sb("total", [P, 2])
        inv = sb("inv", [P, 2])
        ps = core.ps
        wkv_h = wkv[:, :].rearrange("p (h n) -> p h n", h=HEADS)
        with nc.Block() as block:
            @block.sync
            def _(sp):
                sp.dma_start(wkv[:], w_ukv).then_inc(w_loaded, 16)
                sp.dma_start(wq[:], w_uq.rearrange("(k p) n -> p k n", p=P)).then_inc(w_loaded, 16)

            @block.tensor
            def _(pe):
                pe.wait_ge(w_loaded, 32)
                for t in range(QT):
                    if t >= 4:
                        pe.wait_ge(v_kept, t - 3)
                    nc.tensor.matmul(ps[:, t % 4, :], ckv[:, t * P:(t + 1) * P], wkv_h[:, :, NOPE:],
                                     start=True, stop=True).then_inc(v_made, 1)
                pe.wait_ge(v_kept, QT)

                def prepare(h, key):
                    m = 2 * h + key
                    if h and not key:
                        pe.wait_ge(out_kept, QT * h)
                    if m:
                        pe.wait_ge(head_ready, m)
                    for i in range(NH):
                        cols = slice(i * HALF, (i + 1) * HALF)
                        if key:
                            last = nc.tensor.matmul(ps[:, i, :], wkv_h[:, h, 0:NOPE], ckv[:, cols], start=True, stop=True)
                            continue
                        for k in range(2):
                            nc.tensor.matmul(ps[:, i, :], wq[:, k, h * QKD:h * QKD + NOPE], cq[:, k, cols],
                                             start=(k == 0), stop=(k == 1))
                        for k in range(2):
                            last = nc.tensor.matmul(ps[0:ROPE, 2 + i, :], wq[:, k, h * QKD + NOPE:(h + 1) * QKD],
                                                    cq[:, k, cols], start=(k == 0), stop=(k == 1))
                    last.then_inc(raw, 1)
                    pe.wait_ge(squared, 2 * m + 2)
                    for i in range(NH):
                        cols = slice(i * HALF, (i + 1) * HALF)
                        nc.tensor.matmul(ps[:, 4 + i, :], core.c("ones", P), sqn[:, cols], start=True, stop=False)
                        last = nc.tensor.matmul(ps[:, 4 + i, :], core.c("ones", P, ROPE), sqr[:, cols], start=False, stop=True)
                    last.then_inc(summed, 1)
                    pe.wait_ge(head_scaled, 2 * m + 2)
                    for i in range(NH):
                        last = nc.tensor.matmul(ps[0:ROPE, 6 + i, :], core.c("swap", ROPE, ROPE),
                                                rope0[:, i * HALF:(i + 1) * HALF], start=True, stop=True)
                    last.then_inc(turned, 1)

                def scores(u):
                    h, t = divmod(u, QT)
                    if t >= 2:
                        pe.wait_ge(probs_ready, u - 1)
                    for i in range(NH):
                        cols = slice(i * HALF, (i + 1) * HALF)
                        nc.tensor.matmul(ps[:, 2 * (u % 2) + i, :], nope[:, 0, t * P:(t + 1) * P], nope[:, 1, cols],
                                         start=True, stop=False)
                        last = nc.tensor.matmul(ps[:, 2 * (u % 2) + i, :], rope[:, 0, t * P:(t + 1) * P],
                                                rope[:, 1, cols], start=False, stop=True)
                    last.then_inc(scores_ready, 1)

                def turn(u):
                    pe.wait_ge(probs_scaled, u + 1)
                    if u:
                        pe.wait_ge(turned_kept, 2 * u)
                    for k in range(QT):
                        last = nc.tensor.transpose(ps[:, 4 + k // 4, (k % 4) * P:(k % 4 + 1) * P],
                                                   probs[:, u % 2, k * P:(k + 1) * P], core.c("ident", P))
                        if k % 4 == 3:
                            last.then_inc(probs_turned, 1)

                def weigh(u):
                    h, t = divmod(u, QT)
                    if u >= 2:
                        pe.wait_ge(out_kept, u - 1)
                    for k in range(QT):
                        if k % 4 == 0:
                            pe.wait_ge(turned_kept, 2 * u + k // 4 + 1)
                        last = nc.tensor.matmul(ps[:, 6 + u % 2, 0:P], v[:, k, h * VD:(h + 1) * VD], probsT[:, k, :],
                                                start=(k == 0), stop=(k == QT - 1))
                    last.then_inc(out_ready, 1)

                for h in range(HEADS):
                    prepare(h, 0)
                    prepare(h, 1)
                    pe.wait_ge(head_ready, 2 * h + 2)
                    scores(QT * h)
                    for u in range(QT * h, QT * (h + 1)):
                        if u + 1 < QT * (h + 1):
                            scores(u + 1)
                        turn(u)
                        weigh(u)

            @block.scalar
            def _(act):
                for t in range(QT):
                    act.wait_ge(v_made, t + 1)
                    nc.scalar.activation(v[:, t, :], ps[:, t % 4, :], ACT.Copy).then_inc(v_kept, 1)
                for h in range(HEADS):
                    for key in range(2):
                        m = 2 * h + key
                        act.wait_ge(raw, m + 1)
                        if m:
                            act.wait_ge(summed, m)
                        nc.scalar.activation(sqn[:], ps[:, 0:2, :], ACT.Square).then_inc(squared, 1)
                        nc.scalar.activation(sqr[:], kr[:] if key else ps[0:ROPE, 2:4, :], ACT.Square).then_inc(squared, 1)
                        act.wait_ge(summed, m + 1)
                        nc.scalar.activation(std[:], ps[:, 4:6, :], ACT.Sqrt, bias=core.c("eps"),
                                             scale=1.0 / QKD).then_inc(rooted, 1)
                    for u in range(QT * h, QT * (h + 1)):
                        act.wait_ge(shift_ready, u + 1)
                        if u >= 2:
                            act.wait_ge(probs_turned, 2 * (u - 1))
                        b = 2 * (u % 2)
                        nc.scalar.activation(probs[:, u % 2, :], ps[:, b:b + 2, :], ACT.Exp, bias=shift[:, u % 2:u % 2 + 1],
                                             scale=scale, accum_out=total[:, u % 2:u % 2 + 1]).then_inc(probs_ready, 1)
                        for i in range(2):
                            act.wait_ge(probs_turned, 2 * u + i + 1)
                            if u:
                                act.wait_ge(out_ready, u)
                            nc.scalar.activation(probsT[:, 4 * i:4 * i + 4, :], ps[:, 4 + i, :], ACT.Copy).then_inc(turned_kept, 1)
                        act.wait_ge(out_ready, u + 1)
                        t = u % QT
                        nc.scalar.activation(core.h[:, h, t * P:(t + 1) * P], ps[:, 6 + u % 2, 0:P],
                                             ACT.Copy).then_inc(out_kept, 1)

            @block.vector
            def _(dve):
                done = [0]

                def tap():
                    t, j = taps[done[0]]
                    acc = core.h[:, HEADS + j, :]
                    if t == 0:
                        nc.vector.tensor_scalar(acc, y[:, j, t:t + S], core.p1("conv_w", j), core.p1("conv_b", j),
                                                ALU.mult, ALU.add).then_inc(tapped, 1)
                    else:
                        dve.wait_ge(tapped, done[0] - KC + 1)
                        nc.vector.scalar_tensor_tensor(acc, y[:, j, t:t + S], core.p1("conv_w", t * KC + j), acc,
                                                       ALU.mult, ALU.add).then_inc(tapped, 1)
                    done[0] += 1

                for h in range(HEADS):
                    for key in range(2):
                        m = 2 * h + key
                        gn, gr = ("kg_nope", "kg_rope") if key else ("qg_nope", "qg_rope")
                        dve.wait_ge(rooted, m + 1)
                        nc.vector.reciprocal(rstd[:], std[:]).then_inc(inverted, 1)
                        dve.wait_ge(inverted, m + 1)
                        nc.vector.scalar_tensor_tensor(rope0[:], kr[:] if key else ps[0:ROPE, 2:4, :], core.p1(gr, 0, ROPE),
                                                       rstd[0:ROPE, :], ALU.mult, ALU.mult).then_inc(head_scaled, 1)
                        nc.vector.scalar_tensor_tensor(nope[:, key, :], ps[:, 0:2, :], core.p1(gn), rstd[:],
                                                       ALU.mult, ALU.mult).then_inc(head_scaled, 1)
                        dve.wait_ge(head_scaled, 2 * m + 2)
                        nc.vector.tensor_tensor(part[:, 0, :], rope0[:], cos[:], ALU.mult).then_inc(part_made, 1)
                        dve.wait_ge(turned, m + 1)
                        nc.vector.tensor_tensor(part[:, 1, :], ps[0:ROPE, 6:8, :], sin[:], ALU.mult).then_inc(part_made, 1)
                        dve.wait_ge(part_made, 2 * m + 2)
                        nc.vector.tensor_tensor(rope[:, key, :], part[:, 0, :], part[:, 1, :], ALU.add).then_inc(head_ready, 1)
                    for u in range(QT * h, QT * (h + 1)):
                        b, c = 2 * (u % 2), u % 2
                        dve.wait_ge(scores_ready, u + 1)
                        nc.vector.tensor_reduce(peak[:, c:c + 1], ps[:, b:b + 2, :].rearrange("p a n -> p (a n)"), AX_X,
                                                ALU.max).then_inc(peak_found, 1)
                        dve.wait_ge(peak_found, u + 1)
                        nc.vector.tensor_scalar(shift[:, c:c + 1], peak[:, c:c + 1], -scale, None,
                                                ALU.mult).then_inc(shift_ready, 1)
                        for _ in range(per_unit):
                            if done[0] < len(taps):
                                tap()
                        dve.wait_ge(probs_ready, u + 1)
                        nc.vector.reciprocal(inv[:, c:c + 1], total[:, c:c + 1]).then_inc(total_inverted, 1)
                        dve.wait_ge(total_inverted, u + 1)
                        nc.vector.tensor_scalar(probs[:, c, :], probs[:, c, :], inv[:, c:c + 1], None,
                                                ALU.mult).then_inc(probs_scaled, 1)
                assert done[0] == len(taps)


def layer_norm(core, tiles, width, eps, lhsT, g, b, func):
    nc = core.nc
    kt = len(tiles)
    groups = kt if width == HD else 1
    with ExitStack() as held, stage(nc, "mean_sum", "centred", "squared", "summed", "rooted", "inverted", "scaled", "done") as \
            (mean_sum, centred, squared, summed, rooted, inverted, scaled, done):
        sq = held.enter_context(nc.sbuf_tensor("sq", [P, kt, S], F32, allow_name_mangling=True))
        ps = core.ps

        def group(k):
            return k if groups > 1 else 0
        with nc.Block() as block:
            @block.tensor
            def _(pe):
                for second in range(2):
                    for k in range(kt):
                        if second:
                            pe.wait_ge(squared, k + 1)
                            if k == 0:
                                pe.wait_ge(centred, kt)
                        src = sq[:, k, :] if second else tiles[k]
                        for i in range(NH):
                            last = nc.tensor.matmul(ps[:, 2 * group(k) + i, :], lhsT, src[:, i * HALF:(i + 1) * HALF],
                                                    start=(groups > 1 or k == 0), stop=(groups > 1 or k == kt - 1))
                        if groups > 1 or k == kt - 1:
                            last.then_inc(summed if second else mean_sum, 1)

            @block.scalar
            def _(act):
                for k in range(kt):
                    act.wait_ge(centred, k + 1)
                    nc.scalar.activation(sq[:, k, :], tiles[k], ACT.Square).then_inc(squared, 1)
                for q in range(groups):
                    act.wait_ge(summed, q + 1)
                    nc.scalar.activation(sq[:, q, :], flat(ps[:, 2 * q:2 * q + 2, :]), ACT.Sqrt, bias=eps,
                                         scale=1.0 / width).then_inc(rooted, 1)
                for k in range(kt):
                    act.wait_ge(scaled, k + 1)
                    nc.scalar.activation(tiles[k], tiles[k], func, bias=b(k)).then_inc(done, 1)

            @block.vector
            def _(dve):
                for k in range(kt):
                    dve.wait_ge(mean_sum, group(k) + 1)
                    q = 2 * group(k)
                    nc.vector.scalar_tensor_tensor(tiles[k], flat(ps[:, q:q + 2, :]), -1.0 / width, tiles[k],
                                                   ALU.mult, ALU.add).then_inc(centred, 1)
                for q in range(groups):
                    dve.wait_ge(rooted, q + 1)
                    nc.vector.reciprocal(sq[:, q, :], sq[:, q, :]).then_inc(inverted, 1)
                for k in range(kt):
                    dve.wait_ge(inverted, group(k) + 1)
                    nc.vector.scalar_tensor_tensor(tiles[k], tiles[k], g(k), sq[:, group(k), :],
                                                   ALU.mult, ALU.mult).then_inc(scaled, 1)


def out_projection(core, w, gate_at):
    nc = core.nc
    parts = 4
    width = D // parts
    with ExitStack() as held, stage(nc, "wa", "wb", "wc", "wd", "grouped", "added") as (wa, wb, wc, wd, grouped, added):
        ws = held.enter_context(nc.sbuf_tensor("w_out", [P, KD, D], F32, allow_name_mangling=True))
        landed = [wa, wb, wc, wd]
        with nc.Block() as block:
            @block.sync
            def _(sp):
                for i in range(parts):
                    sp.dma_start(ws[:, :, i * width:(i + 1) * width],
                                 w.rearrange("(k p) n -> p k n", p=P)[:, :, i * width:(i + 1) * width]).then_inc(landed[i], 16)

            @block.tensor
            def _(pe):
                for j in range(KD):
                    if j * P % width == 0:
                        pe.wait_ge(landed[j * P // width], 16)
                    if j >= 4:
                        pe.wait_ge(added, j - 3)
                    for i in range(NH):
                        for k in range(KD):
                            last = nc.tensor.matmul(core.ps[:, 2 * (j % 4) + i, :], ws[:, k, j * P:(j + 1) * P],
                                                    core.h[:, k, i * HALF:(i + 1) * HALF],
                                                    start=(k == 0), stop=(k == KD - 1))
                    last.then_inc(grouped, 1)

            @block.vector
            def _(dve):
                for j in range(KD):
                    dve.wait_ge(grouped, j + 1)
                    b = 2 * (j % 4)
                    nc.vector.scalar_tensor_tensor(core.x[:, j, :], core.ps[:, b:b + 2, :].rearrange("p a n -> p (a n)"),
                                                   core.mod[:, gate_at + j:gate_at + j + 1], core.x[:, j, :],
                                                   ALU.mult, ALU.add).then_inc(added, 1)


def route(core, w_router, h_rows, slot_rows, aff_rows):
    nc = core.nc
    with ExitStack() as held, stage(
            nc, "w_loaded", "logits_ready", "peak_found", "less_peak", "exp_ready", "total_ready", "aff_ready",
            "aff_turned", "affT_ready", "eights", "replaced", "ones_set", "picked", "counted", "slots_ready",
            "rows_turned", "rows_kept", "rows_out_a", "rows_out_b", "small_out") as \
            (w_loaded, logits_ready, peak_found, less_peak, exp_ready, total_ready, aff_ready,
             aff_turned, affT_ready, eights, replaced, ones_set, picked, counted, slots_ready,
             rows_turned, rows_kept, rows_out_a, rows_out_b, small_out):
        def sb(name, shape):
            return held.enter_context(nc.sbuf_tensor(name, shape, F32, allow_name_mangling=True))

        wr = sb("w_router", [P, KD, N_EXP])
        peak = sb("peak", [P, QT])
        less = sb("less", [P, QT, N_EXP])
        aff = sb("aff", [P, QT, N_EXP])
        total = sb("total", [P, QT])
        affT = sb("affT", [N_EXP, S])
        left = sb("left", [N_EXP, 2, S])
        big = sb("big", [N_EXP, 2, 8])
        ones = sb("ones_row", [N_EXP, S])
        slots = sb("slots", [N_EXP, S])
        rows = sb("rows", [P, 2, D])
        rows_out = [rows_out_a, rows_out_b]
        ps = core.ps
        logits = ps[:, 0, 0:QT * N_EXP].rearrange("p (t e) -> p t e", t=QT)
        with nc.Block() as block:
            @block.sync
            def _(sp):
                sp.dma_start(wr[:], w_router.rearrange("(k p) e -> p k e", p=P)).then_inc(w_loaded, 16)
                for t in range(QT):
                    sp.wait_ge(rows_kept, 2 * t + 2)
                    sp.dma_start(h_rows[t * P:(t + 1) * P, :], rows[:, t % 2, :]).then_inc(rows_out[t % 2], 16)
                sp.wait_ge(affT_ready, 1)
                sp.dma_start(aff_rows, affT[:]).then_inc(small_out, 16)
                sp.wait_ge(slots_ready, 1)
                sp.dma_start(slot_rows, slots[:]).then_inc(small_out, 16)
                sp.wait_ge(small_out, 32)
                sp.wait_ge(rows_out_a, 16 * QT // 2)
                sp.wait_ge(rows_out_b, 16 * QT // 2)

            @block.tensor
            def _(pe):
                pe.wait_ge(w_loaded, 16)
                for t in range(QT):
                    for k in range(KD):
                        last = nc.tensor.matmul(logits[:, t, :], core.h[:, k, t * P:(t + 1) * P], wr[:, k, :],
                                                start=(k == 0), stop=(k == KD - 1))
                last.then_inc(logits_ready, 1)
                pe.wait_ge(aff_ready, 1)
                for t in range(QT):
                    last = nc.tensor.transpose(ps[0:N_EXP, 2 + t // 4, (t % 4) * P:(t % 4 + 1) * P], aff[:, t, :], core.c("ident", P))
                last.then_inc(aff_turned, 1)
                for t in range(QT):
                    if t >= 2:
                        pe.wait_ge(rows_kept, 2 * (t - 1))
                    for k in range(KD):
                        last = nc.tensor.transpose(ps[:, 4 + 2 * (t % 2) + k // 4, (k % 4) * P:(k % 4 + 1) * P],
                                                   core.h[:, k, t * P:(t + 1) * P], core.c("ident", P))
                    last.then_inc(rows_turned, 1)

            @block.scalar
            def _(act):
                act.wait_ge(less_peak, 1)
                nc.scalar.activation(less[:], less[:], ACT.Exp).then_inc(exp_ready, 1)
                for t in range(QT):
                    act.wait_ge(rows_turned, t + 1)
                    if t >= 2:
                        act.wait_ge(rows_out[t % 2], 16 * (t // 2))
                    for i in range(2):
                        nc.scalar.activation(rows[:, t % 2, i * HALF:(i + 1) * HALF], ps[:, 4 + 2 * (t % 2) + i, :],
                                             ACT.Copy).then_inc(rows_kept, 1)

            @block.vector
            def _(dve):
                nc.vector.memset(ones[:], 1.0).then_inc(ones_set, 1)
                dve.wait_ge(logits_ready, 1)
                nc.vector.tensor_reduce(peak[:], logits, AX_X, ALU.max).then_inc(peak_found, 1)
                dve.wait_ge(peak_found, 1)
                nc.vector.tensor_tensor(less[:], logits, peak[:].unsqueeze(2).to_broadcast([P, QT, N_EXP]),
                                        ALU.subtract).then_inc(less_peak, 1)
                dve.wait_ge(exp_ready, 1)
                nc.vector.tensor_reduce(total[:], less[:], AX_X, ALU.add).then_inc(total_ready, 1)
                dve.wait_ge(total_ready, 1)
                nc.vector.reciprocal(total[:], total[:]).then_inc(total_ready, 1)
                dve.wait_ge(total_ready, 2)
                nc.vector.tensor_tensor(aff[:], less[:], total[:].unsqueeze(2).to_broadcast([P, QT, N_EXP]),
                                        ALU.mult).then_inc(aff_ready, 1)
                dve.wait_ge(aff_turned, 1)
                nc.vector.tensor_copy(affT[:], ps[0:N_EXP, 2:4, :].rearrange("p a n -> p (a n)")).then_inc(affT_ready, 1)
                dve.wait_ge(affT_ready, 1)
                for r in range(TOP8):
                    src = affT[:] if r == 0 else left[:, (r - 1) % 2, :]
                    if r:
                        dve.wait_ge(replaced, r)
                    nc.vector.max(big[:, r % 2, :], src).then_inc(eights, 1)
                    dve.wait_ge(eights, r + 1)
                    nc.vector.match_replace(left[:, r % 2, :], big[:, r % 2, :], src, -1.0).then_inc(replaced, 1)
                dve.wait_ge(replaced, TOP8)
                nc.vector.tensor_scalar(left[:, 0, :], left[:, (TOP8 - 1) % 2, :], 0.0, None, ALU.is_lt).then_inc(picked, 1)
                dve.wait_ge(picked, 1)
                dve.wait_ge(ones_set, 1)
                nc.vector.tensor_tensor_scan(slots[:], ones[:], left[:, 0, :], 0.0, ALU.mult, ALU.add).then_inc(counted, 1)
                dve.wait_ge(counted, 1)
                nc.vector.tensor_tensor(slots[:], slots[:], left[:, 0, :], ALU.mult).then_inc(counted, 1)
                dve.wait_ge(counted, 2)
                nc.vector.tensor_scalar(slots[:], slots[:], -1.0, None, ALU.add).then_inc(slots_ready, 1)


def experts(core, w_gate, w_up, w_down, h_rows, slot_rows, aff_rows, gate_at):
    nc = core.nc
    per = 4
    kp = KD // per
    pieces = 3 * per
    groups = KD * NH
    last_e = N_EXP - 1
    names = [f"w{i}" for i in range(pieces)]
    with ExitStack() as held, stage(
            nc, *names, "w_used", "rows_loaded", "sel_built", "idx_summed", "idx_built", "gate_built", "gathered",
            "xe_turned", "xeT_kept", "silu_ready", "hid_ready", "hid_turned", "hidT_kept",
            "ye_kept", "brought", "added", "spare_set") as sems:
        landed = sems[0:pieces]
        (w_used, rows_loaded, sel_built, idx_summed, idx_built, gate_built, gathered, xe_turned, xeT_kept,
         silu_ready, hid_ready, hid_turned, hidT_kept, ye_kept, brought, added, spare_set) = sems[pieces:]

        def sb(name, shape, dt=F32):
            return held.enter_context(nc.sbuf_tensor(name, shape, dt, allow_name_mangling=True))

        ring = sb("w_ring", [P, pieces, kp, FF])
        sel = sb("sel", [P, 2, S])
        idxf = sb("idxf", [P, 2])
        idx = sb("idx", [P, 2], U32)
        gate = sb("gate", [P, 2])
        xe, xeT, sg, hid, hidT, ye, slot_b, aff_b = (core.h[:, i, :] for i in range(8))
        junk = sb("junk", [P, S])
        spare = sb("spare", [P, 2])
        ps = core.ps
        mats = [w_gate, w_up, w_down]

        with nc.Block() as block:
            def load(eng, e, c):
                eng.dma_start(ring[:, c, :, :], mats[c // per][e].rearrange("(k p) f -> p k f", p=P)[
                    :, (c % per) * kp:(c % per + 1) * kp, :]).then_inc(landed[c], 16)

            @block.sync
            def _(sp):
                for c in range(pieces):
                    load(sp, 0, c)
                with sp.Fori(1, N_EXP) as e:
                    for c in range(pieces):
                        sp.wait_ge(w_used, (e - 1) * pieces + (c + 1))
                        load(sp, e, c)

            @block.gpsimd
            def _(pool):
                def rows(e):
                    pool.dma_start(slot_b, slot_rows[e].partition_broadcast(P)).then_inc(rows_loaded, 16)
                    pool.dma_start(aff_b, aff_rows[e].partition_broadcast(P)).then_inc(rows_loaded, 16)

                def gather(e, b):
                    pool.wait_ge(spare_set, e + 1)
                    pool.wait_ge(idx_built, e + 1)
                    nc.gpsimd.tensor_tensor(spare[:, 1:2], spare[:, 0:1], spare[:, 0:1], ALU.add).then_inc(spare_set, 1)
                    nc.gpsimd.indirect_dma_start(xe, None, h_rows, bass.IndirectOffsetOnAxis(ap=idx[:, b:b + 1], axis=0),
                                                 ).then_inc(gathered, 16)

                nc.gpsimd.memset(spare[:], 0.0).then_inc(spare_set, 1)
                pool.wait_ge(spare_set, 1)
                rows(0)
                gather(0, 0)

                def ahead(e, b):
                    pool.wait_ge(sel_built, e)
                    pool.wait_ge(gate_built, e)
                    rows(e)
                    pool.wait_ge(xe_turned, e)
                    gather(e, b)

                with pool.Fori(0, N_EXP // 2 - 1) as i:
                    ahead(2 * i + 1, 1)
                    ahead(2 * i + 2, 0)
                ahead(last_e, 1)

            @block.tensor
            def _(pe):
                def turn_tokens(e):
                    pe.wait_ge(gathered, 16 * (e + 1))
                    for k in range(KD):
                        last = nc.tensor.transpose(ps[:, 6 + k // 4, (k % 4) * P:(k % 4 + 1) * P],
                                                   xe[:, k * P:(k + 1) * P], core.c("ident", P))
                    last.then_inc(xe_turned, 1)

                def product(e, m, lhs, bank):
                    for k in range(KD):
                        c = m * per + k // kp
                        if k % kp == 0:
                            pe.wait_ge(landed[c], 16 * (e + 1))
                        for i in range(2):
                            last = nc.tensor.matmul(ps[:, bank + i, :], lhs[:, k * P:(k + 1) * P],
                                                    ring[:, c, k % kp, i * HALF:(i + 1) * HALF],
                                                    start=(k == 0), stop=(k == KD - 1))
                        if k % kp == kp - 1 and k < KD - 1:
                            last.then_inc(w_used, 1)
                    return last

                def bring_back(e, b):
                    pe.wait_ge(sel_built, e + 1)
                    pe.wait_ge(ye_kept, e + 1)
                    for n in range(groups):
                        j, i = divmod(n, NH)
                        if n >= 4:
                            pe.wait_ge(added, groups * e + (n - 3))
                        nc.tensor.matmul(ps[:, 4 + n % 4, :], ye[:, j * P:(j + 1) * P], sel[:, b, i * HALF:(i + 1) * HALF],
                                         start=True, stop=True).then_inc(brought, 1)

                def turn_hidden(e):
                    pe.wait_ge(hid_ready, e + 1)
                    for k in range(KD):
                        last = nc.tensor.transpose(ps[:, 4 + k // 4, (k % 4) * P:(k % 4 + 1) * P],
                                                   hid[:, k * P:(k + 1) * P], core.c("ident", P))
                    last.then_inc(hid_turned, 1)

                def expert(e, b, first=False, final=False):
                    pe.wait_ge(xeT_kept, 2 * (e + 1))
                    product(e, 0, xeT, 0).then_inc(w_used, 1)
                    if not first:
                        pe.wait_ge(ye_kept, e)
                    product(e, 1, xeT, 2).then_inc(w_used, 1)
                    if not first:
                        bring_back(e - 1, 1 - b)
                        pe.wait_ge(added, groups * e)
                    turn_hidden(e)
                    if not final:
                        turn_tokens(e + 1)
                    pe.wait_ge(hidT_kept, 2 * (e + 1))
                    product(e, 2, hidT, 2).then_inc(w_used, 1)

                turn_tokens(0)
                expert(0, 0, first=True)
                with pe.Fori(0, N_EXP // 2 - 1) as i:
                    expert(2 * i + 1, 1)
                    expert(2 * i + 2, 0)
                expert(last_e, 1, final=True)
                bring_back(last_e, 1)

            @block.scalar
            def _(act):
                def keep_tokens(e):
                    act.wait_ge(xe_turned, e + 1)
                    for i in range(2):
                        nc.scalar.activation(xeT[:, i * HALF:(i + 1) * HALF], ps[:, 6 + i, :], ACT.Copy).then_inc(xeT_kept, 1)

                def keep_result(e, b):
                    act.wait_ge(w_used, pieces * (e + 1))
                    act.wait_ge(gate_built, e + 1)
                    nc.scalar.activation(ye, ps[:, 2:4, :].rearrange("p a n -> p (a n)"), ACT.Copy,
                                         scale=gate[:, b:b + 1]).then_inc(ye_kept, 1)

                def expert(e, b, first=False, final=False):
                    if not first:
                        keep_result(e - 1, 1 - b)
                    act.wait_ge(w_used, pieces * e + per)
                    nc.scalar.activation(sg, ps[:, 0:2, :].rearrange("p a n -> p (a n)"), ACT.Silu).then_inc(silu_ready, 1)
                    act.wait_ge(hid_turned, e + 1)
                    for i in range(2):
                        nc.scalar.activation(hidT[:, i * HALF:(i + 1) * HALF], ps[:, 4 + i, :], ACT.Copy).then_inc(hidT_kept, 1)
                    if not final:
                        keep_tokens(e + 1)

                keep_tokens(0)
                expert(0, 0, first=True)
                with act.Fori(0, N_EXP // 2 - 1) as i:
                    expert(2 * i + 1, 1)
                    expert(2 * i + 2, 0)
                expert(last_e, 1, final=True)
                keep_result(last_e, 1)

            @block.vector
            def _(dve):
                def find(e, b):
                    dve.wait_ge(rows_loaded, 32 * (e + 1))
                    nc.vector.scalar_tensor_tensor(junk[:], slot_b, core.c("slot"), core.c("token", S), ALU.is_equal,
                                                   ALU.mult, accum_out=idxf[:, b:b + 1]).then_inc(idx_summed, 1)
                    dve.wait_ge(idx_summed, e + 1)
                    nc.vector.tensor_copy(idx[:, b:b + 1], idxf[:, b:b + 1]).then_inc(idx_built, 1)
                    nc.vector.scalar_tensor_tensor(junk[:], slot_b, core.c("slot"), aff_b, ALU.is_equal,
                                                   ALU.mult, accum_out=gate[:, b:b + 1]).then_inc(gate_built, 1)

                def select(e, b):
                    nc.vector.tensor_scalar(sel[:, b, :], slot_b, core.c("slot"), None, ALU.is_equal).then_inc(sel_built, 1)

                def add(e):
                    for n in range(groups):
                        j, i = divmod(n, NH)
                        cols = slice(i * HALF, (i + 1) * HALF)
                        dve.wait_ge(brought, groups * e + (n + 1))
                        nc.vector.scalar_tensor_tensor(core.x[:, j, cols], ps[:, 4 + n % 4, :],
                                                       core.mod[:, gate_at + j:gate_at + j + 1], core.x[:, j, cols],
                                                       ALU.mult, ALU.add).then_inc(added, 1)

                def expert(e, b, first=False, final=False):
                    if not final:
                        if not first:
                            dve.wait_ge(ye_kept, e)
                        find(e + 1, 1 - b)
                    dve.wait_ge(silu_ready, e + 1)
                    dve.wait_ge(w_used, pieces * e + 2 * per)
                    nc.vector.tensor_tensor(hid, sg, ps[:, 2:4, :].rearrange("p a n -> p (a n)"), ALU.mult).then_inc(hid_ready, 1)
                    if not first:
                        add(e - 1)
                    if not final:
                        select(e + 1, 1 - b)

                find(0, 0)
                select(0, 0)
                expert(0, 0, first=True)
                with dve.Fori(0, N_EXP // 2 - 1) as i:
                    expert(2 * i + 1, 1)
                    expert(2 * i + 2, 0)
                expert(last_e, 1, final=True)
                add(last_e)


def store_output(core, src, out):
    nc = core.nc
    with stage(nc, "stored") as (stored,):
        with nc.Block() as block:
            @block.sync
            def _(sp):
                sp.dma_start(out.rearrange("(k p) s -> p k s", p=P), src[:]).then_inc(stored, 16)
                sp.wait_ge(stored, 16)


T_U, T_V, T_XR, T_YG = 0, KA, 2 * KA, 2 * KA + KB
T_R = 2 * KA + 2 * KB
T_K, T_VV, T_WA, T_XG = T_R + KCC, T_R + 2 * KCC, T_R + 3 * KCC, T_R + 3 * KCC + 1
N_P = IN2 // P


def project_two(core, w, p):
    nc = core.nc
    slots = 4
    gelus = set(range(T_U, T_XR)) | set(range(T_YG, T_R))
    with ExitStack() as held, stage(nc, "w0", "w1", "w2", "w3", "grouped", "kept") as (w0, w1, w2, w3, grouped, kept):
        ws = held.enter_context(nc.sbuf_tensor("w_block", [P, slots, KD, P], F32, allow_name_mangling=True))
        landed = [w0, w1, w2, w3]
        w_k = w.rearrange("(k p) n -> p k n", p=P)
        with nc.Block() as block:
            @block.sync
            def _(sp):
                for g in range(N_P):
                    if g >= slots:
                        sp.wait_ge(grouped, g - slots + 1)
                    sp.dma_start(ws[:, g % slots, :, :], w_k[:, :, g * P:(g + 1) * P]).then_inc(landed[g % slots], 16)

            @block.tensor
            def _(pe):
                for g in range(N_P):
                    pe.wait_ge(landed[g % slots], 16 * (g // slots + 1))
                    if g >= 4:
                        pe.wait_ge(kept, g - 3)
                    for i in range(NH):
                        for k in range(KD):
                            last = nc.tensor.matmul(core.ps[:, 2 * (g % 4) + i, :], ws[:, g % slots, k, :],
                                                    core.h[:, k, i * HALF:(i + 1) * HALF],
                                                    start=(k == 0), stop=(k == KD - 1))
                    last.then_inc(grouped, 1)

            @block.scalar
            def _(act):
                for g in range(N_P):
                    act.wait_ge(grouped, g + 1)
                    b = 2 * (g % 4)
                    nc.scalar.activation(p[:, g, :], flat(core.ps[:, b:b + 2, :]),
                                         ACT.Gelu_apprx_tanh if g in gelus else ACT.Copy).then_inc(kept, 1)


def spatial_gate(core, p, w_s, b_s):
    nc = core.nc
    heads = D_A // HD
    with ExitStack() as held, stage(nc, "loaded", "w_turned", "w_masked", "v_turned", "v_kept", "mixed", "gated") as \
            (loaded, w_turned, w_masked, v_turned, v_kept, mixed, gated):
        ws = held.enter_context(nc.sbuf_tensor("w_s", [P, heads, P], F32, allow_name_mangling=True))
        wT = held.enter_context(nc.sbuf_tensor("w_sT", [P, heads, P], F32, allow_name_mangling=True))
        bs = held.enter_context(nc.sbuf_tensor("b_s", [1, heads * P], F32, allow_name_mangling=True))
        vt = held.enter_context(nc.sbuf_tensor("v_tok", [P, QT, KA, P], F32, allow_name_mangling=True))
        ps = core.ps
        with nc.Block() as block:
            @block.sync
            def _(sp):
                sp.dma_start(ws[:], w_s.rearrange("h t s -> t h s")).then_inc(loaded, 16)
                sp.dma_start(bs[:], b_s).then_inc(loaded, 16)

            @block.tensor
            def _(pe):
                for c in range(QT):
                    for k in range(KA):
                        n = c * KA + k
                        last = nc.tensor.transpose(ps[:, n // 4, (n % 4) * P:(n % 4 + 1) * P],
                                                   p[:, T_V + k, c * P:(c + 1) * P], core.c("ident", P))
                    if n % 4 == 3:
                        last.then_inc(v_turned, 1)
                pe.wait_ge(loaded, 32)
                for h in range(heads):
                    last = nc.tensor.transpose(ps[:, 4, h * P:(h + 1) * P], ws[:, h, :], core.c("ident", P))
                last.then_inc(w_turned, 1)
                pe.wait_ge(w_masked, 1)
                pe.wait_ge(v_kept, 4)
                for k in range(KA):
                    for c in range(QT):
                        for half in range(2):
                            h = 2 * k + half
                            out = ps[half * HD:(half + 1) * HD, 4 + 2 * k + c // 4, (c % 4) * P:(c % 4 + 1) * P]
                            nc.tensor.matmul(out, vt[:, c, k, half * HD:(half + 1) * HD], wT[:, h, :], start=True, stop=False)
                            last = nc.tensor.matmul(out, core.c("ones", HD, 1), bs[:, h * P:(h + 1) * P], start=False, stop=True)
                    last.then_inc(mixed, 1)

            @block.scalar
            def _(act):
                for b in range(4):
                    act.wait_ge(v_turned, b + 1)
                    nc.scalar.activation(vt[:, 2 * b:2 * b + 2, :, :].rearrange("p c k n -> p (c k n)"), ps[:, b, :],
                                         ACT.Copy).then_inc(v_kept, 1)

            @block.vector
            def _(dve):
                dve.wait_ge(w_turned, 1)
                mask = core.c("causal", P).unsqueeze(1).to_broadcast([P, heads, P])
                nc.vector.tensor_tensor(wT[:], ps[:, 4, :].rearrange("p (h t) -> p h t", h=heads), mask,
                                        ALU.mult).then_inc(w_masked, 1)
                for k in range(KA):
                    dve.wait_ge(mixed, k + 1)
                    nc.vector.tensor_tensor(core.h[:, k, :], p[:, T_U + k, :], flat(ps[:, 4 + 2 * k:6 + 2 * k, :]),
                                            ALU.mult).then_inc(gated, 1)


def linear_recurrence(core, p, w_a, w_x):
    nc = core.nc
    with ExitStack() as held, stage(nc, "blank", "loaded", "step", "convolved", "gates_ready", "gates_kept", "decayed",
                                    "ratio_ready", "rooted", "out_done") as \
            (blank, loaded, step, convolved, gates_ready, gates_kept, decayed, ratio_ready, rooted, out_done):
        def sb(name, shape):
            return held.enter_context(nc.sbuf_tensor(name, shape, F32, allow_name_mangling=True))

        bd = sb("w_gates", [P, 2, KB, P])
        col = sb("lam_cols", [P, 6, KB])
        xc = sb("xc", [P, S])
        r = sb("r_gate", [P, S])
        ig = sb("i_gate", [P, S])
        a = sb("a_decay", [P, S])
        t = sb("tanh", [P, S])
        u = sb("ratio", [P, S])
        ps = core.ps
        with nc.Block() as block:
            @block.gpsimd
            def _(pool):
                nc.gpsimd.memset(bd[:], 0.0).then_inc(blank, 1)

            @block.sync
            def _(sp):
                sp.wait_ge(blank, 1)
                for g, w in enumerate((w_a, w_x)):
                    for half in range(2):
                        rows = slice(half * HD, (half + 1) * HD)
                        sp.dma_start(bd[rows, g, :, half * HD:(half + 1) * HD],
                                     w.rearrange("(k two) i j -> two i k j", two=2)[half]).then_inc(loaded, 16)

            @block.tensor
            def _(pe):
                pe.wait_ge(loaded, 64)
                for k in range(KB):
                    pe.wait_ge(convolved, k + 1)
                    for g in range(2):
                        for i in range(NH):
                            last = nc.tensor.matmul(ps[:, 2 * g + i, :], bd[:, g, k, :], xc[:, i * HALF:(i + 1) * HALF],
                                                    start=True, stop=True)
                    last.then_inc(gates_ready, 1)

            @block.scalar
            def _(act):
                lam = core.p2("lru_lambda", 0, KB)
                nc.scalar.activation(col[:, 0, :], lam, ACT.Abs).then_inc(decayed, 1)
                act.wait_ge(decayed, 1)
                nc.scalar.activation(col[:, 0, :], col[:, 0, :], ACT.Exp, scale=-1.0).then_inc(decayed, 1)
                for k in range(KB):
                    act.wait_ge(gates_ready, k + 1)
                    if k:
                        act.wait_ge(out_done, k)
                    nc.scalar.activation(r[:], flat(ps[:, 0:2, :]), ACT.Sigmoid, bias=core.p2("lru_b_a", k)).then_inc(gates_kept, 1)
                    nc.scalar.activation(ig[:], flat(ps[:, 2:4, :]), ACT.Sigmoid, bias=core.p2("lru_b_x", k)).then_inc(gates_kept, 1)
                    act.wait_ge(gates_kept, 2 * k + 1)
                    if k == 0:
                        act.wait_ge(ratio_ready, 1)
                    nc.scalar.activation(t[:], r[:], ACT.Tanh, scale=col[:, 5, k:k + 1]).then_inc(decayed, 1)
                    nc.scalar.activation(a[:], r[:], ACT.Exp, scale=col[:, 4, k:k + 1]).then_inc(decayed, 1)
                    act.wait_ge(ratio_ready, k + 2)
                    nc.scalar.activation(u[:], u[:], ACT.Sqrt).then_inc(rooted, 1)

            @block.vector
            def _(dve):
                n = [0]

                def after(ins):
                    ins.then_inc(step, 1)
                    n[0] += 1
                    dve.wait_ge(step, n[0])

                dve.wait_ge(decayed, 2)
                after(nc.vector.tensor_scalar(col[:, 1, :], col[:, 0, :], 2.0, None, ALU.add))
                after(nc.vector.reciprocal(col[:, 1, :], col[:, 1, :]))
                after(nc.vector.tensor_tensor(col[:, 1, :], col[:, 1, :], col[:, 0, :], ALU.mult))
                after(nc.vector.tensor_tensor(col[:, 2, :], col[:, 1, :], col[:, 1, :], ALU.mult))
                terms = 9
                after(nc.vector.tensor_scalar(col[:, 3, :], col[:, 2, :], 1.0 / (2 * terms + 1), 1.0 / (2 * terms - 1),
                                              ALU.mult, ALU.add))
                for m in range(terms - 2, -1, -1):
                    after(nc.vector.tensor_tensor(col[:, 3, :], col[:, 3, :], col[:, 2, :], ALU.mult))
                    after(nc.vector.tensor_scalar(col[:, 3, :], col[:, 3, :], 1.0 / (2 * m + 1), None, ALU.add))
                after(nc.vector.scalar_tensor_tensor(col[:, 3, :], col[:, 3, :], 2.0, col[:, 1, :], ALU.mult, ALU.mult))
                after(nc.vector.tensor_scalar(col[:, 1, :], core.p2("lru_lambda", 0, KB), -1.0, 0.0, ALU.mult, ALU.max))
                after(nc.vector.tensor_tensor(col[:, 3, :], col[:, 3, :], col[:, 1, :], ALU.add))
                after(nc.vector.tensor_scalar(col[:, 4, :], col[:, 3, :], -LRU_C, None, ALU.mult))
                nc.vector.tensor_scalar(col[:, 5, :], col[:, 3, :], LRU_C, None, ALU.mult).then_inc(ratio_ready, 1)
                for k in range(KB):
                    x = p[:, T_XR + k, :]
                    tap = CONV_B - 1
                    after(nc.vector.tensor_scalar(xc[:], x, core.p2("lru_conv_w", tap * KB + k), core.p2("lru_conv_b", k),
                                                  ALU.mult, ALU.add))
                    for back in range(1, CONV_B):
                        ins = nc.vector.scalar_tensor_tensor(xc[:, back:], x[:, 0:S - back],
                                                             core.p2("lru_conv_w", (tap - back) * KB + k), xc[:, back:],
                                                             ALU.mult, ALU.add)
                        if back < CONV_B - 1:
                            after(ins)
                    ins.then_inc(convolved, 1)
                    dve.wait_ge(decayed, 2 + 2 * k + 1)
                    after(nc.vector.tensor_scalar(u[:], t[:], 1.0, None, ALU.add))
                    after(nc.vector.reciprocal(u[:], u[:]))
                    after(nc.vector.scalar_tensor_tensor(u[:], t[:], 2.0, u[:], ALU.mult, ALU.mult))
                    nc.vector.tensor_scalar(u[:], u[:], 2.0 ** -100, None, ALU.max).then_inc(ratio_ready, 1)
                    dve.wait_ge(gates_kept, 2 * k + 2)
                    after(nc.vector.tensor_tensor(ig[:], ig[:], xc[:], ALU.mult))
                    dve.wait_ge(rooted, k + 1)
                    after(nc.vector.tensor_tensor(ig[:], ig[:], u[:], ALU.mult))
                    dve.wait_ge(decayed, 2 + 2 * k + 2)
                    after(nc.vector.tensor_tensor_scan(t[:], a[:], ig[:], 0.0, ALU.mult, ALU.add))
                    nc.vector.tensor_tensor(core.h[:, KA + k, :], p[:, T_YG + k, :], t[:], ALU.mult).then_inc(out_done, 1)
                    dve.wait_ge(out_done, k + 1)


def delta_inputs(core, p, ex, pc, w2, a2, g2):
    nc = core.nc
    with ExitStack() as held, stage(nc, "loaded", "step", "shifted", "acted", "g_ready", "g_kept", "wa_ready",
                                    "fetch", "acted2", "pair_ready", "pair_used", "kept", "keep_set") as \
            (loaded, step, shifted, acted, g_ready, g_kept, wa_ready, fetch, acted2, pair_ready, pair_used,
             kept, keep_set):
        def sb(name, shape):
            return held.enter_context(nc.sbuf_tensor(name, shape, F32, allow_name_mangling=True))

        wa = sb("w2a2", [P, D_C])
        wg = sb("g2", [P, D_C])
        keep = sb("keep", [P, S])
        ps = core.ps
        t1, t2 = sb("t1", [P, S])[:], sb("t2", [P, S])[:]
        t0, t3 = p[:, T_YG + KB - 1, :], p[:, T_XG, :]

        def chunks(x):
            return x.rearrange("p (c t) -> p c t", t=CH)
        with nc.Block() as block:
            @block.sync
            def _(sp):
                sp.dma_start(wa[0:HD, :], w2).then_inc(loaded, 16)
                sp.dma_start(wa[HD:P, :], a2).then_inc(loaded, 16)
                sp.dma_start(wg[:], g2).then_inc(loaded, 16)

            @block.gpsimd
            def _(pool):
                nc.gpsimd.memset(keep[:], 1.0).then_inc(keep_set, 1)
                pool.wait_ge(keep_set, 1)
                nc.gpsimd.memset(chunks(keep[:])[:, :, 0:1], 0.0).then_inc(keep_set, 1)

            @block.tensor
            def _(pe):
                pe.wait_ge(loaded, 48)
                pe.wait_ge(acted, 2)
                for q in range(KCC):
                    for i in range(NH):
                        last = nc.tensor.matmul(ps[:, 2 * q + i, :], wg[:, q * P:(q + 1) * P],
                                                t3[:, i * HALF:(i + 1) * HALF], start=True, stop=True)
                    last.then_inc(g_ready, 1)
                pe.wait_ge(g_kept, KCC)
                for q in range(KCC):
                    if q:
                        pe.wait_ge(acted2, 9 * q)
                        pe.wait_ge(pair_used, 2 * q)
                    for part in range(2):
                        rows = slice(part * HD, (part + 1) * HD)
                        for i in range(NH):
                            last = nc.tensor.matmul(ps[:, 2 * part + i, :], wa[rows, q * P:(q + 1) * P],
                                                    p[rows, T_WA, i * HALF:(i + 1) * HALF], start=True, stop=True)
                    last.then_inc(wa_ready, 1)
                    for part in range(2):
                        pe.wait_ge(fetch, 2 * q + part + 1)
                        for i in range(NH):
                            last = nc.tensor.matmul(ps[:, 4 + 2 * part + i, :], core.c("pair", P), t3[:, i * HALF:(i + 1) * HALF],
                                                    start=True, stop=True)
                        last.then_inc(pair_ready, 1)

            @block.scalar
            def _(act):
                act.wait_ge(shifted, 11)
                nc.scalar.activation(p[0:HD, T_WA, :], p[0:HD, T_WA, :], ACT.Tanh).then_inc(acted, 1)
                nc.scalar.activation(t3, t3, ACT.Sigmoid).then_inc(acted, 1)
                for q in range(KCC):
                    act.wait_ge(g_ready, q + 1)
                    nc.scalar.activation(ex[:, 3 + q, :], flat(ps[:, 2 * q:2 * q + 2, :]), ACT.Copy).then_inc(g_kept, 1)
                for q in range(KCC):
                    act.wait_ge(wa_ready, q + 1)
                    if q:
                        act.wait_ge(kept, q)
                    nc.scalar.activation(t0, flat(ps[:, 0:2, :]), ACT.Sigmoid, bias=core.p2("w0", q)).then_inc(acted2, 1)
                    nc.scalar.activation(t1, flat(ps[:, 2:4, :]), ACT.Sigmoid, bias=core.p2("a0", q)).then_inc(acted2, 1)
                    act.wait_ge(pair_used, 2 * q + 1)
                    nc.scalar.activation(p[:, q, :], p[:, q, :], ACT.Exp).then_inc(acted2, 1)
                    nc.scalar.activation(p[:, 6 + q, :], p[:, 6 + q, :], ACT.Exp).then_inc(acted2, 1)
                    nc.scalar.activation(p[:, 3 + q, :], t2, ACT.Exp, scale=-1.0).then_inc(acted2, 1)
                    nc.scalar.activation(pc[:, q, :], chunks(t2)[:, :, CH - 1], ACT.Exp).then_inc(acted2, 1)
                    nc.scalar.activation(t0, t2, ACT.Exp).then_inc(acted2, 1)
                    nc.scalar.activation(t3, t3, ACT.Sqrt).then_inc(acted2, 1)
                    act.wait_ge(fetch, 2 * q + 2)
                    act.wait_ge(shifted, 12 + q)
                    nc.scalar.activation(ex[:, q, :], t1, ACT.Copy).then_inc(acted2, 1)
                    act.wait_ge(acted2, 9 * q + 9)

            @block.vector
            def _(dve):
                n = [0]

                def after(ins):
                    ins.then_inc(step, 1)
                    n[0] += 1
                    dve.wait_ge(step, n[0])

                for j in range(KP):
                    x = p[:, T_R + j, :]
                    nc.vector.tensor_scalar(t0[:, 0:1], x[:, 0:1], -1.0, None, ALU.mult).then_inc(step, 1)
                    n[0] += 1
                    after(nc.vector.tensor_tensor(t0[:, 1:], x[:, 0:S - 1], x[:, 1:], ALU.subtract))
                    nc.vector.scalar_tensor_tensor(x, t0, core.p2("mu", j), x, ALU.mult, ALU.add).then_inc(shifted, 1)
                    dve.wait_ge(shifted, j + 1)
                dve.wait_ge(keep_set, 2)
                for q in range(KCC):
                    r, k, v = p[:, T_R + q, :], p[:, T_K + q, :], p[:, T_VV + q, :]
                    kk = h_b = core.h[:, KA + KB + q, :]
                    if q == 0:
                        dve.wait_ge(g_ready, KCC)
                    after(nc.vector.tensor_scalar(kk, k, core.p2("k_k", q), None, ALU.mult))
                    nc.vector.tensor_tensor(t3, kk, kk, ALU.mult).then_inc(fetch, 1)
                    dve.wait_ge(acted2, 9 * q + 2)
                    after(nc.vector.tensor_scalar(t0, t0, -math.exp(-0.5), None, ALU.mult))
                    after(nc.vector.tensor_tensor_scan(t2, keep[:], t0, 0.0, ALU.mult, ALU.add))
                    nc.vector.tensor_tensor(p[:, q, :], t2, t0, ALU.subtract).then_inc(step, 1)
                    last = chunks(t2)[:, :, CH - 1:CH].to_broadcast([P, NCH, CH])
                    nc.vector.tensor_tensor(chunks(p[:, 6 + q, :]), last, chunks(t2), ALU.subtract).then_inc(step, 1)
                    n[0] += 2
                    dve.wait_ge(step, n[0])
                    dve.wait_ge(pair_ready, 2 * q + 1)
                    nc.vector.tensor_scalar(t3, flat(ps[:, 4:6, :]), 1e-24, None, ALU.max).then_inc(pair_used, 1)
                    dve.wait_ge(acted2, 9 * q + 8)
                    after(nc.vector.reciprocal(t3, t3))
                    after(nc.vector.tensor_tensor(kk, kk, t3, ALU.mult))
                    after(nc.vector.tensor_tensor(p[:, q, :], p[:, q, :], kk, ALU.mult))
                    after(nc.vector.tensor_tensor(kk, kk, t1, ALU.mult))
                    after(nc.vector.tensor_scalar(t1, t1, -1.0, core.p2("k_a", q), ALU.add, ALU.mult))
                    after(nc.vector.scalar_tensor_tensor(k, t1, 1.0, k, ALU.add, ALU.mult))
                    nc.vector.scalar_tensor_tensor(t3, r, core.p2("r_k", q), k, ALU.mult, ALU.mult).then_inc(fetch, 1)
                    nc.vector.tensor_tensor(t1, k, p[:, 3 + q, :], ALU.mult).then_inc(shifted, 1)
                    dve.wait_ge(shifted, 12 + q)
                    after(nc.vector.tensor_tensor(p[:, 3 + q, :], p[:, 3 + q, :], kk, ALU.mult))
                    after(nc.vector.tensor_tensor(k, k, p[:, 6 + q, :], ALU.mult))
                    after(nc.vector.scalar_tensor_tensor(p[:, 6 + q, :], kk, -1.0, p[:, 6 + q, :], ALU.mult, ALU.mult))
                    after(nc.vector.tensor_tensor(r, r, t0, ALU.mult))
                    dve.wait_ge(pair_ready, 2 * q + 2)
                    nc.vector.tensor_tensor(h_b, v, flat(ps[:, 6:8, :]), ALU.mult).then_inc(pair_used, 1)
                    dve.wait_ge(pair_used, 2 * q + 2)
                    dve.wait_ge(acted2, 9 * q + 9)
                    nc.vector.engine_nop().then_inc(kept, 1)


def delta_chunks(core, p, ex, pc):
    nc = core.nc
    LV = 5
    with ExitStack() as held, stage(
            nc, "joined", "spread", "tok_ready", "tok_kept", "prod_ready", "first_made", "masked", "am_made", "g_ready",
            "g_kept", "xz_ready", "x_made", "z_made", "y_ready", "y_kept", "w1_ready", "w1_kept", "u_ready", "u_kept",
            "o_ready", "o_kept", "s_ready", "s_made") as \
            (joined, spread, tok_ready, tok_kept, prod_ready, first_made, masked, am_made, g_ready,
             g_kept, xz_ready, x_made, z_made, y_ready, y_kept, w1_ready, w1_kept, u_ready, u_kept,
             o_ready, o_kept, s_ready, s_made):
        def sb(name, shape=(P, KCC, P)):
            return held.enter_context(nc.sbuf_tensor(name, list(shape), F32, allow_name_mangling=True))

        wide = KCC * P
        free_a = p[:, T_WA:T_XG + 1, :].rearrange("p a s -> p (a s)")
        free_b = p[:, T_YG + KB - 1, :]

        def view(x, at, n):
            return x[:, at:at + KCC * n].rearrange("p (q n) -> p q n", q=KCC)
        kkd, bi, ki, be, ke = (view(free_a, i * wide, P) for i in range(5))
        vv, kkdT = (view(free_b, i * wide, P) for i in range(2))
        ARK = view(free_b, 2 * wide, CH)
        beT, keT, vT, X, Z, A, AM, AKK, G, Y, W1, U, ST = (
            sb(n) for n in ("beT", "keT", "vT", "X", "Z", "A", "AM", "AKK", "G", "Y", "W1", "U", "ST"))
        ARB = sb("ARB", (P, KCC, CH))
        ps = core.ps

        def bank(b):
            return ps[:, b, 0:wide].rearrange("p (q n) -> p q n", q=KCC)

        def thin(b, at=0):
            return ps[:, b, at:at + KCC * CH].rearrange("p (q n) -> p q n", q=KCC)

        def all_q(mask, n=P):
            return mask.unsqueeze(1).to_broadcast([P, KCC, n])

        def each(lhsT, rhs, out, start=True, stop=True):
            for q in range(KCC):
                last = nc.tensor.matmul(out[:, q, :], lhsT[:, q, :], rhs(q), start=start, stop=stop)
            return last

        def whole(t):
            return lambda q: t[:, q, :]
        sources = [(kkd, lambda cols: p[:, 0:KCC, cols]), (bi, lambda cols: p[:, 3:3 + KCC, cols]),
                   (ki, lambda cols: ex[:, 0:KCC, cols]), (vv, lambda cols: p[:, T_VV:T_VV + KCC, cols]),
                   (ke, lambda cols: p[:, T_K:T_K + KCC, cols]), (be, lambda cols: p[:, 6:6 + KCC, cols])]
        n_src = len(sources)
        with nc.Block() as block:
            @block.tensor
            def _(pe):
                with pe.Fori(0, NCH) as c:
                    cols = bass.ds(c * CH, CH)
                    pe.wait_ge(spread, n_src * c + n_src)
                    for b, t in enumerate((vv, kkd, ke, be)):
                        for q in range(KCC):
                            last = nc.tensor.transpose(bank(b)[:, q, :], t[:, q, :], core.c("ident", P))
                        last.then_inc(tok_ready, 1)
                    each(bi, whole(kkd), bank(4)).then_inc(prod_ready, 1)
                    each(kkd, whole(bi), bank(5)).then_inc(prod_ready, 1)
                    each(ki, whole(kkd), bank(6)).then_inc(prod_ready, 1)
                    each(ki, lambda q: p[:, T_R + q, cols], thin(7))
                    each(bi, lambda q: p[:, T_R + q, cols], thin(7, KCC * CH)).then_inc(prod_ready, 1)
                    pe.wait_ge(first_made, 2 * c + 2)
                    for m in range(LV):
                        if m:
                            pe.wait_ge(x_made, LV * c + m)
                        pe.wait_ge(am_made, LV * c + (m + 1))
                        each(AM, whole(X), bank(4)).then_inc(g_ready, 1)
                        pe.wait_ge(g_kept, LV * c + (m + 1))
                        if m:
                            pe.wait_ge(z_made, (LV - 1) * c + m)
                        else:
                            pe.wait_ge(masked, 4 * c + 4)
                        each(Z, whole(G), bank(5)).then_inc(xz_ready, 1)
                        if m < LV - 1:
                            each(G, whole(Z), bank(6)).then_inc(xz_ready, 1)
                        if m == 0:
                            pe.wait_ge(tok_kept, 4 * c + 4)
                            each(AKK, whole(vT), bank(0)).then_inc(y_ready, 1)
                    pe.wait_ge(x_made, LV * c + LV)
                    each(kkdT, whole(X), bank(1)).then_inc(w1_ready, 1)
                    pe.wait_ge(y_kept, c + 1)
                    pe.wait_ge(w1_kept, c + 1)
                    pe.wait_ge(s_made, KCC * c + KCC)
                    for q in range(KCC):
                        nc.tensor.matmul(bank(2)[:, q, :], X[:, q, :], Y[:, q, :], start=True, stop=False)
                        last = nc.tensor.matmul(bank(2)[:, q, :], W1[:, q, :], ST[:, q, :], start=False, stop=True)
                    last.then_inc(u_ready, 1)
                    pe.wait_ge(u_kept, c + 1)
                    for q in range(KCC):
                        out = thin(3)[:, q, :]
                        nc.tensor.matmul(out, ST[:, q, :], p[:, T_R + q, cols], start=True, stop=False)
                        nc.tensor.matmul(out, vT[:, q, :], ARK[:, q, :], start=False, stop=False)
                        last = nc.tensor.matmul(out, U[:, q, :], ARB[:, q, :], start=False, stop=True)
                    last.then_inc(o_ready, 1)
                    for q in range(KCC):
                        nc.tensor.matmul(bank(7)[:, q, :], keT[:, q, :], vT[:, q, :], start=True, stop=False)
                        last = nc.tensor.matmul(bank(7)[:, q, :], beT[:, q, :], U[:, q, :], start=False, stop=True)
                    last.then_inc(s_ready, 1)

            @block.gpsimd
            def _(pool):
                with pool.Fori(0, NCH) as c:
                    pool.wait_ge(masked, 4 * c + 1)
                    for m in range(LV):
                        if m:
                            pool.wait_ge(g_ready, LV * c + m)
                        nc.gpsimd.tensor_tensor(AM[:], A[:], all_q(core.con[:, CON["levelsT"] + (m + 1) * P:CON["levelsT"] + (m + 2) * P]),
                                                ALU.mult).then_inc(am_made, 1)

            @block.scalar
            def _(act):
                with act.Fori(0, NCH) as c:
                    cols = bass.ds(c * CH, CH)
                    for b, t in enumerate((vT, kkdT, keT, beT)):
                        act.wait_ge(tok_ready, 4 * c + (b + 1))
                        nc.scalar.activation(t[:], bank(b), ACT.Copy).then_inc(tok_kept, 1)
                    for m in range(LV):
                        act.wait_ge(g_ready, LV * c + (m + 1))
                        nc.scalar.activation(G[:], bank(4), ACT.Copy).then_inc(g_kept, 1)
                        if m == 0:
                            act.wait_ge(y_ready, c + 1)
                            nc.scalar.activation(Y[:], bank(0), ACT.Copy).then_inc(y_kept, 1)
                    act.wait_ge(w1_ready, c + 1)
                    nc.scalar.activation(W1[:], bank(1), ACT.Copy).then_inc(w1_kept, 1)
                    act.wait_ge(u_ready, c + 1)
                    nc.scalar.activation(U[:], bank(2), ACT.Copy).then_inc(u_kept, 1)
                    act.wait_ge(o_ready, c + 1)
                    nc.scalar.activation(p[:, T_R:T_R + KCC, cols], thin(3), ACT.Copy).then_inc(o_kept, 1)

            @block.vector
            def _(dve):
                for q in range(KCC):
                    nc.vector.memset(ST[:, q, :], 0.0).then_inc(s_made, 1)
                pair = core.c("pair", P).rearrange("p (h t) -> p h t", h=2)
                with dve.Fori(0, NCH) as c:
                    cols = bass.ds(c * CH, CH)
                    for t, src in sources:
                        for q in range(KCC):
                            s = src(cols)[:, q, :].unsqueeze(1).to_broadcast([P, 2, CH])
                            ins = nc.vector.tensor_tensor(t[:, q, :].rearrange("p (h n) -> p h n", h=2), s, pair, ALU.mult)
                        ins.then_inc(spread, 1)
                    dve.wait_ge(prod_ready, 4 * c + 1)
                    nc.vector.tensor_tensor(X[:], bank(4), all_q(core.c("level0", P)), ALU.mult).then_inc(joined, 1)
                    dve.wait_ge(prod_ready, 4 * c + 2)
                    nc.vector.tensor_tensor(A[:], bank(5), all_q(core.c("strictT", P)), ALU.mult).then_inc(masked, 1)
                    dve.wait_ge(joined, 2 * c + 1)
                    nc.vector.tensor_tensor(X[:], all_q(core.c("ident", P)), X[:], ALU.subtract).then_inc(first_made, 1)
                    dve.wait_ge(masked, 4 * c + 1)
                    nc.vector.tensor_tensor(Z[:], A[:], all_q(core.con[:, CON["levelsT"]:CON["levelsT"] + P]),
                                            ALU.mult).then_inc(joined, 1)
                    dve.wait_ge(joined, 2 * c + 2)
                    nc.vector.tensor_tensor(Z[:], all_q(core.c("ident", P)), Z[:], ALU.subtract).then_inc(first_made, 1)
                    dve.wait_ge(prod_ready, 4 * c + 3)
                    nc.vector.tensor_tensor(AKK[:], bank(6), all_q(core.c("strict", P)), ALU.mult).then_inc(masked, 1)
                    dve.wait_ge(prod_ready, 4 * c + 4)
                    nc.vector.tensor_tensor(ARK[:], thin(7), all_q(core.c("upper", CH), CH), ALU.mult).then_inc(masked, 1)
                    nc.vector.scalar_tensor_tensor(ARB[:], thin(7, KCC * CH), -1.0, all_q(core.c("upper", CH), CH),
                                                   ALU.mult, ALU.mult).then_inc(masked, 1)
                    for m in range(LV):
                        dve.wait_ge(xz_ready, (2 * LV - 1) * c + (2 * m + 1))
                        nc.vector.tensor_tensor(X[:], X[:], bank(5), ALU.subtract).then_inc(x_made, 1)
                        if m < LV - 1:
                            dve.wait_ge(xz_ready, (2 * LV - 1) * c + (2 * m + 2))
                            nc.vector.tensor_tensor(Z[:], Z[:], bank(6), ALU.subtract).then_inc(z_made, 1)
                            dve.wait_ge(z_made, (LV - 1) * c + (m + 1))
                        dve.wait_ge(x_made, LV * c + (m + 1))
                    dve.wait_ge(s_ready, c + 1)
                    for q in range(KCC):
                        nc.vector.scalar_tensor_tensor(ST[:, q, :], ST[:, q, :], pc[:, q, bass.ds(c, 1)], bank(7)[:, q, :],
                                                       ALU.mult, ALU.add).then_inc(s_made, 1)
                    dve.wait_ge(o_kept, c + 1)


def delta_output(core, p, ex):
    nc = core.nc
    with stage(nc, "summed", "gated") as (summed, gated):
        with nc.Block() as block:
            @block.vector
            def _(dve):
                for q in range(KCC):
                    h = core.h[:, KA + KB + q, :]
                    nc.vector.tensor_tensor(h, h, p[:, T_R + q, :], ALU.add).then_inc(summed, 1)
                    dve.wait_ge(summed, q + 1)
                    nc.vector.tensor_tensor(h, h, ex[:, 3 + q, :], ALU.mult).then_inc(gated, 1)


def ffn_up(core, w, hid):
    nc = core.nc
    edge = CONV_FF - 1
    with ExitStack() as held, stage(nc, "w0", "w1", "edges", "product_ready", "gate_kept", "tapped", "silu_ready", "hid_made") as \
            (w0, w1, edges, product_ready, gate_kept, tapped, silu_ready, hid_made):
        def sb(name, shape):
            return held.enter_context(nc.sbuf_tensor(name, shape, F32, allow_name_mangling=True))

        ws = sb("w_up", [P, 2, 2, KD, P])
        g = sb("g_raw", [P, edge + S])
        cv = sb("g_conv", [P, S])
        ps = core.ps
        landed = [w0, w1]
        w_k = w.rearrange("(k p) (a n) -> p k a n", p=P, a=2)
        with nc.Block() as block:
            def loops(eng, body, start=0):
                with eng.Fori(start, KF // 2) as i:
                    for b in range(2):
                        body(2 * i + b, i, b)

            @block.sync
            def _(sp):
                def load(j, b):
                    for a in range(2):
                        sp.dma_start(ws[:, b, a, :, :], w_k[:, :, a, bass.ds(j * P, P)]).then_inc(landed[b], 16)

                def body(j, i, b):
                    sp.wait_ge(product_ready, 2 * (j - 1))
                    load(j, b)
                load(0, 0)
                load(1, 1)
                loops(sp, body, 1)

            @block.tensor
            def _(pe):
                def tile(j, i, b, first=False):
                    pe.wait_ge(landed[b], 32 * (i + 1))
                    for a in range(2):
                        if not first:
                            pe.wait_ge(*((gate_kept, j - 1) if a == 0 else (hid_made, j - 1)))
                        for half in range(NH):
                            for k in range(KD):
                                last = nc.tensor.matmul(ps[:, 4 * b + 2 * a + half, :], ws[:, b, a, k, :],
                                                        core.h[:, k, half * HALF:(half + 1) * HALF],
                                                        start=(k == 0), stop=(k == KD - 1))
                        last.then_inc(product_ready, 1)
                tile(0, 0, 0, True)
                tile(1, 0, 1, True)
                loops(pe, tile, 1)

            @block.scalar
            def _(act):
                def tile(j, i, b, first=False):
                    act.wait_ge(product_ready, 2 * j + 1)
                    if not first:
                        act.wait_ge(tapped, CONV_FF * j)
                    nc.scalar.activation(g[:, edge:], flat(ps[:, 4 * b:4 * b + 2, :]), ACT.Copy).then_inc(gate_kept, 1)
                    act.wait_ge(tapped, CONV_FF * j + CONV_FF)
                    nc.scalar.activation(cv[:], cv[:], ACT.Silu, bias=core.two[:, bass.ds(TWO["ffn_conv_b"] + j, 1)]).then_inc(silu_ready, 1)
                tile(0, 0, 0, True)
                tile(1, 0, 1)
                loops(act, tile, 1)

            @block.vector
            def _(dve):
                nc.vector.memset(g[:, 0:edge], 0.0).then_inc(edges, 1)
                dve.wait_ge(edges, 1)

                def tile(j, i, b):
                    def tap(t):
                        return core.two[:, bass.ds(TWO["ffn_conv_w"] + t * KF + j, 1)]
                    dve.wait_ge(gate_kept, j + 1)
                    nc.vector.tensor_scalar(cv[:], g[:, edge:], tap(edge), None, ALU.mult).then_inc(tapped, 1)
                    for t in range(edge):
                        dve.wait_ge(tapped, CONV_FF * j + (t + 1))
                        nc.vector.scalar_tensor_tensor(cv[:], g[:, t:t + S], tap(t), cv[:], ALU.mult, ALU.add).then_inc(tapped, 1)
                    dve.wait_ge(silu_ready, j + 1)
                    dve.wait_ge(product_ready, 2 * j + 2)
                    nc.vector.tensor_tensor(hid[:, bass.ds(j, 1), :].rearrange("p a s -> p (a s)"), cv[:],
                                            flat(ps[:, 4 * b + 2:4 * b + 4, :]), ALU.mult).then_inc(hid_made, 1)
                    dve.wait_ge(hid_made, j + 1)
                loops(dve, tile)


def ffn_down(core, w, hid, gate_at):
    nc = core.nc
    slots = 3
    with ExitStack() as held, stage(nc, "w0", "w1", "w2", "grouped", "added") as (w0, w1, w2, grouped, added):
        ws = held.enter_context(nc.sbuf_tensor("w_down", [P, slots, KF, P], F32, allow_name_mangling=True))
        landed = [w0, w1, w2]
        with nc.Block() as block:
            @block.sync
            def _(sp):
                for j in range(KD):
                    if j >= slots:
                        sp.wait_ge(grouped, j - slots + 1)
                    sp.dma_start(ws[:, j % slots, :, :],
                                 w.rearrange("(k p) n -> p k n", p=P)[:, :, j * P:(j + 1) * P]).then_inc(landed[j % slots], 16)

            @block.tensor
            def _(pe):
                for j in range(KD):
                    pe.wait_ge(landed[j % slots], 16 * (j // slots + 1))
                    if j >= 4:
                        pe.wait_ge(added, j - 3)
                    for i in range(NH):
                        for k in range(KF):
                            last = nc.tensor.matmul(core.ps[:, 2 * (j % 4) + i, :], ws[:, j % slots, k, :],
                                                    hid[:, k, i * HALF:(i + 1) * HALF], start=(k == 0), stop=(k == KF - 1))
                    last.then_inc(grouped, 1)

            @block.vector
            def _(dve):
                for j in range(KD):
                    dve.wait_ge(grouped, j + 1)
                    b = 2 * (j % 4)
                    nc.vector.scalar_tensor_tensor(core.x[:, j, :], flat(core.ps[:, b:b + 2, :]),
                                                   core.mod[:, gate_at + j:gate_at + j + 1], core.x[:, j, :],
                                                   ALU.mult, ALU.add).then_inc(added, 1)


def program(nc, a, out):
    h_rows = nc.dram_tensor("h_rows", (S, D), F32, kind="Internal").ap()
    slot_rows = nc.dram_tensor("slot_rows", (N_EXP, S), F32, kind="Internal").ap()
    aff_rows = nc.dram_tensor("aff_rows", (N_EXP, S), F32, kind="Internal").ap()
    with ExitStack() as ctx:
        core = Core(nc, ctx)
        with ExitStack() as tables:
            cos = tables.enter_context(nc.sbuf_tensor("cos", [ROPE, S], F32))
            sin = tables.enter_context(nc.sbuf_tensor("sin", [ROPE, S], F32))
            load_inputs(core, cos, sin, a["xT"], a["cT"], a["pos"], a["con"], a["par_two"])
            with nc.Fori(0, DEPTH) as l:
                block_one(core, cos, sin, a, l, h_rows, slot_rows, aff_rows)
        block_two(core, a)
        store_output(core, core.h, out)


def block_one(core, cos, sin, a, l, h_rows, slot_rows, aff_rows):
    nc = core.nc
    modulation(core, 0, a["w_ada"][l], lambda: core.p1("b_ada", 0, P, N_MOD * KD), a["par_one"][l])
    normalise(core, core.p1("norm1_g", 0, P, KD), 0, KD)
    with ExitStack() as held:
        cq = held.enter_context(nc.sbuf_tensor("cq", [P, 2, S], F32))
        ckv = held.enter_context(nc.sbuf_tensor("ckv", [P, S], F32))
        kr = held.enter_context(nc.sbuf_tensor("kr", [ROPE, S], F32))
        y = held.enter_context(nc.sbuf_tensor("y", [P, KC, S + 2 * PAD], F32))
        project_one(core, a["w_in"][l], cq, ckv, kr, y)
        latent_norm(core, cq, ckv)
        attention(core, cos, sin, a["w_uq"][l], a["w_ukv"][l], cq, ckv, kr, y)
    conv = [core.h[:, HEADS + j, :] for j in range(KC)]
    layer_norm(core, conv, CONV_CH, core.c("eps"), core.c("ones", P), lambda k: core.p1("conv_norm_g", k),
               lambda k: core.p1("conv_norm_b", k), ACT.Silu)
    out_projection(core, a["w_out"][l], 2 * KD)
    normalise(core, core.p1("norm2_g", 0, P, KD), 3 * KD, 4 * KD)
    route(core, a["w_router"][l], h_rows, slot_rows, aff_rows)
    experts(core, a["w_gate"][l], a["w_up"][l], a["w_down"][l], h_rows, slot_rows, aff_rows, 5 * KD)


def block_two(core, a):
    nc = core.nc
    modulation(core, 1, a["w_mod_2"], lambda: core.p2("b_mod", 0, N_MOD * KD))
    normalise(core, core.p2("norm_mix", 0, KD), 0, KD)
    with ExitStack() as held:
        p = held.enter_context(nc.sbuf_tensor("p_two", [P, N_P, S], F32))
        pc = held.enter_context(nc.sbuf_tensor("chunk_decay", [P, KCC, NCH], F32))
        project_two(core, a["w_in_2"], p)
        v = [p[:, T_V + k, :] for k in range(KA)]
        layer_norm(core, v, D_A, core.c("ln_eps"), core.c("ones", P), lambda k: core.p2("sgu_ln_g", k),
                   lambda k: core.p2("sgu_ln_b", k), ACT.Identity)
        spatial_gate(core, p, a["sgu_w_2"], a["sgu_b_2"].rearrange("h t -> (h t)").unsqueeze(0))
        linear_recurrence(core, p, a["lru_w_a_2"], a["lru_w_x_2"])
        with nc.sbuf_tensor("ex_two", [P, 2 * KCC, S], F32) as ex:
            delta_inputs(core, p, ex, pc, a["rwkv_w2_2"], a["rwkv_a2_2"], a["rwkv_g2_2"])
            delta_chunks(core, p, ex, pc)
            o = [p[:, T_R + q, :] for q in range(KCC)]
            layer_norm(core, o, HD, core.c("gn_eps"), core.c("pair", P), lambda k: core.p2("ln_w", k),
                       lambda k: core.p2("ln_b", k), ACT.Identity)
            delta_output(core, p, ex)
    out_projection(core, a["w_out_2"], 2 * KD)
    normalise(core, core.p2("norm_ffn", 0, KD), 3 * KD, 4 * KD)
    with nc.sbuf_tensor("ffn_hidden", [P, KF, S], F32) as hid:
        ffn_up(core, a["ffn_w_up_2"], hid)
        ffn_down(core, a["ffn_w_down_2"], hid, 5 * KD)
    normalise(core, core.p2("norm_final", 0, KD), None, None)


ONE_WEIGHTS = ["w_ada", "w_in", "w_uq", "w_ukv", "w_out", "w_router", "w_gate", "w_up", "w_down"]
TWO_WEIGHTS = ["w_mod_2", "w_in_2", "w_out_2", "sgu_w_2", "sgu_b_2", "lru_w_a_2", "lru_w_x_2", "rwkv_w2_2",
               "rwkv_a2_2", "rwkv_g2_2", "ffn_w_up_2", "ffn_w_down_2"]


def lay_out(v):
    def cols(x):
        x = np.asarray(x)
        return np.swapaxes(x.reshape(x.shape[:-1] + (-1, P)), -1, -2)

    def padded(x):
        z = np.zeros((x.shape[0], P, 1), np.float32)
        z[:, :x.shape[1], 0] = x
        return z

    a = {"xT": np.asarray(v["x"])[0].T, "con": constants(), "pos": np.asarray(v["positions"])[0]}
    a["cT"] = np.stack([cols(v["c"][0]), cols(v["c_2"][0])], axis=1)
    one = {"qg_nope": padded(v["q_head_g"][:, :NOPE]), "qg_rope": padded(v["q_head_g"][:, NOPE:]),
           "kg_nope": padded(v["k_head_g"][:, :NOPE]), "kg_rope": padded(v["k_head_g"][:, NOPE:])}
    tap = cols(v["conv_w"])
    one["conv_w"] = np.swapaxes(tap, 1, 2).reshape(DEPTH, P, TAPS * KC)
    for name in ONE:
        if name not in one:
            one[name] = cols(v[name])
    a["par_one"] = np.concatenate([one[n] for n in ONE], axis=2)
    two = {}
    tap = cols(v["lru_conv_w_2"][0])
    two["lru_conv_w"] = np.swapaxes(tap, 0, 1).reshape(P, -1)
    tap = cols(v["ffn_conv_w_2"][0])
    two["ffn_conv_w"] = np.swapaxes(tap, 0, 1).reshape(P, -1)
    other = {"r_k": v["rwkv_r_k_2"].reshape(1, D_C), "norm_final": v["norm_final_2"].reshape(1, D)}
    for name in TWO:
        if name not in two:
            src = other.get(name)
            if src is None:
                src = v[name + "_2"] if name + "_2" in v else v["rwkv_" + name + "_2"]
            two[name] = cols(src[0])
    a["par_two"] = np.concatenate([two[n] for n in TWO], axis=1)
    for n in ONE_WEIGHTS + TWO_WEIGHTS:
        a[n] = np.asarray(v[n])
        if n in TWO_WEIGHTS:
            a[n] = a[n][0]
    return {n: np.ascontiguousarray(x) for n, x in a.items()}


def kernel(**inputs):
    import concourse.bacc as _bacc
    from concourse.bass_utils import run_bass_kernel_spmd as _run

    v = {n: np.asarray(x) for n, x in inputs.items()}
    arrays = lay_out(v)
    nc = _bacc.Bacc("TRN2", target_bir_lowering=False, num_devices=1)
    args = {n: nc.dram_tensor("in_" + n, x.shape, mybir.dt.from_np(x.dtype), kind="ExternalInput").ap()
            for n, x in arrays.items()}
    out = nc.dram_tensor("out_0", (D, S), F32, kind="ExternalOutput").ap()
    program(nc, args, out)
    r = _run(nc, [{"in_" + n: x for n, x in arrays.items()}], core_ids=[0])
    return np.ascontiguousarray(r.results[0]["out_0"].T)[None]
```

```python
import math
from contextlib import ExitStack, contextmanager

import numpy as np

import concourse.bass as bass
from concourse import mybir

F32 = mybir.dt.float32
BF16 = mybir.dt.bfloat16
I32 = mybir.dt.int32
U32 = mybir.dt.uint32
ALU = mybir.AluOpType
ACT = mybir.ActivationFunctionType
AX_X = mybir.AxisListType.X

P = 128
S = 1024
D = 1024
KD = D // P
HALF = 512
NH = S // HALF
DEPTH = 2
N_MOD = 6
EPS = 1e-6

HEADS, NOPE, ROPE, VD = 4, 128, 64, 128
QKD = NOPE + ROPE
Q_RANK, KV_RANK = 256, 128
CONV_CH, TAPS = 512, 31
PAD = TAPS // 2
KC = CONV_CH // P
IN1 = Q_RANK + KV_RANK + ROPE + 2 * CONV_CH
QT = S // P
N_EXP, FF = 16, 1024
CAP = 2 * S // N_EXP
TOP8 = CAP // 8
ROPE_THETA = 10000.0

HD = 64
D_A, D_B, D_C = D // 4, 3 * D // 8, 3 * D // 8
KA, KB, KCC = D_A // P, D_B // P, D_C // P
LRU_C, LN_EPS, GN_EPS = 8.0, 1e-5, 64e-5
CONV_B, CONV_FF = 4, 3
D_FF = 2816
KF = D_FF // P
P_C = 3 * D_C + 256
IN2 = 2 * D_A + 2 * D_B + P_C
KP = P_C // P
CH = 64
NCH = S // CH


def columns(fields):
    at, n = {}, 0
    for name, k in fields:
        at[name] = n
        n += k
    return at, n


ONE, N_ONE = columns([("b_ada", N_MOD * KD), ("norm1_g", KD), ("norm2_g", KD), ("q_latent_g", 2),
                      ("kv_latent_g", 1), ("qg_nope", 1), ("qg_rope", 1), ("kg_nope", 1), ("kg_rope", 1),
                      ("conv_w", TAPS * KC), ("conv_b", KC), ("conv_norm_g", KC), ("conv_norm_b", KC)])
TWO, N_TWO = columns([("b_mod", N_MOD * KD), ("norm_mix", KD), ("norm_ffn", KD), ("norm_final", KD),
                      ("sgu_ln_g", KA), ("sgu_ln_b", KA), ("lru_conv_w", CONV_B * KB), ("lru_conv_b", KB),
                      ("lru_b_a", KB), ("lru_b_x", KB), ("lru_lambda", KB), ("mu", KP), ("w0", KCC),
                      ("a0", KCC), ("k_k", KCC), ("k_a", KCC), ("r_k", KCC), ("ln_w", KCC), ("ln_b", KCC),
                      ("ffn_conv_w", CONV_FF * KF), ("ffn_conv_b", KF)])
CON, N_CON = columns([("ident", P), ("ones", P), ("pair", P), ("swap", ROPE), ("slot", 1), ("inv_freq", 1),
                      ("eps", 1), ("ln_eps", 1), ("gn_eps", 1), ("token", S), ("strict", P), ("strictT", P),
                      ("upper", CH), ("causal", P), ("level0", P), ("levelsT", 6 * P)])


def constants():
    c = np.zeros((P, N_CON), np.float32)
    i, j = np.arange(P)[:, None], np.arange(P)[None, :]
    same = (i // CH) == (j // CH)

    def put(name, value):
        value = np.asarray(value, np.float32)
        c[:value.shape[0], CON[name]:CON[name] + value.shape[1]] = value

    put("ident", i == j)
    put("ones", np.ones((P, P)))
    put("pair", same)
    half = ROPE // 2
    swap = np.zeros((ROPE, ROPE))
    swap[np.arange(half) + half, np.arange(half)] = -1.0
    swap[np.arange(half), np.arange(half) + half] = 1.0
    put("swap", swap)
    put("slot", i)
    freq = (1.0 / (np.float32(ROPE_THETA) ** (np.arange(0, ROPE, 2, dtype=np.float32) / np.float32(ROPE)))).astype(np.float32)
    put("inv_freq", np.concatenate([freq, freq])[:, None])
    put("eps", np.full((P, 1), EPS))
    put("ln_eps", np.full((P, 1), LN_EPS))
    put("gn_eps", np.full((P, 1), GN_EPS))
    put("token", np.tile(np.arange(S)[None, :], (P, 1)))
    put("strict", same & (i % CH < j % CH))
    put("strictT", same & (j % CH < i % CH))
    put("upper", (i % CH) <= j[:, :CH])
    put("causal", i <= j)
    for level in range(6):
        n = 1 << level
        a, b = i % CH, j % CH
        join = same & (a // (2 * n) == b // (2 * n)) & (a % (2 * n) < n) & (b % (2 * n) >= n)
        if level == 0:
            put("level0", join)
        c[:, CON["levelsT"] + level * P:CON["levelsT"] + (level + 1) * P] = join.T
    return c


def flat(x):
    return x.rearrange("p a n -> p (a n)")


@contextmanager
def stage(nc, *names):
    with ExitStack() as held:
        sems = [held.enter_context(nc.semaphore(n)) for n in names]
        yield sems
        nc.clear_and_free_semaphores(sems)
        nc.all_engine_barrier()


class Core:

    def __init__(self, nc, ctx):
        def sb(name, shape, dt=F32):
            return ctx.enter_context(nc.sbuf_tensor(name, shape, dt, allow_name_mangling=True))

        self.nc = nc
        self.x = sb("x_res", [P, KD, S])
        self.h = sb("h_act", [P, KD, S])
        self.con = sb("con", [P, N_CON])
        self.one = sb("par_one", [P, N_ONE])
        self.two = sb("par_two", [P, N_TWO])
        self.cact = sb("cact", [P, 2, KD])
        self.mod = sb("mod", [P, N_MOD * KD])
        self.gain = sb("gain", [P, KD])
        self.rstd = sb("rstd", [P, S])
        self.ps = ctx.enter_context(nc.psum_tensor("ps", [P, 8, HALF], F32))

    def c(self, name, n=1, rows=P):
        return self.con[0:rows, CON[name]:CON[name] + n]

    def p1(self, name, j=0, rows=P, n=1):
        return self.one[0:rows, ONE[name] + j:ONE[name] + j + n]

    def p2(self, name, j=0, n=1):
        return self.two[:, TWO[name] + j:TWO[name] + j + n]


def load_inputs(core, cos, sin, xT, cT, pos, con, par_two):
    nc = core.nc
    with ExitStack() as held, stage(nc, "loaded", "c_loaded", "pos_loaded", "c_ready", "angle", "turned", "tabled") as \
            (loaded, c_loaded, pos_loaded, c_ready, angle, turned, tabled):
        craw = held.enter_context(nc.sbuf_tensor("craw", [P, 2, KD], F32, allow_name_mangling=True))
        posi = held.enter_context(nc.sbuf_tensor("posi", [ROPE, S], I32, allow_name_mangling=True))
        ang = held.enter_context(nc.sbuf_tensor("ang", [ROPE, S], F32, allow_name_mangling=True))
        cyc = held.enter_context(nc.sbuf_tensor("cyc", [ROPE, S], F32, allow_name_mangling=True))
        red = held.enter_context(nc.sbuf_tensor("red", [ROPE, 2, S], F32, allow_name_mangling=True))
        full = 2.0 * math.pi
        two_a = 6.28125
        two_b = float(np.float32(np.round((full - two_a) * 2.0 ** 20) / 2.0 ** 20))
        two_c = float(np.float32(full - two_a - two_b))
        magic = 1.5 * 2.0 ** 23
        pi_below = 3.1415925
        with nc.Block() as block:
            @block.sync
            def _(sp):
                sp.dma_start(posi[:], pos.partition_broadcast(ROPE)).then_inc(pos_loaded, 16)
                sp.dma_start(craw[:], cT).then_inc(c_loaded, 16)
                sp.dma_start(core.con[:], con).then_inc(pos_loaded, 16)
                sp.dma_start(core.two[:], par_two).then_inc(loaded, 16)
                sp.dma_start(core.x[:], xT.rearrange("(k p) s -> p k s", p=P)).then_inc(loaded, 16)
                sp.wait_ge(loaded, 32)

            @block.scalar
            def _(act):
                act.wait_ge(c_loaded, 16)
                nc.scalar.activation(core.cact[:], craw[:], ACT.Silu).then_inc(c_ready, 1)
                act.wait_ge(turned, 2)
                nc.scalar.activation(sin[:], red[:, 0, :], ACT.Sin).then_inc(tabled, 1)
                nc.scalar.activation(cos[:], red[:, 1, :], ACT.Sin).then_inc(tabled, 1)

            @block.vector
            def _(dve):
                n = [0]

                def after(ins):
                    ins.then_inc(angle, 1)
                    n[0] += 1
                    dve.wait_ge(angle, n[0])

                dve.wait_ge(pos_loaded, 32)
                after(nc.vector.tensor_copy(ang[:], posi[:]))
                after(nc.vector.tensor_scalar(ang[:], ang[:], core.c("inv_freq", rows=ROPE), None, ALU.mult))
                for j, shift in enumerate((0.0, 0.25)):
                    after(nc.vector.tensor_scalar(cyc[:], ang[:], 1.0 / full, shift, ALU.mult, ALU.add))
                    after(nc.vector.tensor_scalar(cyc[:], cyc[:], magic, None, ALU.add))
                    after(nc.vector.tensor_scalar(cyc[:], cyc[:], magic, None, ALU.subtract))
                    after(nc.vector.scalar_tensor_tensor(red[:, j, :], cyc[:], -two_a, ang[:], ALU.mult, ALU.add))
                    after(nc.vector.scalar_tensor_tensor(red[:, j, :], cyc[:], -two_b, red[:, j, :], ALU.mult, ALU.add))
                    after(nc.vector.scalar_tensor_tensor(red[:, j, :], cyc[:], -two_c, red[:, j, :], ALU.mult, ALU.add))
                    if j:
                        after(nc.vector.tensor_scalar(red[:, j, :], red[:, j, :], math.pi / 2, None, ALU.add))
                    nc.vector.tensor_scalar(red[:, j, :], red[:, j, :], pi_below, -pi_below, ALU.min, ALU.max).then_inc(turned, 1)


def modulation(core, which, w, bias, par=None):
    nc = core.nc
    slots = 3
    nm = N_MOD * KD
    pieces = 4
    width = N_MOD * D // pieces
    with ExitStack() as held, stage(nc, "w0", "w1", "w2", "par_loaded", "rows_added", "summed", "mod_ready", "squared",
                                    "sq_used", "rooted", "inverted") as \
            (w0, w1, w2, par_loaded, rows_added, summed, mod_ready, squared, sq_used, rooted, inverted):
        wm = held.enter_context(nc.sbuf_tensor("wmod", [P, slots, N_MOD * D], F32, allow_name_mangling=True))
        acc = held.enter_context(nc.sbuf_tensor("wmod_sum", [P, N_MOD * D], F32, allow_name_mangling=True))
        cols = core.ps[:, 0, 0:nm]
        sq = held.enter_context(nc.sbuf_tensor("sq_mod", [P, 2, S], F32, allow_name_mangling=True))
        landed = [w0, w1, w2]
        with nc.Block() as block:
            @block.scalar
            def _(act):
                for k in range(KD):
                    if k >= 2:
                        act.wait_ge(sq_used, k - 1)
                    nc.scalar.activation(sq[:, k % 2, :], core.x[:, k, :], ACT.Square).then_inc(squared, 1)
                act.wait_ge(sq_used, KD)
                nc.scalar.activation(core.rstd[:], flat(core.ps[:, 2:4, :]), ACT.Sqrt, bias=core.c("eps"),
                                     scale=1.0 / D).then_inc(rooted, 1)

            @block.sync
            def _(sp):
                if par is not None:
                    sp.dma_start(core.one[:], par).then_inc(par_loaded, 16)
                for k in range(KD):
                    if k >= slots:
                        sp.wait_ge(rows_added, k - slots + 1)
                    sp.dma_start(wm[:, k % slots, :], w[k * P:(k + 1) * P, :]).then_inc(landed[k % slots], 16)

            @block.vector
            def _(dve):
                dve.wait_ge(landed[0], 16)
                nc.vector.tensor_scalar(acc[:], wm[:, 0, :], core.cact[:, which, 0:1], None, ALU.mult).then_inc(rows_added, 1)
                for k in range(1, KD):
                    dve.wait_ge(landed[k % slots], 16 * (k // slots + 1))
                    dve.wait_ge(rows_added, k)
                    if k == KD // 2:
                        dve.wait_ge(rooted, 1)
                        nc.vector.reciprocal(core.rstd[:], core.rstd[:]).then_inc(inverted, 1)
                    for i in range(pieces if k == KD - 1 else 1):
                        part = slice(i * width, (i + 1) * width) if k == KD - 1 else slice(0, N_MOD * D)
                        nc.vector.scalar_tensor_tensor(acc[:, part], wm[:, k % slots, part], core.cact[:, which, k:k + 1],
                                                       acc[:, part], ALU.mult, ALU.add).then_inc(rows_added, 1)
                if par is not None:
                    dve.wait_ge(par_loaded, 16)
                dve.wait_ge(summed, 1)
                nc.vector.tensor_tensor(core.mod[:], cols, bias(), ALU.add).then_inc(mod_ready, 1)

            @block.tensor
            def _(pe):
                for k in range(KD):
                    pe.wait_ge(squared, k + 1)
                    for i in range(NH):
                        last = nc.tensor.matmul(core.ps[:, 2 + i, :], core.c("ones", P), sq[:, k % 2, i * HALF:(i + 1) * HALF],
                                                start=(k == 0), stop=(k == KD - 1))
                    last.then_inc(sq_used, 1)
                for j in range(nm):
                    if j % (nm // pieces) == 0:
                        pe.wait_ge(rows_added, KD + j // (nm // pieces))
                    last = nc.tensor.matmul(cols[:, j:j + 1], acc[:, j * P:(j + 1) * P], core.c("ones"), start=True, stop=True)
                last.then_inc(summed, 1)


def scale_tiles(core, dve, gains, gained, scaled):
    nc = core.nc
    nc.vector.scalar_tensor_tensor(core.gain[:], core.mod[:, KD:2 * KD], 1.0, gains, ALU.add, ALU.mult).then_inc(gained, 1)
    dve.wait_ge(gained, 1)
    for k in range(KD):
        nc.vector.scalar_tensor_tensor(core.h[:, k, :], core.x[:, k, :], core.gain[:, k:k + 1], core.rstd[:],
                                       ALU.mult, ALU.mult).then_inc(scaled, 1)


def shift_tiles(core, act, scaled, shifted):
    nc = core.nc
    for k in range(KD):
        act.wait_ge(scaled, k + 1)
        nc.scalar.activation(core.h[:, k, :], core.h[:, k, :], ACT.Identity, bias=core.mod[:, k:k + 1]).then_inc(shifted, 1)


def square_tiles(core, act, sq, added, squared, totalled):
    nc = core.nc
    for j in range(KD):
        act.wait_ge(added, j + 1)
        if j >= 3:
            act.wait_ge(totalled, j - 2)
        dest = sq[:, j % 2, :] if j else core.rstd[:]
        nc.scalar.activation(dest, core.x[:, j, :], ACT.Square).then_inc(squared, 1)


def add_and_total(core, dve, gate_at, sq, grouped, added, squared, totalled):
    nc = core.nc
    for j in range(KD + 1):
        if j < KD:
            dve.wait_ge(grouped, j + 1)
            b = 2 * (j % 4)
            nc.vector.scalar_tensor_tensor(core.x[:, j, :], flat(core.ps[:, b:b + 2, :]),
                                           core.mod[:, gate_at + j:gate_at + j + 1], core.x[:, j, :],
                                           ALU.mult, ALU.add).then_inc(added, 1)
        t = j - 1
        if t >= 1:
            dve.wait_ge(squared, t + 1)
            if t >= 2:
                dve.wait_ge(totalled, t - 1)
            nc.vector.tensor_tensor(core.rstd[:], core.rstd[:], sq[:, t % 2, :], ALU.add).then_inc(totalled, 1)


def normalise(core, gains, shift_at, scale_at, dest=None):
    nc = core.nc
    with ExitStack() as held, stage(nc, "summed", "rooted", "gained", "inverted", "scaled", "shifted") as \
            (summed, rooted, gained, inverted, scaled, shifted):
        std = held.enter_context(nc.sbuf_tensor("std", [P, S], F32, allow_name_mangling=True))
        rstd = core.rstd
        out = core.h if dest is None else dest
        total = core.ps[:, 0:NH, :]
        with nc.Block() as block:
            @block.scalar
            def _(act):
                act.wait_ge(summed, 1)
                nc.scalar.activation(std[:], total, ACT.Sqrt, bias=core.c("eps"), scale=1.0 / D).then_inc(rooted, 1)
                if scale_at is not None:
                    for k in range(KD):
                        act.wait_ge(scaled, k + 1)
                        nc.scalar.activation(out[:, k, :], out[:, k, :], ACT.Identity,
                                             bias=core.mod[:, shift_at + k:shift_at + k + 1]).then_inc(shifted, 1)

            @block.tensor
            def _(pe):
                for i in range(NH):
                    last = nc.tensor.matmul(core.ps[:, i, :], core.c("ones", P), rstd[:, i * HALF:(i + 1) * HALF],
                                            start=True, stop=True)
                last.then_inc(summed, 1)

            @block.vector
            def _(dve):
                if scale_at is None:
                    nc.vector.tensor_copy(core.gain[:], gains).then_inc(gained, 1)
                else:
                    nc.vector.scalar_tensor_tensor(core.gain[:], core.mod[:, scale_at:scale_at + KD], 1.0, gains,
                                                   ALU.add, ALU.mult).then_inc(gained, 1)
                dve.wait_ge(rooted, 1)
                nc.vector.reciprocal(rstd[:], std[:]).then_inc(inverted, 1)
                dve.wait_ge(inverted, 1)
                dve.wait_ge(gained, 1)
                for k in range(KD):
                    nc.vector.scalar_tensor_tensor(out[:, k, :], core.x[:, k, :], core.gain[:, k:k + 1], rstd[:],
                                                   ALU.mult, ALU.mult).then_inc(scaled, 1)


def project_one(core, w, gains, cq, ckv, kr, y):
    nc = core.nc
    dests = [cq[:, 0, :], cq[:, 1, :], ckv[:, :], kr[:, :]]
    columns_of = [(0, P), (P, P), (Q_RANK, P), (Q_RANK + KV_RANK, ROPE)]
    first = Q_RANK + KV_RANK + ROPE
    latents = [((0, 1), Q_RANK, "q_latent_g"), ((2,), KV_RANK, "kv_latent_g")]
    turns = [("plain", g) for g in range(len(dests))] + [("value", 0), ("gate", 0), ("sum", 0), ("sum", 1)]
    for j in range(1, KC):
        turns += [("value", j), ("gate", j)]
    pairs = 4
    with ExitStack() as held, stage(nc, "w_lat", "w_conv", "produced", "copied", "squared", "sigmoided", "gated", "rooted",
                                    "inverted", "scaled", "cleared", "gained", "h_scaled", "h_shifted") as \
            (w_lat, w_conv, produced, copied, squared, sigmoided, gated, rooted, inverted, scaled, cleared,
             gained, h_scaled, h_shifted):
        ws = held.enter_context(nc.sbuf_tensor("w_in", [P, KD, IN1], F32, allow_name_mangling=True))
        sig = held.enter_context(nc.sbuf_tensor("sig", [P, 2, S], F32, allow_name_mangling=True))
        sq = held.enter_context(nc.sbuf_tensor("sq", [P, 3, S], F32, allow_name_mangling=True))
        rstd = held.enter_context(nc.sbuf_tensor("rstd", [P, 2, S], F32, allow_name_mangling=True))
        w_k = w.rearrange("(k p) n -> p k n", p=P)

        def banks(what, j):
            b = 2 * (turns.index((what, j)) % pairs)
            return core.ps[:, b:b + 2, :]

        def done(what, j):
            return turns.index((what, j)) + 1

        with nc.Block() as block:
            @block.sync
            def _(sp):
                sp.dma_start(ws[:, :, 0:first], w_k[:, :, 0:first]).then_inc(w_lat, 16)
                sp.dma_start(ws[:, :, first:IN1], w_k[:, :, first:IN1]).then_inc(w_conv, 16)

            @block.tensor
            def _(pe):
                pe.wait_ge(w_lat, 16)
                for t, (what, j) in enumerate(turns):
                    if t == len(dests):
                        pe.wait_ge(w_conv, 16)
                    if t >= pairs:
                        had, i = turns[t - pairs]
                        if had == "plain":
                            pe.wait_ge(copied, i + 1)
                            if i < 3:
                                pe.wait_ge(squared, i + 1)
                        elif had == "value":
                            pe.wait_ge(gated, i + 1)
                        elif had == "gate":
                            pe.wait_ge(sigmoided, i + 1)
                        else:
                            pe.wait_ge(rooted, i + 1)
                    out = banks(what, j)
                    if what == "sum":
                        tiles = latents[j][0]
                        pe.wait_ge(squared, tiles[-1] + 1)
                        for i in range(NH):
                            for k in tiles:
                                last = nc.tensor.matmul(out[:, i, :], core.c("ones", P), sq[:, k, i * HALF:(i + 1) * HALF],
                                                        start=(k == tiles[0]), stop=(k == tiles[-1]))
                    else:
                        if what == "plain":
                            col, width = columns_of[j]
                        else:
                            col, width = first + (CONV_CH if what == "gate" else 0) + j * P, P
                        for i in range(NH):
                            for k in range(KD):
                                if t == 0 and i == 0:
                                    pe.wait_ge(h_shifted, k + 1)
                                last = nc.tensor.matmul(out[0:width, i, :], ws[:, k, col:col + width],
                                                        core.h[:, k, i * HALF:(i + 1) * HALF],
                                                        start=(k == 0), stop=(k == KD - 1))
                    last.then_inc(produced, 1)

            @block.scalar
            def _(act):
                shift_tiles(core, act, h_scaled, h_shifted)
                for g, dest in enumerate(dests):
                    act.wait_ge(produced, done("plain", g))
                    src = banks("plain", g)[0:columns_of[g][1]]
                    nc.scalar.activation(dest, src, ACT.Copy).then_inc(copied, 1)
                    if g < 3:
                        nc.scalar.activation(sq[:, g, :], src, ACT.Square).then_inc(squared, 1)
                for j in range(KC):
                    act.wait_ge(produced, done("gate", j))
                    if j >= 2:
                        act.wait_ge(gated, j - 1)
                    nc.scalar.activation(sig[:, j % 2, :], banks("gate", j), ACT.Sigmoid).then_inc(sigmoided, 1)
                    if j == 0:
                        for m, (_, width, _) in enumerate(latents):
                            act.wait_ge(produced, done("sum", m))
                            nc.scalar.activation(rstd[:, m, :], banks("sum", m), ACT.Sqrt, bias=core.c("eps"),
                                                 scale=1.0 / width).then_inc(rooted, 1)

            @block.vector
            def _(dve):
                scale_tiles(core, dve, gains, gained, h_scaled)
                nc.vector.memset(y[:, :, 0:PAD], 0.0)
                nc.vector.memset(y[:, :, PAD + S:], 0.0).then_inc(cleared, 1)
                for j in range(KC):
                    dve.wait_ge(sigmoided, j + 1)
                    nc.vector.tensor_tensor(y[:, j, PAD:PAD + S], banks("value", j), sig[:, j % 2, :],
                                            ALU.mult).then_inc(gated, 1)
                    if j == 0:
                        for m, (tiles, _, g) in enumerate(latents):
                            dve.wait_ge(rooted, m + 1)
                            nc.vector.reciprocal(rstd[:, m, :], rstd[:, m, :]).then_inc(inverted, 1)
                            dve.wait_ge(inverted, m + 1)
                            dve.wait_ge(copied, tiles[-1] + 1)
                            for k in tiles:
                                nc.vector.scalar_tensor_tensor(dests[k], dests[k], core.p1(g, k - tiles[0]), rstd[:, m, :],
                                                               ALU.mult, ALU.mult).then_inc(scaled, 1)


def attention(core, cos, sin, w_uq, w_ukv, cq, ckv, kr, y):
    nc = core.nc
    scale = 1.0 / math.sqrt(QKD)
    units = HEADS * QT
    taps = [(t, j) for t in range(TAPS) for j in range(KC)]
    per_unit = -(-len(taps) // units)
    with ExitStack() as held, stage(
            nc, "w_loaded", "v_made", "v_kept", "raw", "squared", "summed", "rooted", "inverted", "head_scaled",
            "turned", "part_made", "head_ready", "scores_ready", "peak_found", "shift_ready", "probs_ready",
            "total_inverted", "probs_scaled", "probs_turned", "turned_kept", "out_ready", "out_kept", "tapped") as \
            (w_loaded, v_made, v_kept, raw, squared, summed, rooted, inverted, head_scaled,
             turned, part_made, head_ready, scores_ready, peak_found, shift_ready, probs_ready,
             total_inverted, probs_scaled, probs_turned, turned_kept, out_ready, out_kept, tapped):
        def sb(name, shape):
            return held.enter_context(nc.sbuf_tensor(name, shape, F32, allow_name_mangling=True))

        wq = sb("wq", [P, 2, HEADS * QKD])
        wkv = sb("wkv", [P, HEADS * (NOPE + VD)])
        v = sb("v", [P, QT, HEADS * VD])
        nope = sb("nope", [P, 2, S])
        rope = sb("rope", [ROPE, 2, S])
        sqn = sb("sqn", [P, S])
        sqr = sb("sqr", [ROPE, S])
        std = sb("std", [P, S])
        rstd = core.rstd
        rope0 = sb("rope0", [ROPE, S])
        part = sb("part", [ROPE, 2, S])
        probs = sb("probs", [P, 2, S])
        probsT = sb("probsT", [P, 2, QT, P])
        peak = sb("peak", [P, 2])
        shift = sb("shift", [P, 2])
        total = sb("total", [P, 2])
        inv = sb("inv", [P, 2])
        ps = core.ps
        wkv_h = wkv[:, :].rearrange("p (h n) -> p h n", h=HEADS)
        with nc.Block() as block:
            @block.sync
            def _(sp):
                sp.dma_start(wkv[:], w_ukv).then_inc(w_loaded, 16)
                sp.dma_start(wq[:], w_uq.rearrange("(k p) n -> p k n", p=P)).then_inc(w_loaded, 16)

            @block.tensor
            def _(pe):
                pe.wait_ge(w_loaded, 32)
                for t in range(QT):
                    if t >= 4:
                        pe.wait_ge(v_kept, t - 3)
                    nc.tensor.matmul(ps[:, t % 4, :], ckv[:, t * P:(t + 1) * P], wkv_h[:, :, NOPE:],
                                     start=True, stop=True).then_inc(v_made, 1)
                pe.wait_ge(v_kept, QT)

                def sum_squares(n):
                    pe.wait_ge(squared, 2 * n)
                    for i in range(NH):
                        cols = slice(i * HALF, (i + 1) * HALF)
                        nc.tensor.matmul(ps[:, 6 + i, :], core.c("ones", P), sqn[:, cols], start=True, stop=False)
                        last = nc.tensor.matmul(ps[:, 6 + i, :], core.c("ones", P, ROPE), sqr[:, cols], start=False, stop=True)
                    last.then_inc(summed, 1)

                def swap_halves(n, bank):
                    pe.wait_ge(head_scaled, 2 * n)
                    for i in range(NH):
                        last = nc.tensor.matmul(ps[0:ROPE, bank + i, :], core.c("swap", ROPE, ROPE),
                                                rope0[:, i * HALF:(i + 1) * HALF], start=True, stop=True)
                    last.then_inc(turned, 1)

                def prepare(h):
                    if h:
                        pe.wait_ge(out_kept, QT * h)
                    for i in range(NH):
                        cols = slice(i * HALF, (i + 1) * HALF)
                        for k in range(2):
                            nc.tensor.matmul(ps[:, i, :], wq[:, k, h * QKD:h * QKD + NOPE], cq[:, k, cols],
                                             start=(k == 0), stop=(k == 1))
                        for k in range(2):
                            last = nc.tensor.matmul(ps[0:ROPE, 2 + i, :], wq[:, k, h * QKD + NOPE:(h + 1) * QKD],
                                                    cq[:, k, cols], start=(k == 0), stop=(k == 1))
                    last.then_inc(raw, 1)
                    for i in range(NH):
                        cols = slice(i * HALF, (i + 1) * HALF)
                        last = nc.tensor.matmul(ps[:, 4 + i, :], wkv_h[:, h, 0:NOPE], ckv[:, cols], start=True, stop=True)
                    last.then_inc(raw, 1)
                    sum_squares(2 * h + 1)
                    pe.wait_ge(rooted, 2 * h + 1)
                    sum_squares(2 * h + 2)
                    swap_halves(2 * h + 1, 0)
                    swap_halves(2 * h + 2, 2)

                def scores(u):
                    h, t = divmod(u, QT)
                    if t >= 2:
                        pe.wait_ge(probs_ready, u - 1)
                    for i in range(NH):
                        cols = slice(i * HALF, (i + 1) * HALF)
                        nc.tensor.matmul(ps[:, 2 * (u % 2) + i, :], nope[:, 0, t * P:(t + 1) * P], nope[:, 1, cols],
                                         start=True, stop=False)
                        last = nc.tensor.matmul(ps[:, 2 * (u % 2) + i, :], rope[:, 0, t * P:(t + 1) * P],
                                                rope[:, 1, cols], start=False, stop=True)
                    last.then_inc(scores_ready, 1)

                def turn(u):
                    pe.wait_ge(probs_scaled, u + 1)
                    if u:
                        pe.wait_ge(turned_kept, 2 * u)
                    for k in range(QT):
                        last = nc.tensor.transpose(ps[:, 4 + k // 4, (k % 4) * P:(k % 4 + 1) * P],
                                                   probs[:, u % 2, k * P:(k + 1) * P], core.c("ident", P))
                        if k % 4 == 3:
                            last.then_inc(probs_turned, 1)

                def weigh(u):
                    h, t = divmod(u, QT)
                    if u >= 2:
                        pe.wait_ge(out_kept, u - 1)
                    pe.wait_ge(turned_kept, 2 * u + 2)
                    for k in range(QT):
                        last = nc.tensor.matmul(ps[:, 6 + u % 2, 0:P], v[:, k, h * VD:(h + 1) * VD], probsT[:, u % 2, k, :],
                                                start=(k == 0), stop=(k == QT - 1))
                    last.then_inc(out_ready, 1)

                for h in range(HEADS):
                    prepare(h)
                    pe.wait_ge(head_ready, 2 * h + 2)
                    scores(QT * h)
                    for u in range(QT * h, QT * (h + 1)):
                        if u + 1 < QT * (h + 1):
                            scores(u + 1)
                        turn(u)
                        if u > QT * h:
                            weigh(u - 1)
                    weigh(QT * (h + 1) - 1)

            @block.scalar
            def _(act):
                for t in range(QT):
                    act.wait_ge(v_made, t + 1)
                    nc.scalar.activation(v[:, t, :], ps[:, t % 4, :], ACT.Copy).then_inc(v_kept, 1)
                def root(m):
                    act.wait_ge(summed, m + 1)
                    if m:
                        act.wait_ge(inverted, m)
                    nc.scalar.activation(std[:], ps[:, 6:8, :], ACT.Sqrt, bias=core.c("eps"),
                                         scale=1.0 / QKD).then_inc(rooted, 1)

                def exponentials(u):
                    act.wait_ge(shift_ready, u + 1)
                    if u >= 2:
                        act.wait_ge(probs_turned, 2 * (u - 1))
                    b = 2 * (u % 2)
                    nc.scalar.activation(probs[:, u % 2, :], ps[:, b:b + 2, :], ACT.Exp, bias=shift[:, u % 2:u % 2 + 1],
                                         scale=scale, accum_out=total[:, u % 2:u % 2 + 1]).then_inc(probs_ready, 1)

                def keep_turned(u):
                    if u >= 2:
                        act.wait_ge(out_ready, u - 1)
                    for i in range(2):
                        act.wait_ge(probs_turned, 2 * u + i + 1)
                        nc.scalar.activation(probsT[:, u % 2, 4 * i:4 * i + 4, :], ps[:, 4 + i, :], ACT.Copy).then_inc(turned_kept, 1)

                def keep_out(u):
                    h, t = divmod(u, QT)
                    act.wait_ge(out_ready, u + 1)
                    nc.scalar.activation(core.h[:, h, t * P:(t + 1) * P], ps[:, 6 + u % 2, 0:P], ACT.Copy).then_inc(out_kept, 1)

                for h in range(HEADS):
                    m = 2 * h
                    act.wait_ge(raw, m + 1)
                    if m:
                        act.wait_ge(summed, m)
                    nc.scalar.activation(sqn[:], ps[:, 0:2, :], ACT.Square).then_inc(squared, 1)
                    nc.scalar.activation(sqr[:], ps[0:ROPE, 2:4, :], ACT.Square).then_inc(squared, 1)
                    root(m)
                    act.wait_ge(raw, m + 2)
                    nc.scalar.activation(sqn[:], ps[:, 4:6, :], ACT.Square).then_inc(squared, 1)
                    nc.scalar.activation(sqr[:], kr[:], ACT.Square).then_inc(squared, 1)
                    root(m + 1)
                    first, end = QT * h, QT * (h + 1)
                    for u in range(first, end + 2):
                        if u < end:
                            exponentials(u)
                        if first <= u - 1 < end:
                            keep_turned(u - 1)
                        if first <= u - 2:
                            keep_out(u - 2)

            @block.vector
            def _(dve):
                done = [0]

                def tap():
                    t, j = taps[done[0]]
                    acc = core.h[:, HEADS + j, :]
                    if t == 0:
                        nc.vector.tensor_scalar(acc, y[:, j, t:t + S], core.p1("conv_w", j), core.p1("conv_b", j),
                                                ALU.mult, ALU.add).then_inc(tapped, 1)
                    else:
                        dve.wait_ge(tapped, done[0] - KC + 1)
                        nc.vector.scalar_tensor_tensor(acc, y[:, j, t:t + S], core.p1("conv_w", t * KC + j), acc,
                                                       ALU.mult, ALU.add).then_inc(tapped, 1)
                    done[0] += 1

                def tap_some(n):
                    for _ in range(n):
                        if done[0] < len(taps):
                            tap()

                def invert(m):
                    dve.wait_ge(rooted, m + 1)
                    nc.vector.reciprocal(rstd[:], std[:]).then_inc(inverted, 1)
                    dve.wait_ge(inverted, m + 1)

                def scale_head(m, key):
                    gn, gr = ("kg_nope", "kg_rope") if key else ("qg_nope", "qg_rope")
                    b = 4 if key else 0
                    nc.vector.scalar_tensor_tensor(rope0[:], kr[:] if key else ps[0:ROPE, 2:4, :], core.p1(gr, 0, ROPE),
                                                   rstd[0:ROPE, :], ALU.mult, ALU.mult).then_inc(head_scaled, 1)
                    nc.vector.scalar_tensor_tensor(nope[:, key, :], ps[:, b:b + 2, :], core.p1(gn), rstd[:],
                                                   ALU.mult, ALU.mult).then_inc(head_scaled, 1)
                    dve.wait_ge(head_scaled, 2 * m + 2)
                    nc.vector.tensor_tensor(part[:, 0, :], rope0[:], cos[:], ALU.mult).then_inc(part_made, 1)

                def rotate(m, key):
                    dve.wait_ge(turned, m + 1)
                    nc.vector.tensor_tensor(part[:, 1, :], ps[0:ROPE, 2 * key:2 * key + 2, :], sin[:], ALU.mult).then_inc(part_made, 1)
                    dve.wait_ge(part_made, 2 * m + 2)
                    nc.vector.tensor_tensor(rope[:, key, :], part[:, 0, :], part[:, 1, :], ALU.add).then_inc(head_ready, 1)

                for h in range(HEADS):
                    invert(2 * h)
                    scale_head(2 * h, 0)
                    invert(2 * h + 1)
                    rotate(2 * h, 0)
                    dve.wait_ge(head_ready, 2 * h + 1)
                    scale_head(2 * h + 1, 1)
                    rotate(2 * h + 1, 1)
                    for u in range(QT * h, QT * (h + 1)):
                        b, c = 2 * (u % 2), u % 2
                        dve.wait_ge(scores_ready, u + 1)
                        nc.vector.tensor_reduce(peak[:, c:c + 1], ps[:, b:b + 2, :].rearrange("p a n -> p (a n)"), AX_X,
                                                ALU.max).then_inc(peak_found, 1)
                        dve.wait_ge(peak_found, u + 1)
                        nc.vector.tensor_scalar(shift[:, c:c + 1], peak[:, c:c + 1], -scale, None,
                                                ALU.mult).then_inc(shift_ready, 1)
                        tap_some(1)
                        dve.wait_ge(probs_ready, u + 1)
                        nc.vector.reciprocal(inv[:, c:c + 1], total[:, c:c + 1]).then_inc(total_inverted, 1)
                        dve.wait_ge(total_inverted, u + 1)
                        nc.vector.tensor_scalar(probs[:, c, :], probs[:, c, :], inv[:, c:c + 1], None,
                                                ALU.mult).then_inc(probs_scaled, 1)
                        tap_some(per_unit - 1)
                assert done[0] == len(taps)


def layer_norm(core, tiles, width, eps, lhsT, g, b, func):
    nc = core.nc
    kt = len(tiles)
    groups = kt if width == HD else 1
    with ExitStack() as held, stage(nc, "mean_sum", "centred", "squared", "summed", "rooted", "inverted", "scaled", "done") as \
            (mean_sum, centred, squared, summed, rooted, inverted, scaled, done):
        sq = held.enter_context(nc.sbuf_tensor("sq", [P, kt, S], F32, allow_name_mangling=True))
        ps = core.ps

        def group(k):
            return k if groups > 1 else 0
        with nc.Block() as block:
            @block.tensor
            def _(pe):
                for second in range(2):
                    for k in range(kt):
                        if second:
                            pe.wait_ge(squared, k + 1)
                            if k == 0:
                                pe.wait_ge(centred, kt)
                        src = sq[:, k, :] if second else tiles[k]
                        for i in range(NH):
                            last = nc.tensor.matmul(ps[:, 2 * group(k) + i, :], lhsT, src[:, i * HALF:(i + 1) * HALF],
                                                    start=(groups > 1 or k == 0), stop=(groups > 1 or k == kt - 1))
                        if groups > 1 or k == kt - 1:
                            last.then_inc(summed if second else mean_sum, 1)

            @block.scalar
            def _(act):
                for k in range(kt):
                    act.wait_ge(centred, k + 1)
                    nc.scalar.activation(sq[:, k, :], tiles[k], ACT.Square).then_inc(squared, 1)
                for q in range(groups):
                    act.wait_ge(summed, q + 1)
                    nc.scalar.activation(sq[:, q, :], flat(ps[:, 2 * q:2 * q + 2, :]), ACT.Sqrt, bias=eps,
                                         scale=1.0 / width).then_inc(rooted, 1)
                for k in range(kt):
                    act.wait_ge(scaled, k + 1)
                    nc.scalar.activation(tiles[k], tiles[k], func, bias=b(k)).then_inc(done, 1)

            @block.vector
            def _(dve):
                for k in range(kt):
                    dve.wait_ge(mean_sum, group(k) + 1)
                    q = 2 * group(k)
                    nc.vector.scalar_tensor_tensor(tiles[k], flat(ps[:, q:q + 2, :]), -1.0 / width, tiles[k],
                                                   ALU.mult, ALU.add).then_inc(centred, 1)
                for q in range(groups):
                    dve.wait_ge(rooted, q + 1)
                    nc.vector.reciprocal(sq[:, q, :], sq[:, q, :]).then_inc(inverted, 1)
                for k in range(kt):
                    dve.wait_ge(inverted, group(k) + 1)
                    nc.vector.scalar_tensor_tensor(tiles[k], tiles[k], g(k), sq[:, group(k), :],
                                                   ALU.mult, ALU.mult).then_inc(scaled, 1)


def out_projection(core, w, gate_at):
    nc = core.nc
    parts = 4
    width = D // parts
    with ExitStack() as held, stage(nc, "wa", "wb", "wc", "wd", "grouped", "added", "squared",
                                    "totalled") as \
            (wa, wb, wc, wd, grouped, added, squared, totalled):
        ws = held.enter_context(nc.sbuf_tensor("w_out", [P, KD, D], F32, allow_name_mangling=True))
        sq = held.enter_context(nc.sbuf_tensor("sq", [P, 2, S], F32, allow_name_mangling=True))
        landed = [wa, wb, wc, wd]
        with nc.Block() as block:
            @block.sync
            def _(sp):
                for i in range(parts):
                    sp.dma_start(ws[:, :, i * width:(i + 1) * width],
                                 w.rearrange("(k p) n -> p k n", p=P)[:, :, i * width:(i + 1) * width]).then_inc(landed[i], 16)

            @block.tensor
            def _(pe):
                for j in range(KD):
                    if j * P % width == 0:
                        pe.wait_ge(landed[j * P // width], 16)
                    if j >= 4:
                        pe.wait_ge(added, j - 3)
                    for i in range(NH):
                        for k in range(KD):
                            last = nc.tensor.matmul(core.ps[:, 2 * (j % 4) + i, :], ws[:, k, j * P:(j + 1) * P],
                                                    core.h[:, k, i * HALF:(i + 1) * HALF],
                                                    start=(k == 0), stop=(k == KD - 1))
                    last.then_inc(grouped, 1)

            @block.scalar
            def _(act):
                square_tiles(core, act, sq, added, squared, totalled)

            @block.vector
            def _(dve):
                add_and_total(core, dve, gate_at, sq, grouped, added, squared, totalled)


PER = 4
PIECES = 3 * PER
KPP = KD // PER


def load_piece(eng, ring, landed, mats, e, c):
    eng.dma_start(ring[:, c, :, :], mats[c // PER][e].rearrange("(k p) f -> p k f", p=P)[
        :, (c % PER) * KPP:(c % PER + 1) * KPP, :]).then_inc(landed[c], 16)


def route(core, ring, landed, mats, w_router, h_rows, slot_rows, aff_rows):
    nc = core.nc
    with ExitStack() as held, stage(
            nc, "w_loaded", "logits_ready", "peak_found", "less_peak", "exp_ready", "total_ready", "aff_ready",
            "aff_turned", "affT_ready", "eights", "replaced", "ones_set", "picked", "counted", "slots_ready",
            "rows_turned", "rows_kept", "rows_out_a", "rows_out_b", "small_out") as \
            (w_loaded, logits_ready, peak_found, less_peak, exp_ready, total_ready, aff_ready,
             aff_turned, affT_ready, eights, replaced, ones_set, picked, counted, slots_ready,
             rows_turned, rows_kept, rows_out_a, rows_out_b, small_out):
        def sb(name, shape):
            return held.enter_context(nc.sbuf_tensor(name, shape, F32, allow_name_mangling=True))

        wr = sb("w_router", [P, KD, N_EXP])
        peak = sb("peak", [P, QT])
        less = sb("less", [P, QT, N_EXP])
        aff = sb("aff", [P, QT, N_EXP])
        total = sb("total", [P, QT])
        affT = sb("affT", [N_EXP, S])
        left = sb("left", [N_EXP, 2, S])
        big = sb("big", [N_EXP, 2, 8])
        slots = core.rstd[0:N_EXP, :]
        rows = sb("rows", [P, 2, D])
        rows_out = [rows_out_a, rows_out_b]
        ps = core.ps
        logits = ps[:, 0, 0:QT * N_EXP].rearrange("p (t e) -> p t e", t=QT)
        with nc.Block() as block:
            @block.sync
            def _(sp):
                sp.dma_start(wr[:], w_router.rearrange("(k p) e -> p k e", p=P)).then_inc(w_loaded, 16)
                for t in range(QT):
                    sp.wait_ge(rows_kept, 2 * t + 2)
                    sp.dma_start(h_rows[t * P:(t + 1) * P, :], rows[:, t % 2, :]).then_inc(rows_out[t % 2], 16)
                for c in range(PIECES):
                    load_piece(sp, ring, landed, mats, 0, c)
                sp.wait_ge(affT_ready, 1)
                sp.dma_start(aff_rows, affT[:]).then_inc(small_out, 16)
                sp.wait_ge(slots_ready, 1)
                sp.dma_start(slot_rows, slots).then_inc(small_out, 16)
                sp.wait_ge(small_out, 32)
                sp.wait_ge(rows_out_a, 16 * QT // 2)
                sp.wait_ge(rows_out_b, 16 * QT // 2)

            @block.tensor
            def _(pe):
                pe.wait_ge(w_loaded, 16)
                for t in range(QT):
                    for k in range(KD):
                        last = nc.tensor.matmul(logits[:, t, :], core.h[:, k, t * P:(t + 1) * P], wr[:, k, :],
                                                start=(k == 0), stop=(k == KD - 1))
                last.then_inc(logits_ready, 1)
                pe.wait_ge(aff_ready, 1)
                for t in range(QT):
                    last = nc.tensor.transpose(ps[0:N_EXP, 2 + t // 4, (t % 4) * P:(t % 4 + 1) * P], aff[:, t, :], core.c("ident", P))
                last.then_inc(aff_turned, 1)
                for t in range(QT):
                    if t >= 2:
                        pe.wait_ge(rows_kept, 2 * (t - 1))
                    for k in range(KD):
                        last = nc.tensor.transpose(ps[:, 4 + 2 * (t % 2) + k // 4, (k % 4) * P:(k % 4 + 1) * P],
                                                   core.h[:, k, t * P:(t + 1) * P], core.c("ident", P))
                    last.then_inc(rows_turned, 1)

            @block.scalar
            def _(act):
                act.wait_ge(less_peak, 1)
                nc.scalar.activation(less[:], less[:], ACT.Exp).then_inc(exp_ready, 1)
                for t in range(QT):
                    act.wait_ge(rows_turned, t + 1)
                    if t >= 2:
                        act.wait_ge(rows_out[t % 2], 16 * (t // 2))
                    for i in range(2):
                        nc.scalar.activation(rows[:, t % 2, i * HALF:(i + 1) * HALF], ps[:, 4 + 2 * (t % 2) + i, :],
                                             ACT.Copy).then_inc(rows_kept, 1)

            @block.vector
            def _(dve):
                dve.wait_ge(logits_ready, 1)
                nc.vector.tensor_reduce(peak[:], logits, AX_X, ALU.max).then_inc(peak_found, 1)
                dve.wait_ge(peak_found, 1)
                nc.vector.tensor_tensor(less[:], logits, peak[:].unsqueeze(2).to_broadcast([P, QT, N_EXP]),
                                        ALU.subtract).then_inc(less_peak, 1)
                dve.wait_ge(exp_ready, 1)
                nc.vector.tensor_reduce(total[:], less[:], AX_X, ALU.add).then_inc(total_ready, 1)
                dve.wait_ge(total_ready, 1)
                nc.vector.reciprocal(total[:], total[:]).then_inc(total_ready, 1)
                dve.wait_ge(total_ready, 2)
                nc.vector.tensor_tensor(aff[:], less[:], total[:].unsqueeze(2).to_broadcast([P, QT, N_EXP]),
                                        ALU.mult).then_inc(aff_ready, 1)
                dve.wait_ge(aff_turned, 1)
                nc.vector.tensor_copy(affT[:], ps[0:N_EXP, 2:4, :].rearrange("p a n -> p (a n)")).then_inc(affT_ready, 1)
                dve.wait_ge(affT_ready, 1)
                for r in range(TOP8):
                    src = affT[:] if r == 0 else left[:, (r - 1) % 2, :]
                    if r:
                        dve.wait_ge(replaced, r)
                    nc.vector.max(big[:, r % 2, :], src).then_inc(eights, 1)
                    dve.wait_ge(eights, r + 1)
                    nc.vector.match_replace(left[:, r % 2, :], big[:, r % 2, :], src, -1.0).then_inc(replaced, 1)
                dve.wait_ge(replaced, TOP8)
                nc.vector.tensor_scalar(left[:, 0, :], left[:, (TOP8 - 1) % 2, :], 0.0, None, ALU.is_lt).then_inc(picked, 1)
                dve.wait_ge(picked, 1)
                nc.vector.memset(left[:, 1, :], 1.0).then_inc(ones_set, 1)
                dve.wait_ge(ones_set, 1)
                nc.vector.tensor_tensor_scan(slots, left[:, 1, :], left[:, 0, :], 0.0, ALU.mult, ALU.add).then_inc(counted, 1)
                dve.wait_ge(counted, 1)
                nc.vector.tensor_tensor(slots, slots, left[:, 0, :], ALU.mult).then_inc(counted, 1)
                dve.wait_ge(counted, 2)
                nc.vector.tensor_scalar(slots, slots, -1.0, None, ALU.add).then_inc(slots_ready, 1)


def experts(core, ring, landed, mats, h_rows, slot_rows, aff_rows, gate_at):
    nc = core.nc
    per, pieces, kp = PER, PIECES, KPP
    groups = KD * NH
    last_e = N_EXP - 1
    with ExitStack() as held, stage(
            nc, "w_used", "rows_loaded", "sel_built", "idx_summed", "idx_built", "gate_built", "gathered",
            "xe_turned", "xeT_kept", "silu_ready", "hid_ready", "hid_turned", "hidT_kept",
            "ye_kept", "part_cast", "part_less", "brought", "added", "spare_set") as sems:
        (w_used, rows_loaded, sel_built, idx_summed, idx_built, gate_built, gathered, xe_turned, xeT_kept,
         silu_ready, hid_ready, hid_turned, hidT_kept, ye_kept, part_cast, part_less, brought, added,
         spare_set) = sems

        def sb(name, shape, dt=F32):
            return held.enter_context(nc.sbuf_tensor(name, shape, dt, allow_name_mangling=True))

        sel = sb("sel", [P, 2, S], BF16)
        part = sb("result_parts", [P, 3, D], BF16)
        idxf = sb("idxf", [P, 2])
        idx = sb("idx", [P, 2], U32)
        gate = sb("gate", [P, 2])
        xe, xeT, sg, hid, hidT, ye, slot_b, aff_b = (core.h[:, i, :] for i in range(8))
        junk = sb("junk", [P, S])
        spare = sb("spare", [P, 2])
        ps = core.ps

        with nc.Block() as block:
            @block.sync
            def _(sp):
                with sp.Fori(1, N_EXP) as e:
                    for c in range(pieces):
                        sp.wait_ge(w_used, (e - 1) * pieces + (c + 1))
                        load_piece(sp, ring, landed, mats, e, c)

            @block.gpsimd
            def _(pool):
                def rows(e):
                    pool.dma_start(slot_b, slot_rows[e].partition_broadcast(P)).then_inc(rows_loaded, 16)
                    pool.dma_start(aff_b, aff_rows[e].partition_broadcast(P)).then_inc(rows_loaded, 16)

                def gather(e, b):
                    pool.wait_ge(spare_set, e + 1)
                    pool.wait_ge(idx_built, e + 1)
                    nc.gpsimd.tensor_tensor(spare[:, 1:2], spare[:, 0:1], spare[:, 0:1], ALU.add).then_inc(spare_set, 1)
                    nc.gpsimd.indirect_dma_start(xe, None, h_rows, bass.IndirectOffsetOnAxis(ap=idx[:, b:b + 1], axis=0),
                                                 ).then_inc(gathered, 16)

                nc.gpsimd.memset(spare[:], 0.0).then_inc(spare_set, 1)
                pool.wait_ge(spare_set, 1)
                rows(0)
                gather(0, 0)

                def ahead(e, b):
                    pool.wait_ge(sel_built, e)
                    pool.wait_ge(gate_built, e)
                    rows(e)
                    pool.wait_ge(xe_turned, e)
                    gather(e, b)

                with pool.Fori(0, N_EXP // 2 - 1) as i:
                    ahead(2 * i + 1, 1)
                    ahead(2 * i + 2, 0)
                ahead(last_e, 1)

            @block.tensor
            def _(pe):
                def turn_tokens(e):
                    pe.wait_ge(gathered, 16 * (e + 1))
                    for k in range(KD):
                        last = nc.tensor.transpose(ps[:, 6 + k // 4, (k % 4) * P:(k % 4 + 1) * P],
                                                   xe[:, k * P:(k + 1) * P], core.c("ident", P))
                    last.then_inc(xe_turned, 1)

                def product(e, m, lhs, bank):
                    for k in range(KD):
                        c = m * per + k // kp
                        if k % kp == 0:
                            pe.wait_ge(landed[c], 16 * (e + 1))
                        for i in range(2):
                            last = nc.tensor.matmul(ps[:, bank + i, :], lhs[:, k * P:(k + 1) * P],
                                                    ring[:, c, k % kp, i * HALF:(i + 1) * HALF],
                                                    start=(k == 0), stop=(k == KD - 1))
                        if k % kp == kp - 1 and k < KD - 1:
                            last.then_inc(w_used, 1)
                    return last

                def bring_back(e, b):
                    pe.wait_ge(sel_built, e + 1)
                    pe.wait_ge(part_less, 2 * e + 2)
                    for n in range(groups):
                        j, i = divmod(n, NH)
                        if n >= 4:
                            pe.wait_ge(added, groups * e + (n - 3))
                        for m in range(3):
                            last = nc.tensor.matmul(ps[:, 4 + n % 4, :], part[:, m, j * P:(j + 1) * P],
                                                    sel[:, b, i * HALF:(i + 1) * HALF], start=(m == 0), stop=(m == 2))
                        last.then_inc(brought, 1)

                def turn_hidden(e):
                    pe.wait_ge(hid_ready, e + 1)
                    for k in range(KD):
                        last = nc.tensor.transpose(ps[:, 4 + k // 4, (k % 4) * P:(k % 4 + 1) * P],
                                                   hid[:, k * P:(k + 1) * P], core.c("ident", P))
                    last.then_inc(hid_turned, 1)

                def expert(e, b, first=False, final=False):
                    pe.wait_ge(xeT_kept, 2 * (e + 1))
                    product(e, 0, xeT, 0).then_inc(w_used, 1)
                    if not first:
                        pe.wait_ge(ye_kept, e)
                    product(e, 1, xeT, 2).then_inc(w_used, 1)
                    if not first:
                        bring_back(e - 1, 1 - b)
                        pe.wait_ge(added, groups * e)
                    turn_hidden(e)
                    if not final:
                        turn_tokens(e + 1)
                    pe.wait_ge(hidT_kept, 2 * (e + 1))
                    product(e, 2, hidT, 2).then_inc(w_used, 1)

                turn_tokens(0)
                expert(0, 0, first=True)
                with pe.Fori(0, N_EXP // 2 - 1) as i:
                    expert(2 * i + 1, 1)
                    expert(2 * i + 2, 0)
                expert(last_e, 1, final=True)
                bring_back(last_e, 1)

            @block.scalar
            def _(act):
                def keep_tokens(e):
                    act.wait_ge(xe_turned, e + 1)
                    for i in range(2):
                        nc.scalar.activation(xeT[:, i * HALF:(i + 1) * HALF], ps[:, 6 + i, :], ACT.Copy).then_inc(xeT_kept, 1)

                def keep_result(e, b):
                    act.wait_ge(w_used, pieces * (e + 1))
                    act.wait_ge(gate_built, e + 1)
                    nc.scalar.activation(ye, ps[:, 2:4, :].rearrange("p a n -> p (a n)"), ACT.Copy,
                                         scale=gate[:, b:b + 1]).then_inc(ye_kept, 1)
                    act.wait_ge(ye_kept, e + 1)
                    nc.scalar.activation(part[:, 0, :], ye, ACT.Copy).then_inc(part_cast, 1)
                    act.wait_ge(part_less, 2 * e + 1)
                    nc.scalar.activation(part[:, 1, :], ye, ACT.Copy).then_inc(part_cast, 1)

                def expert(e, b, first=False, final=False):
                    if not first:
                        keep_result(e - 1, 1 - b)
                    act.wait_ge(w_used, pieces * e + per)
                    nc.scalar.activation(sg, ps[:, 0:2, :].rearrange("p a n -> p (a n)"), ACT.Silu).then_inc(silu_ready, 1)
                    act.wait_ge(hid_turned, e + 1)
                    for i in range(2):
                        nc.scalar.activation(hidT[:, i * HALF:(i + 1) * HALF], ps[:, 4 + i, :], ACT.Copy).then_inc(hidT_kept, 1)
                    if not final:
                        keep_tokens(e + 1)

                keep_tokens(0)
                expert(0, 0, first=True)
                with act.Fori(0, N_EXP // 2 - 1) as i:
                    expert(2 * i + 1, 1)
                    expert(2 * i + 2, 0)
                expert(last_e, 1, final=True)
                keep_result(last_e, 1)

            @block.vector
            def _(dve):
                def find(e, b):
                    dve.wait_ge(rows_loaded, 32 * (e + 1))
                    nc.vector.scalar_tensor_tensor(junk[:], slot_b, core.c("slot"), core.c("token", S), ALU.is_equal,
                                                   ALU.mult, accum_out=idxf[:, b:b + 1]).then_inc(idx_summed, 1)
                    dve.wait_ge(idx_summed, e + 1)
                    nc.vector.tensor_copy(idx[:, b:b + 1], idxf[:, b:b + 1]).then_inc(idx_built, 1)
                    nc.vector.scalar_tensor_tensor(junk[:], slot_b, core.c("slot"), aff_b, ALU.is_equal,
                                                   ALU.mult, accum_out=gate[:, b:b + 1]).then_inc(gate_built, 1)

                def select(e, b):
                    nc.vector.tensor_scalar(sel[:, b, :], slot_b, core.c("slot"), None, ALU.is_equal).then_inc(sel_built, 1)

                def split(e):
                    dve.wait_ge(part_cast, 2 * e + 1)
                    nc.vector.tensor_tensor(ye, ye, part[:, 0, :], ALU.subtract).then_inc(part_less, 1)
                    dve.wait_ge(part_cast, 2 * e + 2)
                    nc.vector.tensor_tensor(part[:, 2, :], ye, part[:, 1, :], ALU.subtract).then_inc(part_less, 1)

                def add(e):
                    for n in range(groups):
                        j, i = divmod(n, NH)
                        cols = slice(i * HALF, (i + 1) * HALF)
                        dve.wait_ge(brought, groups * e + (n + 1))
                        nc.vector.scalar_tensor_tensor(core.x[:, j, cols], ps[:, 4 + n % 4, :],
                                                       core.mod[:, gate_at + j:gate_at + j + 1], core.x[:, j, cols],
                                                       ALU.mult, ALU.add).then_inc(added, 1)

                def expert(e, b, first=False, final=False):
                    if not first:
                        split(e - 1)
                    if not final:
                        if not first:
                            dve.wait_ge(ye_kept, e)
                        find(e + 1, 1 - b)
                    dve.wait_ge(silu_ready, e + 1)
                    dve.wait_ge(w_used, pieces * e + 2 * per)
                    nc.vector.tensor_tensor(hid, sg, ps[:, 2:4, :].rearrange("p a n -> p (a n)"), ALU.mult).then_inc(hid_ready, 1)
                    if not first:
                        add(e - 1)
                    if not final:
                        select(e + 1, 1 - b)

                find(0, 0)
                select(0, 0)
                expert(0, 0, first=True)
                with dve.Fori(0, N_EXP // 2 - 1) as i:
                    expert(2 * i + 1, 1)
                    expert(2 * i + 2, 0)
                expert(last_e, 1, final=True)
                split(last_e)
                add(last_e)


def store_output(core, src, out):
    nc = core.nc
    with stage(nc, "stored") as (stored,):
        with nc.Block() as block:
            @block.sync
            def _(sp):
                sp.dma_start(out.rearrange("(k p) s -> p k s", p=P), src[:]).then_inc(stored, 16)
                sp.wait_ge(stored, 16)


T_U, T_V, T_XR, T_YG = 0, KA, 2 * KA, 2 * KA + KB
T_R = 2 * KA + 2 * KB
T_K, T_VV, T_WA, T_XG = T_R + KCC, T_R + 2 * KCC, T_R + 3 * KCC, T_R + 3 * KCC + 1
N_P = IN2 // P


def project_two(core, w, gains, p):
    nc = core.nc
    slots = 4
    gelus = set(range(T_U, T_XR)) | set(range(T_YG, T_R))
    with ExitStack() as held, stage(nc, "w0", "w1", "w2", "w3", "grouped", "kept", "gained", "h_scaled", "h_shifted") as \
            (w0, w1, w2, w3, grouped, kept, gained, h_scaled, h_shifted):
        ws = held.enter_context(nc.sbuf_tensor("w_block", [P, slots, KD, P], F32, allow_name_mangling=True))
        landed = [w0, w1, w2, w3]
        w_k = w.rearrange("(k p) n -> p k n", p=P)
        with nc.Block() as block:
            @block.sync
            def _(sp):
                for g in range(N_P):
                    if g >= slots:
                        sp.wait_ge(grouped, g - slots + 1)
                    sp.dma_start(ws[:, g % slots, :, :], w_k[:, :, g * P:(g + 1) * P]).then_inc(landed[g % slots], 16)

            @block.tensor
            def _(pe):
                for g in range(N_P):
                    pe.wait_ge(landed[g % slots], 16 * (g // slots + 1))
                    if g >= 4:
                        pe.wait_ge(kept, g - 3)
                    for i in range(NH):
                        for k in range(KD):
                            if g == 0 and i == 0:
                                pe.wait_ge(h_shifted, k + 1)
                            last = nc.tensor.matmul(core.ps[:, 2 * (g % 4) + i, :], ws[:, g % slots, k, :],
                                                    core.h[:, k, i * HALF:(i + 1) * HALF],
                                                    start=(k == 0), stop=(k == KD - 1))
                    last.then_inc(grouped, 1)

            @block.vector
            def _(dve):
                scale_tiles(core, dve, gains, gained, h_scaled)

            @block.scalar
            def _(act):
                shift_tiles(core, act, h_scaled, h_shifted)
                for g in range(N_P):
                    act.wait_ge(grouped, g + 1)
                    b = 2 * (g % 4)
                    nc.scalar.activation(p[:, g, :], flat(core.ps[:, b:b + 2, :]),
                                         ACT.Gelu_apprx_tanh if g in gelus else ACT.Copy).then_inc(kept, 1)


def spatial_gate(core, p, w_s, b_s):
    nc = core.nc
    heads = D_A // HD
    with ExitStack() as held, stage(nc, "loaded", "w_turned", "w_masked", "v_turned", "v_kept", "mixed", "gated") as \
            (loaded, w_turned, w_masked, v_turned, v_kept, mixed, gated):
        ws = held.enter_context(nc.sbuf_tensor("w_s", [P, heads, P], F32, allow_name_mangling=True))
        wT = held.enter_context(nc.sbuf_tensor("w_sT", [P, heads, P], F32, allow_name_mangling=True))
        bs = held.enter_context(nc.sbuf_tensor("b_s", [1, heads * P], F32, allow_name_mangling=True))
        vt = held.enter_context(nc.sbuf_tensor("v_tok", [P, QT, KA, P], F32, allow_name_mangling=True))
        ps = core.ps
        with nc.Block() as block:
            @block.sync
            def _(sp):
                sp.dma_start(ws[:], w_s.rearrange("h t s -> t h s")).then_inc(loaded, 16)
                sp.dma_start(bs[:], b_s).then_inc(loaded, 16)

            @block.tensor
            def _(pe):
                for c in range(QT):
                    for k in range(KA):
                        n = c * KA + k
                        last = nc.tensor.transpose(ps[:, n // 4, (n % 4) * P:(n % 4 + 1) * P],
                                                   p[:, T_V + k, c * P:(c + 1) * P], core.c("ident", P))
                    if n % 4 == 3:
                        last.then_inc(v_turned, 1)
                pe.wait_ge(loaded, 32)
                for h in range(heads):
                    last = nc.tensor.transpose(ps[:, 4, h * P:(h + 1) * P], ws[:, h, :], core.c("ident", P))
                last.then_inc(w_turned, 1)
                pe.wait_ge(w_masked, 1)
                pe.wait_ge(v_kept, 4)
                for k in range(KA):
                    for c in range(QT):
                        for half in range(2):
                            h = 2 * k + half
                            out = ps[half * HD:(half + 1) * HD, 4 + 2 * k + c // 4, (c % 4) * P:(c % 4 + 1) * P]
                            nc.tensor.matmul(out, vt[:, c, k, half * HD:(half + 1) * HD], wT[:, h, :], start=True, stop=False)
                            last = nc.tensor.matmul(out, core.c("ones", HD, 1), bs[:, h * P:(h + 1) * P], start=False, stop=True)
                    last.then_inc(mixed, 1)

            @block.scalar
            def _(act):
                for b in range(4):
                    act.wait_ge(v_turned, b + 1)
                    nc.scalar.activation(vt[:, 2 * b:2 * b + 2, :, :].rearrange("p c k n -> p (c k n)"), ps[:, b, :],
                                         ACT.Copy).then_inc(v_kept, 1)

            @block.vector
            def _(dve):
                dve.wait_ge(w_turned, 1)
                mask = core.c("causal", P).unsqueeze(1).to_broadcast([P, heads, P])
                nc.vector.tensor_tensor(wT[:], ps[:, 4, :].rearrange("p (h t) -> p h t", h=heads), mask,
                                        ALU.mult).then_inc(w_masked, 1)
                for k in range(KA):
                    dve.wait_ge(mixed, k + 1)
                    nc.vector.tensor_tensor(core.h[:, k, :], p[:, T_U + k, :], flat(ps[:, 4 + 2 * k:6 + 2 * k, :]),
                                            ALU.mult).then_inc(gated, 1)


def linear_recurrence(core, p, w_a, w_x):
    nc = core.nc
    with ExitStack() as held, stage(nc, "blank", "loaded", "step", "convolved", "gates_ready", "gates_kept", "decayed",
                                    "ratio_ready", "rooted", "out_done") as \
            (blank, loaded, step, convolved, gates_ready, gates_kept, decayed, ratio_ready, rooted, out_done):
        def sb(name, shape):
            return held.enter_context(nc.sbuf_tensor(name, shape, F32, allow_name_mangling=True))

        bd = sb("w_gates", [P, 2, KB, P])
        col = sb("lam_cols", [P, 6, KB])
        xc = sb("xc", [P, S])
        r = sb("r_gate", [P, S])
        ig = sb("i_gate", [P, S])
        a = sb("a_decay", [P, S])
        t = sb("tanh", [P, S])
        u = sb("ratio", [P, S])
        ps = core.ps
        with nc.Block() as block:
            @block.gpsimd
            def _(pool):
                nc.gpsimd.memset(bd[:], 0.0).then_inc(blank, 1)

            @block.sync
            def _(sp):
                sp.wait_ge(blank, 1)
                for g, w in enumerate((w_a, w_x)):
                    for half in range(2):
                        rows = slice(half * HD, (half + 1) * HD)
                        sp.dma_start(bd[rows, g, :, half * HD:(half + 1) * HD],
                                     w.rearrange("(k two) i j -> two i k j", two=2)[half]).then_inc(loaded, 16)

            @block.tensor
            def _(pe):
                pe.wait_ge(loaded, 64)
                for k in range(KB):
                    pe.wait_ge(convolved, k + 1)
                    for g in range(2):
                        for i in range(NH):
                            last = nc.tensor.matmul(ps[:, 2 * g + i, :], bd[:, g, k, :], xc[:, i * HALF:(i + 1) * HALF],
                                                    start=True, stop=True)
                    last.then_inc(gates_ready, 1)

            @block.scalar
            def _(act):
                lam = core.p2("lru_lambda", 0, KB)
                nc.scalar.activation(col[:, 0, :], lam, ACT.Abs).then_inc(decayed, 1)
                act.wait_ge(decayed, 1)
                nc.scalar.activation(col[:, 0, :], col[:, 0, :], ACT.Exp, scale=-1.0).then_inc(decayed, 1)
                for k in range(KB):
                    act.wait_ge(gates_ready, k + 1)
                    if k:
                        act.wait_ge(out_done, k)
                    nc.scalar.activation(r[:], flat(ps[:, 0:2, :]), ACT.Sigmoid, bias=core.p2("lru_b_a", k)).then_inc(gates_kept, 1)
                    nc.scalar.activation(ig[:], flat(ps[:, 2:4, :]), ACT.Sigmoid, bias=core.p2("lru_b_x", k)).then_inc(gates_kept, 1)
                    act.wait_ge(gates_kept, 2 * k + 1)
                    if k == 0:
                        act.wait_ge(ratio_ready, 1)
                    nc.scalar.activation(t[:], r[:], ACT.Tanh, scale=col[:, 5, k:k + 1]).then_inc(decayed, 1)
                    nc.scalar.activation(a[:], r[:], ACT.Exp, scale=col[:, 4, k:k + 1]).then_inc(decayed, 1)
                    act.wait_ge(ratio_ready, k + 2)
                    nc.scalar.activation(u[:], u[:], ACT.Sqrt).then_inc(rooted, 1)

            @block.vector
            def _(dve):
                n = [0]

                def after(ins):
                    ins.then_inc(step, 1)
                    n[0] += 1
                    dve.wait_ge(step, n[0])

                dve.wait_ge(decayed, 2)
                after(nc.vector.tensor_scalar(col[:, 1, :], col[:, 0, :], 2.0, None, ALU.add))
                after(nc.vector.reciprocal(col[:, 1, :], col[:, 1, :]))
                after(nc.vector.tensor_tensor(col[:, 1, :], col[:, 1, :], col[:, 0, :], ALU.mult))
                after(nc.vector.tensor_tensor(col[:, 2, :], col[:, 1, :], col[:, 1, :], ALU.mult))
                terms = 9
                after(nc.vector.tensor_scalar(col[:, 3, :], col[:, 2, :], 1.0 / (2 * terms + 1), 1.0 / (2 * terms - 1),
                                              ALU.mult, ALU.add))
                for m in range(terms - 2, -1, -1):
                    after(nc.vector.tensor_tensor(col[:, 3, :], col[:, 3, :], col[:, 2, :], ALU.mult))
                    after(nc.vector.tensor_scalar(col[:, 3, :], col[:, 3, :], 1.0 / (2 * m + 1), None, ALU.add))
                after(nc.vector.scalar_tensor_tensor(col[:, 3, :], col[:, 3, :], 2.0, col[:, 1, :], ALU.mult, ALU.mult))
                after(nc.vector.tensor_scalar(col[:, 1, :], core.p2("lru_lambda", 0, KB), -1.0, 0.0, ALU.mult, ALU.max))
                after(nc.vector.tensor_tensor(col[:, 3, :], col[:, 3, :], col[:, 1, :], ALU.add))
                after(nc.vector.tensor_scalar(col[:, 4, :], col[:, 3, :], -LRU_C, None, ALU.mult))
                nc.vector.tensor_scalar(col[:, 5, :], col[:, 3, :], LRU_C, None, ALU.mult).then_inc(ratio_ready, 1)
                for k in range(KB):
                    x = p[:, T_XR + k, :]
                    tap = CONV_B - 1
                    after(nc.vector.tensor_scalar(xc[:], x, core.p2("lru_conv_w", tap * KB + k), core.p2("lru_conv_b", k),
                                                  ALU.mult, ALU.add))
                    for back in range(1, CONV_B):
                        ins = nc.vector.scalar_tensor_tensor(xc[:, back:], x[:, 0:S - back],
                                                             core.p2("lru_conv_w", (tap - back) * KB + k), xc[:, back:],
                                                             ALU.mult, ALU.add)
                        if back < CONV_B - 1:
                            after(ins)
                    ins.then_inc(convolved, 1)
                    dve.wait_ge(decayed, 2 + 2 * k + 1)
                    after(nc.vector.tensor_scalar(u[:], t[:], 1.0, None, ALU.add))
                    after(nc.vector.reciprocal(u[:], u[:]))
                    after(nc.vector.scalar_tensor_tensor(u[:], t[:], 2.0, u[:], ALU.mult, ALU.mult))
                    nc.vector.tensor_scalar(u[:], u[:], 2.0 ** -100, None, ALU.max).then_inc(ratio_ready, 1)
                    dve.wait_ge(gates_kept, 2 * k + 2)
                    after(nc.vector.tensor_tensor(ig[:], ig[:], xc[:], ALU.mult))
                    dve.wait_ge(rooted, k + 1)
                    after(nc.vector.tensor_tensor(ig[:], ig[:], u[:], ALU.mult))
                    dve.wait_ge(decayed, 2 + 2 * k + 2)
                    after(nc.vector.tensor_tensor_scan(t[:], a[:], ig[:], 0.0, ALU.mult, ALU.add))
                    nc.vector.tensor_tensor(core.h[:, KA + k, :], p[:, T_YG + k, :], t[:], ALU.mult).then_inc(out_done, 1)
                    dve.wait_ge(out_done, k + 1)


def delta_inputs(core, p, ex, pc, w2, a2, g2):
    nc = core.nc
    with ExitStack() as held, stage(nc, "loaded", "step", "shifted", "acted", "g_ready", "g_kept", "wa_ready",
                                    "fetch", "acted2", "pair_ready", "pair_used", "kept", "keep_set") as \
            (loaded, step, shifted, acted, g_ready, g_kept, wa_ready, fetch, acted2, pair_ready, pair_used,
             kept, keep_set):
        def sb(name, shape):
            return held.enter_context(nc.sbuf_tensor(name, shape, F32, allow_name_mangling=True))

        wa = sb("w2a2", [P, D_C])
        wg = sb("g2", [P, D_C])
        keep = sb("keep", [P, S])
        ps = core.ps
        t1, t2 = sb("t1", [P, S])[:], sb("t2", [P, S])[:]
        t0, t3 = p[:, T_YG + KB - 1, :], p[:, T_XG, :]

        def chunks(x):
            return x.rearrange("p (c t) -> p c t", t=CH)
        with nc.Block() as block:
            @block.sync
            def _(sp):
                sp.dma_start(wa[0:HD, :], w2).then_inc(loaded, 16)
                sp.dma_start(wa[HD:P, :], a2).then_inc(loaded, 16)
                sp.dma_start(wg[:], g2).then_inc(loaded, 16)

            @block.gpsimd
            def _(pool):
                nc.gpsimd.memset(keep[:], 1.0).then_inc(keep_set, 1)
                pool.wait_ge(keep_set, 1)
                nc.gpsimd.memset(chunks(keep[:])[:, :, 0:1], 0.0).then_inc(keep_set, 1)

            @block.tensor
            def _(pe):
                pe.wait_ge(loaded, 48)
                pe.wait_ge(acted, 2)
                for q in range(KCC):
                    for i in range(NH):
                        last = nc.tensor.matmul(ps[:, 2 * q + i, :], wg[:, q * P:(q + 1) * P],
                                                t3[:, i * HALF:(i + 1) * HALF], start=True, stop=True)
                    last.then_inc(g_ready, 1)
                pe.wait_ge(g_kept, KCC)
                for q in range(KCC):
                    if q:
                        pe.wait_ge(acted2, 9 * q)
                        pe.wait_ge(pair_used, 2 * q)
                    for part in range(2):
                        rows = slice(part * HD, (part + 1) * HD)
                        for i in range(NH):
                            last = nc.tensor.matmul(ps[:, 2 * part + i, :], wa[rows, q * P:(q + 1) * P],
                                                    p[rows, T_WA, i * HALF:(i + 1) * HALF], start=True, stop=True)
                    last.then_inc(wa_ready, 1)
                    for part in range(2):
                        pe.wait_ge(fetch, 2 * q + part + 1)
                        for i in range(NH):
                            last = nc.tensor.matmul(ps[:, 4 + 2 * part + i, :], core.c("pair", P), t3[:, i * HALF:(i + 1) * HALF],
                                                    start=True, stop=True)
                        last.then_inc(pair_ready, 1)

            @block.scalar
            def _(act):
                act.wait_ge(shifted, 11)
                nc.scalar.activation(p[0:HD, T_WA, :], p[0:HD, T_WA, :], ACT.Tanh).then_inc(acted, 1)
                nc.scalar.activation(t3, t3, ACT.Sigmoid).then_inc(acted, 1)
                for q in range(KCC):
                    act.wait_ge(g_ready, q + 1)
                    nc.scalar.activation(ex[:, 3 + q, :], flat(ps[:, 2 * q:2 * q + 2, :]), ACT.Copy).then_inc(g_kept, 1)
                for q in range(KCC):
                    act.wait_ge(wa_ready, q + 1)
                    if q:
                        act.wait_ge(kept, q)
                    nc.scalar.activation(t0, flat(ps[:, 0:2, :]), ACT.Sigmoid, bias=core.p2("w0", q)).then_inc(acted2, 1)
                    nc.scalar.activation(t1, flat(ps[:, 2:4, :]), ACT.Sigmoid, bias=core.p2("a0", q)).then_inc(acted2, 1)
                    act.wait_ge(pair_used, 2 * q + 1)
                    nc.scalar.activation(p[:, q, :], p[:, q, :], ACT.Exp).then_inc(acted2, 1)
                    nc.scalar.activation(p[:, 6 + q, :], p[:, 6 + q, :], ACT.Exp).then_inc(acted2, 1)
                    nc.scalar.activation(p[:, 3 + q, :], t2, ACT.Exp, scale=-1.0).then_inc(acted2, 1)
                    nc.scalar.activation(pc[:, q, :], chunks(t2)[:, :, CH - 1], ACT.Exp).then_inc(acted2, 1)
                    nc.scalar.activation(t0, t2, ACT.Exp).then_inc(acted2, 1)
                    nc.scalar.activation(t3, t3, ACT.Sqrt).then_inc(acted2, 1)
                    act.wait_ge(fetch, 2 * q + 2)
                    act.wait_ge(shifted, 12 + q)
                    nc.scalar.activation(ex[:, q, :], t1, ACT.Copy).then_inc(acted2, 1)
                    act.wait_ge(acted2, 9 * q + 9)

            @block.vector
            def _(dve):
                n = [0]

                def after(ins):
                    ins.then_inc(step, 1)
                    n[0] += 1
                    dve.wait_ge(step, n[0])

                for j in range(KP):
                    x = p[:, T_R + j, :]
                    nc.vector.tensor_scalar(t0[:, 0:1], x[:, 0:1], -1.0, None, ALU.mult).then_inc(step, 1)
                    n[0] += 1
                    after(nc.vector.tensor_tensor(t0[:, 1:], x[:, 0:S - 1], x[:, 1:], ALU.subtract))
                    nc.vector.scalar_tensor_tensor(x, t0, core.p2("mu", j), x, ALU.mult, ALU.add).then_inc(shifted, 1)
                    dve.wait_ge(shifted, j + 1)
                dve.wait_ge(keep_set, 2)
                for q in range(KCC):
                    r, k, v = p[:, T_R + q, :], p[:, T_K + q, :], p[:, T_VV + q, :]
                    kk = h_b = core.h[:, KA + KB + q, :]
                    if q == 0:
                        dve.wait_ge(g_ready, KCC)
                    after(nc.vector.tensor_scalar(kk, k, core.p2("k_k", q), None, ALU.mult))
                    nc.vector.tensor_tensor(t3, kk, kk, ALU.mult).then_inc(fetch, 1)
                    dve.wait_ge(acted2, 9 * q + 2)
                    after(nc.vector.tensor_scalar(t0, t0, -math.exp(-0.5), None, ALU.mult))
                    after(nc.vector.tensor_tensor_scan(t2, keep[:], t0, 0.0, ALU.mult, ALU.add))
                    nc.vector.tensor_tensor(p[:, q, :], t2, t0, ALU.subtract).then_inc(step, 1)
                    last = chunks(t2)[:, :, CH - 1:CH].to_broadcast([P, NCH, CH])
                    nc.vector.tensor_tensor(chunks(p[:, 6 + q, :]), last, chunks(t2), ALU.subtract).then_inc(step, 1)
                    n[0] += 2
                    dve.wait_ge(step, n[0])
                    dve.wait_ge(pair_ready, 2 * q + 1)
                    nc.vector.tensor_scalar(t3, flat(ps[:, 4:6, :]), 1e-24, None, ALU.max).then_inc(pair_used, 1)
                    dve.wait_ge(acted2, 9 * q + 8)
                    after(nc.vector.reciprocal(t3, t3))
                    after(nc.vector.tensor_tensor(kk, kk, t3, ALU.mult))
                    after(nc.vector.tensor_tensor(p[:, q, :], p[:, q, :], kk, ALU.mult))
                    after(nc.vector.tensor_tensor(kk, kk, t1, ALU.mult))
                    after(nc.vector.tensor_scalar(t1, t1, -1.0, core.p2("k_a", q), ALU.add, ALU.mult))
                    after(nc.vector.scalar_tensor_tensor(k, t1, 1.0, k, ALU.add, ALU.mult))
                    nc.vector.scalar_tensor_tensor(t3, r, core.p2("r_k", q), k, ALU.mult, ALU.mult).then_inc(fetch, 1)
                    nc.vector.tensor_tensor(t1, k, p[:, 3 + q, :], ALU.mult).then_inc(shifted, 1)
                    dve.wait_ge(shifted, 12 + q)
                    after(nc.vector.tensor_tensor(p[:, 3 + q, :], p[:, 3 + q, :], kk, ALU.mult))
                    after(nc.vector.tensor_tensor(k, k, p[:, 6 + q, :], ALU.mult))
                    after(nc.vector.scalar_tensor_tensor(p[:, 6 + q, :], kk, -1.0, p[:, 6 + q, :], ALU.mult, ALU.mult))
                    after(nc.vector.tensor_tensor(r, r, t0, ALU.mult))
                    dve.wait_ge(pair_ready, 2 * q + 2)
                    nc.vector.tensor_tensor(h_b, v, flat(ps[:, 6:8, :]), ALU.mult).then_inc(pair_used, 1)
                    dve.wait_ge(pair_used, 2 * q + 2)
                    dve.wait_ge(acted2, 9 * q + 9)
                    nc.vector.engine_nop().then_inc(kept, 1)


def delta_chunks(core, p, ex, pc):
    nc = core.nc
    LV = 5
    with ExitStack() as held, stage(
            nc, "joined", "spread", "tok_ready", "tok_kept", "prod_ready", "first_made", "masked", "am_made", "g_ready",
            "g_kept", "xz_ready", "x_made", "z_made", "y_ready", "y_kept", "w1_ready", "w1_kept", "u_ready", "u_kept",
            "o_ready", "o_kept", "s_ready", "s_made") as \
            (joined, spread, tok_ready, tok_kept, prod_ready, first_made, masked, am_made, g_ready,
             g_kept, xz_ready, x_made, z_made, y_ready, y_kept, w1_ready, w1_kept, u_ready, u_kept,
             o_ready, o_kept, s_ready, s_made):
        def sb(name, shape=(P, KCC, P)):
            return held.enter_context(nc.sbuf_tensor(name, list(shape), F32, allow_name_mangling=True))

        wide = KCC * P
        free_a = p[:, T_WA:T_XG + 1, :].rearrange("p a s -> p (a s)")
        free_b = p[:, T_YG + KB - 1, :]

        def view(x, at, n):
            return x[:, at:at + KCC * n].rearrange("p (q n) -> p q n", q=KCC)
        kkd, bi, ki, be, ke = (view(free_a, i * wide, P) for i in range(5))
        vv, kkdT = (view(free_b, i * wide, P) for i in range(2))
        ARK = view(free_b, 2 * wide, CH)
        beT, keT = (view(core.rstd, i * wide, P) for i in range(2))
        vT, X, Z, A, AM, AKK, G, Y, W1, U, ST = (
            sb(n) for n in ("vT", "X", "Z", "A", "AM", "AKK", "G", "Y", "W1", "U", "ST"))
        ARB = sb("ARB", (P, KCC, CH))
        ps = core.ps

        def bank(b):
            return ps[:, b, 0:wide].rearrange("p (q n) -> p q n", q=KCC)

        def thin(b, at=0):
            return ps[:, b, at:at + KCC * CH].rearrange("p (q n) -> p q n", q=KCC)

        def all_q(mask, n=P):
            return mask.unsqueeze(1).to_broadcast([P, KCC, n])

        def each(lhsT, rhs, out, start=True, stop=True):
            for q in range(KCC):
                last = nc.tensor.matmul(out[:, q, :], lhsT[:, q, :], rhs(q), start=start, stop=stop)
            return last

        def whole(t):
            return lambda q: t[:, q, :]
        sources = [(kkd, lambda cols: p[:, 0:KCC, cols]), (bi, lambda cols: p[:, 3:3 + KCC, cols]),
                   (ki, lambda cols: ex[:, 0:KCC, cols]), (vv, lambda cols: p[:, T_VV:T_VV + KCC, cols]),
                   (ke, lambda cols: p[:, T_K:T_K + KCC, cols]), (be, lambda cols: p[:, 6:6 + KCC, cols])]
        n_src = len(sources)
        with nc.Block() as block:
            @block.tensor
            def _(pe):
                with pe.Fori(0, NCH) as c:
                    cols = bass.ds(c * CH, CH)
                    pe.wait_ge(spread, n_src * c + n_src)
                    for b, t in enumerate((vv, kkd, ke, be)):
                        for q in range(KCC):
                            last = nc.tensor.transpose(bank(b)[:, q, :], t[:, q, :], core.c("ident", P))
                        last.then_inc(tok_ready, 1)
                    each(bi, whole(kkd), bank(4)).then_inc(prod_ready, 1)
                    each(kkd, whole(bi), bank(5)).then_inc(prod_ready, 1)
                    each(ki, whole(kkd), bank(6)).then_inc(prod_ready, 1)
                    each(ki, lambda q: p[:, T_R + q, cols], thin(7))
                    each(bi, lambda q: p[:, T_R + q, cols], thin(7, KCC * CH)).then_inc(prod_ready, 1)
                    pe.wait_ge(first_made, 2 * c + 2)
                    for m in range(LV):
                        if m:
                            pe.wait_ge(x_made, LV * c + m)
                        pe.wait_ge(am_made, LV * c + (m + 1))
                        each(AM, whole(X), bank(4)).then_inc(g_ready, 1)
                        pe.wait_ge(g_kept, LV * c + (m + 1))
                        if m:
                            pe.wait_ge(z_made, (LV - 1) * c + m)
                        else:
                            pe.wait_ge(masked, 4 * c + 4)
                        each(Z, whole(G), bank(5)).then_inc(xz_ready, 1)
                        if m < LV - 1:
                            each(G, whole(Z), bank(6)).then_inc(xz_ready, 1)
                        if m == 0:
                            pe.wait_ge(tok_kept, 4 * c + 4)
                            each(AKK, whole(vT), bank(0)).then_inc(y_ready, 1)
                    pe.wait_ge(x_made, LV * c + LV)
                    each(kkdT, whole(X), bank(1)).then_inc(w1_ready, 1)
                    pe.wait_ge(y_kept, c + 1)
                    pe.wait_ge(w1_kept, c + 1)
                    pe.wait_ge(s_made, KCC * c + KCC)
                    for q in range(KCC):
                        nc.tensor.matmul(bank(2)[:, q, :], X[:, q, :], Y[:, q, :], start=True, stop=False)
                        last = nc.tensor.matmul(bank(2)[:, q, :], W1[:, q, :], ST[:, q, :], start=False, stop=True)
                    last.then_inc(u_ready, 1)
                    pe.wait_ge(u_kept, c + 1)
                    for q in range(KCC):
                        out = thin(3)[:, q, :]
                        nc.tensor.matmul(out, ST[:, q, :], p[:, T_R + q, cols], start=True, stop=False)
                        nc.tensor.matmul(out, vT[:, q, :], ARK[:, q, :], start=False, stop=False)
                        last = nc.tensor.matmul(out, U[:, q, :], ARB[:, q, :], start=False, stop=True)
                    last.then_inc(o_ready, 1)
                    for q in range(KCC):
                        nc.tensor.matmul(bank(7)[:, q, :], keT[:, q, :], vT[:, q, :], start=True, stop=False)
                        last = nc.tensor.matmul(bank(7)[:, q, :], beT[:, q, :], U[:, q, :], start=False, stop=True)
                    last.then_inc(s_ready, 1)

            @block.gpsimd
            def _(pool):
                with pool.Fori(0, NCH) as c:
                    pool.wait_ge(masked, 4 * c + 1)
                    for m in range(LV):
                        if m:
                            pool.wait_ge(g_ready, LV * c + m)
                        nc.gpsimd.tensor_tensor(AM[:], A[:], all_q(core.con[:, CON["levelsT"] + (m + 1) * P:CON["levelsT"] + (m + 2) * P]),
                                                ALU.mult).then_inc(am_made, 1)

            @block.scalar
            def _(act):
                with act.Fori(0, NCH) as c:
                    cols = bass.ds(c * CH, CH)
                    for b, t in enumerate((vT, kkdT, keT, beT)):
                        act.wait_ge(tok_ready, 4 * c + (b + 1))
                        nc.scalar.activation(t[:], bank(b), ACT.Copy).then_inc(tok_kept, 1)
                    for m in range(LV):
                        act.wait_ge(g_ready, LV * c + (m + 1))
                        nc.scalar.activation(G[:], bank(4), ACT.Copy).then_inc(g_kept, 1)
                        if m == 0:
                            act.wait_ge(y_ready, c + 1)
                            nc.scalar.activation(Y[:], bank(0), ACT.Copy).then_inc(y_kept, 1)
                    act.wait_ge(w1_ready, c + 1)
                    nc.scalar.activation(W1[:], bank(1), ACT.Copy).then_inc(w1_kept, 1)
                    act.wait_ge(u_ready, c + 1)
                    nc.scalar.activation(U[:], bank(2), ACT.Copy).then_inc(u_kept, 1)
                    act.wait_ge(o_ready, c + 1)
                    nc.scalar.activation(p[:, T_R:T_R + KCC, cols], thin(3), ACT.Copy).then_inc(o_kept, 1)

            @block.vector
            def _(dve):
                for q in range(KCC):
                    nc.vector.memset(ST[:, q, :], 0.0).then_inc(s_made, 1)
                pair = core.c("pair", P).rearrange("p (h t) -> p h t", h=2)
                with dve.Fori(0, NCH) as c:
                    cols = bass.ds(c * CH, CH)
                    for t, src in sources:
                        for q in range(KCC):
                            s = src(cols)[:, q, :].unsqueeze(1).to_broadcast([P, 2, CH])
                            ins = nc.vector.tensor_tensor(t[:, q, :].rearrange("p (h n) -> p h n", h=2), s, pair, ALU.mult)
                        ins.then_inc(spread, 1)
                    dve.wait_ge(prod_ready, 4 * c + 1)
                    nc.vector.tensor_tensor(X[:], bank(4), all_q(core.c("level0", P)), ALU.mult).then_inc(joined, 1)
                    dve.wait_ge(prod_ready, 4 * c + 2)
                    nc.vector.tensor_tensor(A[:], bank(5), all_q(core.c("strictT", P)), ALU.mult).then_inc(masked, 1)
                    dve.wait_ge(joined, 2 * c + 1)
                    nc.vector.tensor_tensor(X[:], all_q(core.c("ident", P)), X[:], ALU.subtract).then_inc(first_made, 1)
                    dve.wait_ge(masked, 4 * c + 1)
                    nc.vector.tensor_tensor(Z[:], A[:], all_q(core.con[:, CON["levelsT"]:CON["levelsT"] + P]),
                                            ALU.mult).then_inc(joined, 1)
                    dve.wait_ge(joined, 2 * c + 2)
                    nc.vector.tensor_tensor(Z[:], all_q(core.c("ident", P)), Z[:], ALU.subtract).then_inc(first_made, 1)
                    dve.wait_ge(prod_ready, 4 * c + 3)
                    nc.vector.tensor_tensor(AKK[:], bank(6), all_q(core.c("strict", P)), ALU.mult).then_inc(masked, 1)
                    dve.wait_ge(prod_ready, 4 * c + 4)
                    nc.vector.tensor_tensor(ARK[:], thin(7), all_q(core.c("upper", CH), CH), ALU.mult).then_inc(masked, 1)
                    nc.vector.scalar_tensor_tensor(ARB[:], thin(7, KCC * CH), -1.0, all_q(core.c("upper", CH), CH),
                                                   ALU.mult, ALU.mult).then_inc(masked, 1)
                    for m in range(LV):
                        dve.wait_ge(xz_ready, (2 * LV - 1) * c + (2 * m + 1))
                        nc.vector.tensor_tensor(X[:], X[:], bank(5), ALU.subtract).then_inc(x_made, 1)
                        if m < LV - 1:
                            dve.wait_ge(xz_ready, (2 * LV - 1) * c + (2 * m + 2))
                            nc.vector.tensor_tensor(Z[:], Z[:], bank(6), ALU.subtract).then_inc(z_made, 1)
                            dve.wait_ge(z_made, (LV - 1) * c + (m + 1))
                        dve.wait_ge(x_made, LV * c + (m + 1))
                    dve.wait_ge(s_ready, c + 1)
                    for q in range(KCC):
                        nc.vector.scalar_tensor_tensor(ST[:, q, :], ST[:, q, :], pc[:, q, bass.ds(c, 1)], bank(7)[:, q, :],
                                                       ALU.mult, ALU.add).then_inc(s_made, 1)
                    dve.wait_ge(o_kept, c + 1)


def delta_output(core, p, ex):
    nc = core.nc
    with stage(nc, "summed", "gated") as (summed, gated):
        with nc.Block() as block:
            @block.vector
            def _(dve):
                for q in range(KCC):
                    h = core.h[:, KA + KB + q, :]
                    nc.vector.tensor_tensor(h, h, p[:, T_R + q, :], ALU.add).then_inc(summed, 1)
                    dve.wait_ge(summed, q + 1)
                    nc.vector.tensor_tensor(h, h, ex[:, 3 + q, :], ALU.mult).then_inc(gated, 1)


def ffn_up(core, w, hid):
    nc = core.nc
    edge = CONV_FF - 1
    with ExitStack() as held, stage(nc, "w0", "w1", "edges", "product_ready", "gate_kept", "tapped", "silu_ready", "hid_made") as \
            (w0, w1, edges, product_ready, gate_kept, tapped, silu_ready, hid_made):
        def sb(name, shape):
            return held.enter_context(nc.sbuf_tensor(name, shape, F32, allow_name_mangling=True))

        ws = sb("w_up", [P, 2, 2, KD, P])
        g = sb("g_raw", [P, edge + S])
        cv = sb("g_conv", [P, S])
        ps = core.ps
        landed = [w0, w1]
        w_k = w.rearrange("(k p) (a n) -> p k a n", p=P, a=2)
        with nc.Block() as block:
            def loops(eng, body, start=0):
                with eng.Fori(start, KF // 2) as i:
                    for b in range(2):
                        body(2 * i + b, i, b)

            @block.sync
            def _(sp):
                def load(j, b):
                    for a in range(2):
                        sp.dma_start(ws[:, b, a, :, :], w_k[:, :, a, bass.ds(j * P, P)]).then_inc(landed[b], 16)

                def body(j, i, b):
                    sp.wait_ge(product_ready, 2 * (j - 1))
                    load(j, b)
                load(0, 0)
                load(1, 1)
                loops(sp, body, 1)

            @block.tensor
            def _(pe):
                def tile(j, i, b, first=False):
                    pe.wait_ge(landed[b], 32 * (i + 1))
                    for a in range(2):
                        if not first:
                            pe.wait_ge(*((gate_kept, j - 1) if a == 0 else (hid_made, j - 1)))
                        for half in range(NH):
                            for k in range(KD):
                                last = nc.tensor.matmul(ps[:, 4 * b + 2 * a + half, :], ws[:, b, a, k, :],
                                                        core.h[:, k, half * HALF:(half + 1) * HALF],
                                                        start=(k == 0), stop=(k == KD - 1))
                        last.then_inc(product_ready, 1)
                tile(0, 0, 0, True)
                tile(1, 0, 1, True)
                loops(pe, tile, 1)

            @block.scalar
            def _(act):
                def tile(j, i, b, first=False):
                    act.wait_ge(product_ready, 2 * j + 1)
                    if not first:
                        act.wait_ge(tapped, CONV_FF * j)
                    nc.scalar.activation(g[:, edge:], flat(ps[:, 4 * b:4 * b + 2, :]), ACT.Copy).then_inc(gate_kept, 1)
                    act.wait_ge(tapped, CONV_FF * j + CONV_FF)
                    nc.scalar.activation(cv[:], cv[:], ACT.Silu, bias=core.two[:, bass.ds(TWO["ffn_conv_b"] + j, 1)]).then_inc(silu_ready, 1)
                tile(0, 0, 0, True)
                tile(1, 0, 1)
                loops(act, tile, 1)

            @block.vector
            def _(dve):
                nc.vector.memset(g[:, 0:edge], 0.0).then_inc(edges, 1)
                dve.wait_ge(edges, 1)

                def tile(j, i, b):
                    def tap(t):
                        return core.two[:, bass.ds(TWO["ffn_conv_w"] + t * KF + j, 1)]
                    dve.wait_ge(gate_kept, j + 1)
                    nc.vector.tensor_scalar(cv[:], g[:, edge:], tap(edge), None, ALU.mult).then_inc(tapped, 1)
                    for t in range(edge):
                        dve.wait_ge(tapped, CONV_FF * j + (t + 1))
                        nc.vector.scalar_tensor_tensor(cv[:], g[:, t:t + S], tap(t), cv[:], ALU.mult, ALU.add).then_inc(tapped, 1)
                    dve.wait_ge(silu_ready, j + 1)
                    dve.wait_ge(product_ready, 2 * j + 2)
                    nc.vector.tensor_tensor(hid[:, bass.ds(j, 1), :].rearrange("p a s -> p (a s)"), cv[:],
                                            flat(ps[:, 4 * b + 2:4 * b + 4, :]), ALU.mult).then_inc(hid_made, 1)
                    dve.wait_ge(hid_made, j + 1)
                loops(dve, tile)


def ffn_down(core, w, hid, gate_at):
    nc = core.nc
    slots = 3
    with ExitStack() as held, stage(nc, "w0", "w1", "w2", "grouped", "added", "squared",
                                    "totalled") as \
            (w0, w1, w2, grouped, added, squared, totalled):
        ws = held.enter_context(nc.sbuf_tensor("w_down", [P, slots, KF, P], F32, allow_name_mangling=True))
        sq = core.h[:, 0:2, :]
        landed = [w0, w1, w2]
        with nc.Block() as block:
            @block.sync
            def _(sp):
                for j in range(KD):
                    if j >= slots:
                        sp.wait_ge(grouped, j - slots + 1)
                    sp.dma_start(ws[:, j % slots, :, :],
                                 w.rearrange("(k p) n -> p k n", p=P)[:, :, j * P:(j + 1) * P]).then_inc(landed[j % slots], 16)

            @block.tensor
            def _(pe):
                for j in range(KD):
                    pe.wait_ge(landed[j % slots], 16 * (j // slots + 1))
                    if j >= 4:
                        pe.wait_ge(added, j - 3)
                    for i in range(NH):
                        for k in range(KF):
                            last = nc.tensor.matmul(core.ps[:, 2 * (j % 4) + i, :], ws[:, j % slots, k, :],
                                                    hid[:, k, i * HALF:(i + 1) * HALF], start=(k == 0), stop=(k == KF - 1))
                    last.then_inc(grouped, 1)

            @block.scalar
            def _(act):
                square_tiles(core, act, sq, added, squared, totalled)

            @block.vector
            def _(dve):
                add_and_total(core, dve, gate_at, sq, grouped, added, squared, totalled)


def program(nc, a, out):
    h_rows = nc.dram_tensor("h_rows", (S, D), F32, kind="Internal").ap()
    slot_rows = nc.dram_tensor("slot_rows", (N_EXP, S), F32, kind="Internal").ap()
    aff_rows = nc.dram_tensor("aff_rows", (N_EXP, S), F32, kind="Internal").ap()
    with ExitStack() as ctx:
        core = Core(nc, ctx)
        with ExitStack() as tables:
            cos = tables.enter_context(nc.sbuf_tensor("cos", [ROPE, S], F32))
            sin = tables.enter_context(nc.sbuf_tensor("sin", [ROPE, S], F32))
            load_inputs(core, cos, sin, a["xT"], a["cT"], a["pos"], a["con"], a["par_two"])
            with nc.Fori(0, DEPTH) as l:
                block_one(core, cos, sin, a, l, h_rows, slot_rows, aff_rows)
        block_two(core, a)
        store_output(core, core.h, out)


def block_one(core, cos, sin, a, l, h_rows, slot_rows, aff_rows):
    nc = core.nc
    modulation(core, 0, a["w_ada"][l], lambda: core.p1("b_ada", 0, P, N_MOD * KD), a["par_one"][l])
    with ExitStack() as held:
        cq = held.enter_context(nc.sbuf_tensor("cq", [P, 2, S], F32))
        ckv = held.enter_context(nc.sbuf_tensor("ckv", [P, S], F32))
        kr = held.enter_context(nc.sbuf_tensor("kr", [ROPE, S], F32))
        y = held.enter_context(nc.sbuf_tensor("y", [P, KC, S + 2 * PAD], F32))
        project_one(core, a["w_in"][l], core.p1("norm1_g", 0, P, KD), cq, ckv, kr, y)
        attention(core, cos, sin, a["w_uq"][l], a["w_ukv"][l], cq, ckv, kr, y)
    conv = [core.h[:, HEADS + j, :] for j in range(KC)]
    layer_norm(core, conv, CONV_CH, core.c("eps"), core.c("ones", P), lambda k: core.p1("conv_norm_g", k),
               lambda k: core.p1("conv_norm_b", k), ACT.Silu)
    out_projection(core, a["w_out"][l], 2 * KD)
    normalise(core, core.p1("norm2_g", 0, P, KD), 3 * KD, 4 * KD)
    mats = [a["w_gate"][l], a["w_up"][l], a["w_down"][l]]
    with nc.sbuf_tensor("w_ring", [P, PIECES, KPP, FF], F32) as ring, \
            stage(nc, *[f"w{i}" for i in range(PIECES)]) as landed:
        route(core, ring, landed, mats, a["w_router"][l], h_rows, slot_rows, aff_rows)
        experts(core, ring, landed, mats, h_rows, slot_rows, aff_rows, 5 * KD)


def block_two(core, a):
    nc = core.nc
    modulation(core, 1, a["w_mod_2"], lambda: core.p2("b_mod", 0, N_MOD * KD))
    with ExitStack() as held:
        p = held.enter_context(nc.sbuf_tensor("p_two", [P, N_P, S], F32))
        pc = held.enter_context(nc.sbuf_tensor("chunk_decay", [P, KCC, NCH], F32))
        project_two(core, a["w_in_2"], core.p2("norm_mix", 0, KD), p)
        v = [p[:, T_V + k, :] for k in range(KA)]
        layer_norm(core, v, D_A, core.c("ln_eps"), core.c("ones", P), lambda k: core.p2("sgu_ln_g", k),
                   lambda k: core.p2("sgu_ln_b", k), ACT.Identity)
        spatial_gate(core, p, a["sgu_w_2"], a["sgu_b_2"].rearrange("h t -> (h t)").unsqueeze(0))
        linear_recurrence(core, p, a["lru_w_a_2"], a["lru_w_x_2"])
        with nc.sbuf_tensor("ex_two", [P, 2 * KCC, S], F32) as ex:
            delta_inputs(core, p, ex, pc, a["rwkv_w2_2"], a["rwkv_a2_2"], a["rwkv_g2_2"])
            delta_chunks(core, p, ex, pc)
            o = [p[:, T_R + q, :] for q in range(KCC)]
            layer_norm(core, o, HD, core.c("gn_eps"), core.c("pair", P), lambda k: core.p2("ln_w", k),
                       lambda k: core.p2("ln_b", k), ACT.Identity)
            delta_output(core, p, ex)
    out_projection(core, a["w_out_2"], 2 * KD)
    normalise(core, core.p2("norm_ffn", 0, KD), 3 * KD, 4 * KD)
    with nc.sbuf_tensor("ffn_hidden", [P, KF, S], F32) as hid:
        ffn_up(core, a["ffn_w_up_2"], hid)
        ffn_down(core, a["ffn_w_down_2"], hid, 5 * KD)
    normalise(core, core.p2("norm_final", 0, KD), None, None)


ONE_WEIGHTS = ["w_ada", "w_in", "w_uq", "w_ukv", "w_out", "w_router", "w_gate", "w_up", "w_down"]
TWO_WEIGHTS = ["w_mod_2", "w_in_2", "w_out_2", "sgu_w_2", "sgu_b_2", "lru_w_a_2", "lru_w_x_2", "rwkv_w2_2",
               "rwkv_a2_2", "rwkv_g2_2", "ffn_w_up_2", "ffn_w_down_2"]


def lay_out(v):
    def cols(x):
        x = np.asarray(x)
        return np.swapaxes(x.reshape(x.shape[:-1] + (-1, P)), -1, -2)

    def padded(x):
        z = np.zeros((x.shape[0], P, 1), np.float32)
        z[:, :x.shape[1], 0] = x
        return z

    a = {"xT": np.asarray(v["x"])[0].T, "con": constants(), "pos": np.asarray(v["positions"])[0]}
    a["cT"] = np.stack([cols(v["c"][0]), cols(v["c_2"][0])], axis=1)
    one = {"qg_nope": padded(v["q_head_g"][:, :NOPE]), "qg_rope": padded(v["q_head_g"][:, NOPE:]),
           "kg_nope": padded(v["k_head_g"][:, :NOPE]), "kg_rope": padded(v["k_head_g"][:, NOPE:])}
    tap = cols(v["conv_w"])
    one["conv_w"] = np.swapaxes(tap, 1, 2).reshape(DEPTH, P, TAPS * KC)
    for name in ONE:
        if name not in one:
            one[name] = cols(v[name])
    a["par_one"] = np.concatenate([one[n] for n in ONE], axis=2)
    two = {}
    tap = cols(v["lru_conv_w_2"][0])
    two["lru_conv_w"] = np.swapaxes(tap, 0, 1).reshape(P, -1)
    tap = cols(v["ffn_conv_w_2"][0])
    two["ffn_conv_w"] = np.swapaxes(tap, 0, 1).reshape(P, -1)
    other = {"r_k": v["rwkv_r_k_2"].reshape(1, D_C), "norm_final": v["norm_final_2"].reshape(1, D)}
    for name in TWO:
        if name not in two:
            src = other.get(name)
            if src is None:
                src = v[name + "_2"] if name + "_2" in v else v["rwkv_" + name + "_2"]
            two[name] = cols(src[0])
    a["par_two"] = np.concatenate([two[n] for n in TWO], axis=1)
    for n in ONE_WEIGHTS + TWO_WEIGHTS:
        a[n] = np.asarray(v[n])
        if n in TWO_WEIGHTS:
            a[n] = a[n][0]
    return {n: np.ascontiguousarray(x) for n, x in a.items()}


def kernel(**inputs):
    import concourse.bacc as _bacc
    from concourse.bass_utils import run_bass_kernel_spmd as _run

    v = {n: np.asarray(x) for n, x in inputs.items()}
    arrays = lay_out(v)
    nc = _bacc.Bacc("TRN2", target_bir_lowering=False, num_devices=1)
    args = {n: nc.dram_tensor("in_" + n, x.shape, mybir.dt.from_np(x.dtype), kind="ExternalInput").ap()
            for n, x in arrays.items()}
    out = nc.dram_tensor("out_0", (D, S), F32, kind="ExternalOutput").ap()
    program(nc, args, out)
    r = _run(nc, [{"in_" + n: x for n, x in arrays.items()}], core_ids=[0])
    return np.ascontiguousarray(r.results[0]["out_0"].T)[None]
```
